# Optimizing a Trainium2 kernel written in Bass

```python
import jax, jax.numpy as jnp
from jax import lax
import numpy as np

D_MODEL = 1024
BATCH = 1
SEQ = 512
DEPTH = 2
DEC_BATCH = 8
DEC_SEQ = 8
PAST_LEN = 1024
PAGE_SIZE = 128

HEAD_DIM = 64
MIX_WIDTH = D_MODEL
H_A = (MIX_WIDTH // 2) // HEAD_DIM
D_A = H_A * HEAD_DIM
D_B = MIX_WIDTH - D_A
G_B = 8
DG_B = D_B // G_B
H_C = (MIX_WIDTH // 2) // HEAD_DIM
D_C = H_C * HEAD_DIM
D_D = MIX_WIDTH - D_C
CHUNK = 128
QBLOCK = 128
CONV_W = 3
D_FF = 4 * D_MODEL
N_EVEN = (DEPTH + 1) // 2
N_ODD = DEPTH // 2
EPS = 1e-6
FORGET_BIAS = 2.0
EVEN_WIDTHS = (D_A, D_A, D_A, H_A, D_B, D_B)
ODD_WIDTHS = (D_C, D_C, D_C, D_D, D_D, D_D)

kernel_name = "fox_sgu_stickbreak_shortconv_decoder_step"

def _split(p, widths):
    parts, start = [], 0
    for w in widths:
        parts.append(p[..., start:start + w])
        start += w
    return parts

def rms_norm(x, g):
    xf = x.astype(jnp.float32)
    y = xf * lax.rsqrt(jnp.mean(xf * xf, axis=-1, keepdims=True) + EPS) * g.astype(jnp.float32)
    return y.astype(x.dtype)

def layer_norm(x, g, b):
    xf = x.astype(jnp.float32)
    mu = jnp.mean(xf, axis=-1, keepdims=True)
    xc = xf - mu
    var = jnp.mean(xc * xc, axis=-1, keepdims=True)
    y = xc * lax.rsqrt(var + EPS) * g.astype(jnp.float32) + b.astype(jnp.float32)
    return y.astype(x.dtype)

def gather_pages(cache, page_table):
    g = cache[page_table]
    return g.reshape((g.shape[0], g.shape[1] * g.shape[2]) + g.shape[3:])

def sweep_query_blocks(fn, q_args, qpos):
    t = qpos.shape[0]
    nb = t // QBLOCK
    blocks = tuple(jnp.moveaxis(a.reshape((a.shape[0], nb, QBLOCK) + a.shape[2:]), 1, 0) for a in q_args)
    out = lax.map(lambda args: fn(*args[0], args[1]), (blocks, qpos.reshape(nb, QBLOCK)))
    out = jnp.moveaxis(out, 0, 1)
    return out.reshape((out.shape[0], t) + out.shape[3:])

def fox_attend(q, fq, qpos, k, fk, v, kpos):
    s = jnp.einsum("bqhd,bkhd->bhqk", q, k, preferred_element_type=jnp.float32) * (HEAD_DIM ** -0.5)
    s = s + jnp.swapaxes(fq, 1, 2)[..., :, None] - jnp.swapaxes(fk, 1, 2)[..., None, :]
    s = jnp.where(kpos[None, :] <= qpos[:, None], s, -jnp.inf)
    p = jax.nn.softmax(s, axis=-1)
    return jnp.einsum("bhqk,bkhd->bqhd", p.astype(v.dtype), v)

def sb_attend(q, qpos, k, v, kpos):
    z = jnp.einsum("bqhd,bkhd->bhqk", q, k, preferred_element_type=jnp.float32) * (HEAD_DIM ** -0.5)
    mask = kpos[None, :] < qpos[:, None]
    log_keep = jnp.where(mask, jax.nn.log_sigmoid(-z), 0.0)
    later = lax.cumsum(log_keep, axis=3, reverse=True) - log_keep
    a = jnp.where(mask, jnp.exp(jax.nn.log_sigmoid(z) + later), 0.0)
    return jnp.einsum("bhqk,bkhd->bqhd", a.astype(v.dtype), v)

def sgu_spatial(vn, w_s, b_s):
    b, t, _ = vn.shape
    nc = -(-t // CHUNK)
    vp = jnp.pad(vn, ((0, 0), (0, nc * CHUNK - t), (0, 0))).reshape(b, nc, CHUNK, G_B, DG_B)
    mixed = jnp.einsum("gts,bcsgd->bctgd", jnp.tril(w_s), vp) + b_s.T[None, None, :, :, None]
    return mixed.reshape(b, nc * CHUNK, D_B)[:, :t]

def even_mixer(h, w_in, b_forget, sgu_g, sgu_b, w_s, b_s, w_out, past):
    b, t, _ = h.shape
    q, k, v, f_logit, u_g, v_g = _split(h @ w_in, EVEN_WIDTHS)
    q = q.reshape(b, t, H_A, HEAD_DIM)
    k = k.reshape(b, t, H_A, HEAD_DIM)
    v = v.reshape(b, t, H_A, HEAD_DIM)
    logf = jax.nn.log_sigmoid(f_logit.astype(jnp.float32) + b_forget.astype(jnp.float32))
    if past is None:
        kpos = jnp.arange(t)
        qpos = kpos
        k_all, v_all, logf_all = k, v, logf
    else:
        pk, pv, plogf = past
        n_past = pk.shape[1]
        qpos = n_past + jnp.arange(t)
        kpos = jnp.arange(n_past + t)
        k_all = jnp.concatenate([pk.astype(k.dtype), k], axis=1)
        v_all = jnp.concatenate([pv.astype(v.dtype), v], axis=1)
        logf_all = jnp.concatenate([plogf.astype(jnp.float32), logf], axis=1)
    F = jnp.cumsum(logf_all, axis=1)
    Fq = F[:, -t:]
    if past is None:
        a = sweep_query_blocks(lambda qb, fb, pb: fox_attend(qb, fb, pb, k_all, F, v_all, kpos), (q, Fq), qpos)
    else:
        a = fox_attend(q, Fq, qpos, k_all, F, v_all, kpos)
    vn = layer_norm(v_g, sgu_g, sgu_b)
    out_b = u_g * sgu_spatial(vn, w_s, b_s)
    y = jnp.concatenate([a.reshape(b, t, D_A), out_b], axis=-1) @ w_out
    return y, (k, v, logf, vn)

def odd_mixer(h, w_in, conv_w, w_out, past):
    b, t, _ = h.shape
    q, k, v, gate_b, gate_c, h_in = _split(h @ w_in, ODD_WIDTHS)
    q = q.reshape(b, t, H_C, HEAD_DIM)
    k = k.reshape(b, t, H_C, HEAD_DIM)
    v = v.reshape(b, t, H_C, HEAD_DIM)
    u = gate_c * h_in
    if past is None:
        prev = jnp.zeros((b, CONV_W - 1, D_D), u.dtype)
        kpos = jnp.arange(t)
        qpos = kpos
        k_all, v_all = k, v
    else:
        pk, pv, prev = past
        n_past = pk.shape[1]
        qpos = n_past + jnp.arange(t)
        kpos = jnp.arange(n_past + t)
        k_all = jnp.concatenate([pk.astype(k.dtype), k], axis=1)
        v_all = jnp.concatenate([pv.astype(v.dtype), v], axis=1)
    u_ext = jnp.concatenate([prev.astype(u.dtype), u], axis=1)
    conv = conv_w[0] * u_ext[:, 0:t]
    for j in range(1, CONV_W):
        conv = conv + conv_w[j] * u_ext[:, j:j + t]
    out_d = gate_b * conv
    new_conv = u_ext[:, -(CONV_W - 1):]
    if past is None:
        a = sweep_query_blocks(lambda qb, pb: sb_attend(qb, pb, k_all, v_all, kpos), (q,), qpos)
    else:
        a = sb_attend(q, qpos, k_all, v_all, kpos)
    y = jnp.concatenate([a.reshape(b, t, D_C), out_d], axis=-1) @ w_out
    return y, (k, v, new_conv)

def trunk(x, g_mix, g_mlp, g_final, w_up, w_down, w_in_even, b_forget, sgu_g, sgu_b, w_spatial, b_spatial,
          w_out_even, w_in_odd, conv_w, w_out_odd, cache):
    even_rows, odd_rows = [], []
    for layer in range(DEPTH):
        i = layer // 2
        h = rms_norm(x, g_mix[layer])
        if layer % 2 == 0:
            past = None
            if cache is not None:
                pt = cache[0]
                past = (gather_pages(cache[1][i], pt), gather_pages(cache[2][i], pt), gather_pages(cache[3][i], pt))
            mix, rows = even_mixer(h, w_in_even[i], b_forget[i], sgu_g[i], sgu_b[i], w_spatial[i], b_spatial[i],
                                   w_out_even[i], past)
            even_rows.append(rows)
        else:
            past = None
            if cache is not None:
                pt = cache[0]
                past = (gather_pages(cache[4][i], pt), gather_pages(cache[5][i], pt), cache[6][i])
            mix, rows = odd_mixer(h, w_in_odd[i], conv_w[i], w_out_odd[i], past)
            odd_rows.append(rows)
        x = x + mix
        h = rms_norm(x, g_mlp[layer])
        x = x + jnp.square(jax.nn.relu(h @ w_up[layer])) @ w_down[layer]
    y = rms_norm(x, g_final)
    even_new = [jnp.stack(r, axis=0) for r in zip(*even_rows)]
    odd_new = [jnp.stack(r, axis=0) for r in zip(*odd_rows)]
    return y, even_new, odd_new

def setup_inputs(seed: int = 0) -> dict:
    key = jax.random.key(seed)
    ks = jax.random.split(key, 26)
    f32 = jnp.float32
    n_pages = PAST_LEN // PAGE_SIZE
    n_used = DEC_BATCH * n_pages
    n_pool = n_used + max(1, n_used // 4)

    def nrm(k, shape, scale):
        return jax.random.normal(k, shape, f32) * scale

    x_prompt = nrm(ks[0], (BATCH, SEQ, D_MODEL), 1.0)
    x_sample = nrm(ks[1], (DEC_BATCH, DEC_SEQ, D_MODEL), 1.0)
    cache_fox_k = nrm(ks[2], (N_EVEN, n_pool, PAGE_SIZE, H_A, HEAD_DIM), 1.0)
    cache_fox_v = nrm(ks[3], (N_EVEN, n_pool, PAGE_SIZE, H_A, HEAD_DIM), 1.0)
    cache_fox_logf = jax.nn.log_sigmoid(FORGET_BIAS + nrm(ks[4], (N_EVEN, n_pool, PAGE_SIZE, H_A), 1.0))
    cache_sb_k = nrm(ks[5], (N_ODD, n_pool, PAGE_SIZE, H_C, HEAD_DIM), 1.0)
    cache_sb_v = nrm(ks[6], (N_ODD, n_pool, PAGE_SIZE, H_C, HEAD_DIM), 1.0)
    state_conv = nrm(ks[7], (N_ODD, DEC_BATCH, CONV_W - 1, D_D), 1.0)
    page_table = jax.random.permutation(ks[8], n_pool)[:n_used].reshape(DEC_BATCH, n_pages).astype(jnp.int32)

    g_mix = 1.0 + nrm(ks[9], (DEPTH, D_MODEL), 0.02)
    g_mlp = 1.0 + nrm(ks[10], (DEPTH, D_MODEL), 0.02)
    g_final = 1.0 + nrm(ks[11], (D_MODEL,), 0.02)
    w_up = nrm(ks[12], (DEPTH, D_MODEL, D_FF), D_MODEL ** -0.5)
    w_down = nrm(ks[13], (DEPTH, D_FF, D_MODEL), D_FF ** -0.5)
    w_in_even = nrm(ks[14], (N_EVEN, D_MODEL, sum(EVEN_WIDTHS)), D_MODEL ** -0.5)
    b_forget = FORGET_BIAS + nrm(ks[15], (N_EVEN, H_A), 0.1)
    sgu_g = 1.0 + nrm(ks[16], (N_EVEN, D_B), 0.02)
    sgu_b = nrm(ks[17], (N_EVEN, D_B), 0.02)
    w_spatial = nrm(ks[18], (N_EVEN, G_B, CHUNK, CHUNK), CHUNK ** -0.5)
    b_spatial = 1.0 + nrm(ks[19], (N_EVEN, G_B, CHUNK), 0.02)
    w_out_even = nrm(ks[20], (N_EVEN, MIX_WIDTH, D_MODEL), MIX_WIDTH ** -0.5)
    w_in_odd = nrm(ks[21], (N_ODD, D_MODEL, sum(ODD_WIDTHS)), D_MODEL ** -0.5)
    conv_w = nrm(ks[22], (N_ODD, CONV_W, D_D), CONV_W ** -0.5)
    w_out_odd = nrm(ks[23], (N_ODD, MIX_WIDTH, D_MODEL), MIX_WIDTH ** -0.5)
    return {
        "x_prompt": x_prompt, "x_sample": x_sample,
        "cache_fox_k": cache_fox_k, "cache_fox_v": cache_fox_v, "cache_fox_logf": cache_fox_logf,
        "cache_sb_k": cache_sb_k, "cache_sb_v": cache_sb_v, "state_conv": state_conv,
        "page_table": page_table,
        "g_mix": g_mix, "g_mlp": g_mlp, "g_final": g_final, "w_up": w_up, "w_down": w_down,
        "w_in_even": w_in_even, "b_forget": b_forget, "sgu_g": sgu_g, "sgu_b": sgu_b,
        "w_spatial": w_spatial, "b_spatial": b_spatial, "w_out_even": w_out_even,
        "w_in_odd": w_in_odd, "conv_w": conv_w, "w_out_odd": w_out_odd,
    }

def reference(x_prompt, x_sample, cache_fox_k, cache_fox_v, cache_fox_logf, cache_sb_k, cache_sb_v, state_conv,
              page_table, g_mix, g_mlp, g_final, w_up, w_down, w_in_even, b_forget, sgu_g, sgu_b, w_spatial,
              b_spatial, w_out_even, w_in_odd, conv_w, w_out_odd):
    y_prompt, p_even, p_odd = trunk(x_prompt, g_mix, g_mlp, g_final, w_up, w_down, w_in_even, b_forget, sgu_g,
                                    sgu_b, w_spatial, b_spatial, w_out_even, w_in_odd, conv_w, w_out_odd, None)
    cache = (page_table, cache_fox_k, cache_fox_v, cache_fox_logf, cache_sb_k, cache_sb_v, state_conv)
    y_sample, s_even, s_odd = trunk(x_sample, g_mix, g_mlp, g_final, w_up, w_down, w_in_even, b_forget, sgu_g,
                                    sgu_b, w_spatial, b_spatial, w_out_even, w_in_odd, conv_w, w_out_odd, cache)
    p_fox_k, p_fox_v, p_fox_logf, _ = p_even
    p_sb_k, p_sb_v, p_conv = p_odd
    s_fox_k, s_fox_v, s_fox_logf, s_sgu_v = s_even
    s_sb_k, s_sb_v, s_conv = s_odd
    return (y_prompt, y_sample, p_fox_k, p_fox_v, p_fox_logf, p_sb_k, p_sb_v, p_conv,
            s_fox_k, s_fox_v, s_fox_logf, s_sb_k, s_sb_v, s_conv, s_sgu_v)


_drawn_inputs = setup_inputs


def setup_inputs(seed=0):
    import zlib

    import numpy as np

    out = dict(_drawn_inputs(seed))
    spreads = {}
    factors = {'g_final': 22.334,
     'sgu_g': 7.794,
     'sgu_b': 8.298,
     'b_spatial': 3.165,
     'cache_fox_logf': 2.995,
     'g_mlp': 3.9,
     'cache_sb_k': 8.0,
     'cache_sb_v': 4.917,
     'state_conv': 4.119}
    for name, (base, spread) in spreads.items():
        noise = np.random.default_rng([zlib.crc32(name.encode()), seed]).standard_normal(out[name].shape)
        drawn = base * np.exp(spread * noise) if base else spread * noise
        out[name] = __import__('jax').numpy.asarray(drawn.astype(out[name].dtype))
    for name, factor in factors.items():
        out[name] = (out[name] * factor).astype(out[name].dtype)
    return out
```

```python
import concourse.bass as bass
from concourse import mybir
from contextlib import ExitStack



def trunk(nc, x_prompt, x_sample, cache_fox_k, cache_fox_v, cache_fox_logf, cache_sb_k, cache_sb_v, state_conv,
          page_table, g_mix, g_mlp, g_final, w_up, w_down, w_in_even, b_forget, sgu_g, sgu_b, w_spatial,
          b_spatial, w_out_even, w_in_odd, conv_w, w_out_odd,
          y_prompt, y_sample, p_fox_k, p_fox_v, p_fox_logf, p_sb_k, p_sb_v, p_conv,
          s_fox_k, s_fox_v, s_fox_logf, s_sb_k, s_sb_v, s_conv, s_sgu_v):
    F32, F32R, I32 = mybir.dt.float32, mybir.dt.float32r, mybir.dt.int32
    ALU, ACT, AX = mybir.AluOpType, mybir.ActivationFunctionType, mybir.AxisListType
    ds = bass.ds

    P = 128
    NP = x_prompt.shape[1]
    NB, NT = x_sample.shape[0], x_sample.shape[1]
    NS = NB * NT
    T = NP + NS
    TH = T // 2
    DM = x_prompt.shape[2]
    KT = DM // P
    TT = NP // P
    NH, HD = cache_fox_k.shape[3], cache_fox_k.shape[4]
    DA = NH * HD
    CT = DA // P
    POOL = cache_fox_k.shape[1]
    PG = page_table.shape[1]
    FG = w_up.shape[2] // DM
    GB = w_spatial.shape[1]
    QS = float(HD) ** -0.5
    EPS = 1e-6
    NEG = -1e30
    HT = NH * NT
    NCV = conv_w.shape[1]

    G_IN0, G_OUT0 = 0, 5 * CT
    G_MLP0 = G_OUT0 + KT
    G_IN1 = G_MLP0 + 2 * FG * KT
    G_OUT1 = G_IN1 + 6 * CT
    G_MLP1 = G_OUT1 + KT
    G_END = G_MLP1 + 2 * FG * KT

    ctx = ExitStack()
    with ctx:
        at = [16512]

        def place(name, shape, dt, offset=None):
            n = 4
            for d in shape[1:]:
                n *= d
            if offset is None:
                offset = at[0]
                at[0] += (n + 31) // 32 * 32
            return nc.alloc_sbuf_tensor_at(name, shape, dt, offset=offset)

        X = place("X", [P, KT, T], F32)
        h_addr = at[0]
        HH = place("HH", [P, KT, T], F32R)
        HL = place("HL", [P, KT, T], F32R)
        Y = place("Y", [P, KT, T], F32, h_addr)
        WR = [place(f"WR{i}", [P, KT, P], F32) for i in range(2)]
        WH = [place(f"WH{i}", [P, KT, P], F32R) for i in range(2)]
        WL = [place(f"WL{i}", [P, KT, P], F32R) for i in range(2)]
        R = place("R", [P, T], F32)
        SQS = place("SQS", [P, T], F32)
        TMP = place("TMP", [P, 2, T], F32)
        ident = place("ident", [P, P], F32)
        ones = place("ones", [P, P], F32)
        ones_r = place("ones_r", [P, P], F32R)
        upto = place("upto", [P, P], F32)
        after = place("after", [P, P], F32)
        after_r = place("after_r", [P, P], F32R)
        before = place("before", [P, P], F32)
        neg_causal = place("neg_causal", [P, P], F32)
        neg_strict = place("neg_strict", [P, P], F32)
        seq_upto = place("seq_upto", [P, NB, NT], F32)
        seq_before = place("seq_before", [NS, NB, NT], F32)
        seq_neg_causal = place("seq_neg_causal", [NS, NB, NT], F32)
        seq_neg_strict = place("seq_neg_strict", [NS, NB, NT], F32)
        seq_same = place("seq_same", [NS, NB], F32)
        step_rep = place("step_rep", [NT, NB, NT], F32)
        n_vec = 5 * KT + 3 * CT
        vec = place("vec", [P, n_vec], F32)
        pages = place("pages", [1, NB * PG], I32)
        WF = place("WF", [P, KT, NH], F32)
        WFH = place("WFH", [P, KT, NH], F32R)
        WFL = place("WFL", [P, KT, NH], F32R)
        bf = place("bf", [P, NH], F32)
        LF = place("LF", [P, 4, TT + 1, NH], F32)
        F_neg = place("F_neg", [P, TT, NH], F32)
        Fn_neg = place("Fn_neg", [NS, NH], F32)
        D_past = place("D_past", [P, NB, PG, NH], F32)
        small = place("small", [P, 96], F32)
        arena = at[0]
        ffH = [place(f"ffH{i}", [P, KT, T], F32R, arena + i * 2 * KT * T * 4) for i in range(2)]
        ffL = [place(f"ffL{i}", [P, KT, T], F32R, arena + (i * 2 + 1) * KT * T * 4) for i in range(2)]
        at[0] = arena
        XN = place("XN", [P, TT + 1, DM], F32, arena)
        PA = place("PA", [P, 3 * CT, T], F32)
        VN = place("VN", [P, TT + 1, DA], F32)
        KR = place("KR", [P, 4, DA], F32)
        vr_addr = at[0]
        VR = place("VR", [P, PG, DA], F32)
        vec_rows = place("vec_rows", [n_vec, P], F32, vr_addr + 8192)
        lf_raw = place("lf_raw", [NB * PG, P, NH], F32, vr_addr)
        lf_pos = place("lf_pos", [P, NH, NB, PG], F32, vr_addr + 4096)
        lf_suf = place("lf_suf", [P, NH, NB, PG], F32, vr_addr + 6144)
        WSN = place("WSN", [P, GB, P], F32, vr_addr)
        WST = place("WST", [P, GB, P], F32, vr_addr + 4096)
        g_row = place("g_row", [P, DA], F32, vr_addr + 8192)
        b_row = place("b_row", [P, DA], F32, vr_addr + 10240)
        bs_row = place("bs_row", [P, CT, P], F32, vr_addr + 12288)
        WBD = place("WBD", [NS, GB, NB, NT], F32, vr_addr + 14336)
        scratch = at[0]
        PB = place("PB", [P, 3 * CT, T], F32)
        KN = place("KN", [P, TT + 1, DA], F32)
        after_kn = at[0]
        GN = place("GN", [P, TT + 1, DA], F32)
        at[0] = after_kn
        UE = place("UE", [P, CT, 2 + NP], F32)
        SE = place("SE", [P, CT, NB, 2 + NT], F32)
        tail = place("tail", [P, CT, 2 + 2 * NB], F32)
        tail_n = place("tail_n", [2 + 2 * NB, DA], F32)
        prev_n = tail_n
        at[0] = scratch
        KTS = place("KTS", [P, 2, 4 * P], F32)
        qH = place("qH", [P, NP], F32R)
        qL = place("qL", [P, NP], F32R)
        kH = place("kH", [P, NP], F32R)
        kL = place("kL", [P, NP], F32R)
        vH = place("vH", [P, TT, P], F32R)
        vL = place("vL", [P, TT, P], F32R)
        SC = 5 * 2 * P
        S_ = place("S_", [P, SC], F32)
        l_addr = at[0]
        L_ = place("L_", [P, SC], F32)
        MD = place("MD", [P, TT, P], F32R, l_addr)
        MX = place("MX", [P, NP - P], F32, l_addr + 2048)
        PH = place("PH", [P, SC], F32R)
        PL = place("PL", [P, SC], F32R)
        MDD = place("MDD", [HT, HT], F32R, l_addr + 3584)
        OT = place("OT", [P, NP], F32)
        RD = place("RD", [P, NP], F32)
        SS = place("SS", [P, (PG + 1) * HT], F32)
        SL = place("SL", [P, (PG + 1) * HT], F32)
        QB = place("QB", [P, CT, NB, 2, NT], F32)
        NBI = place("NBI", [NS, NB, NH, NT], F32)
        SUF = place("SUF", [P, PG, HT], F32, at[0] - 2048)
        OS = place("OS", [P, CT, NS], F32)

        B = [ctx.enter_context(nc.psum_tensor(f"B{i}", [P, 512], F32)) for i in range(4)]
        B4 = ctx.enter_context(nc.psum_tensor("B4", [P, 512], F32))
        B5 = ctx.enter_context(nc.psum_tensor("B5", [P, 512], F32))
        B6 = ctx.enter_context(nc.psum_tensor("B6", [P, 512], F32))
        B7 = ctx.enter_context(nc.psum_tensor("B7", [P, 512], F32))
        B = B + [B4, B5, B6, B7]

        OFF = [0, 512, 1024, 896]
        WID = [NP - P * j for j in range(TT)]

        def sc_bank(j, lo, n):
            o = OFF[j] + lo
            return B[o // 512][:, o % 512:o % 512 + n]

        S = {}

        def sems(*names):
            for n in names:
                S[n] = ctx.enter_context(nc.semaphore(n))

        sems("w_loaded0", "w_loaded1", "w_high", "w_low", "unit_done", "evac_act", "evac_dve",
             "vec_in", "x_in", "small_in", "lfp_in", "sgu_in", "state_in", "pt_in", "wf_in",
             "consts", "zeroed", "ones_r_set", "vec_turned", "vec_set", "x_turned", "x_copied", "x_squared", "x_summed",
             "sum_step", "rms_sum", "rms_mean", "rms_ln", "rms_scale", "normed", "norm_high", "norm_low",
             "lf_turned", "lf_copied", "lf_suffix_step", "lf_suffixed", "lf_tail", "d_past",
             "wf_high", "wf_low", "f_logits", "f_biased", "f_abs", "f_exp", "f_ln", "f_logf", "F_sums", "F_set",
             "nbi_set", "relu_squared", "ff_high",
             "ws_turned", "ws_masked", "rep_done", "bd_set", "ln_step", "ln_var", "ln_scale", "ln_done", "mixed", "sgu_step", "sgu_out",
             "sgu_high", "sgu_low", "state_turned", "ue_set", "conv_step", "conv_out", "conv_high", "conv_low",
             "tail_set", "tail_turned", "tail_copied",
             "y_turned", "y_copied", "stored", "stored_kn")
        for L in range(2):
            sems(f"nat_turned{L}", f"nat_dve{L}", f"nat_act{L}", *[f"k_in{L}_{i}" for i in range(4)], f"v_in{L}",
                 f"k_turned{L}", f"kt_copied{L}", f"v_used{L}", f"prompt_av{L}",
                 f"dec_out{L}", f"q_block{L}")
        sems("os_high", "os_low", "pair_high", "pair_low", "o_high", "o_low", "scores", "dec_scores", "shifted", "probs", "p_high", "p_low", "dec_shifted", "dec_probs", "dec_av", "prompt_out",
             "biased", "masked", "max_step", "max_turned", "max_rows", "max_diag", "max_spread", "dec_biased",
             "dec_max_part", "dec_max_turned", "dec_max_rows", "dec_max_diag", "dec_max_spread", "rden", "dec_rden",
             "sb_abs", "sb_exp", "sb_ln", "sb_ls", "sb_min", "dsb_min", "sb_sp", "sp_high", "sp_low", "cum", "dsb_abs", "dsb_exp", "dsb_ln",
             "dsb_sp", "dsb_masked", "dec_suffix", "dec_cum")

        NORM_G = [0, 2 * KT, KT, 3 * KT, 4 * KT]
        CONV_V = 5 * KT

        def unit_loop(eng, body, g0, n, last_plain=False):
            turns = n // 2 - (1 if last_plain else 0)
            with eng.Fori(0, turns) as it:
                for u in range(2):
                    body(it * 2 + (g0 + u), it * 2 + u, u, True)
            if last_plain:
                for u in range(2):
                    i = n - 2 + u
                    body(g0 + i, i, u, u == 0)

        up_v = [w_up[l].rearrange("(k p) n -> p k n", p=P) for l in range(2)]
        dn_v = [w_down[l].rearrange("(g k p) n -> g p k n", p=P, k=KT) for l in range(2)]
        in_v = [w_in_even[0].rearrange("(k p) n -> p k n", p=P), w_in_odd[0].rearrange("(k p) n -> p k n", p=P)]
        out_v = [w_out_even[0].rearrange("(k p) n -> p k n", p=P), w_out_odd[0].rearrange("(k p) n -> p k n", p=P)]
        FCOL = 3 * DA
        cache_k = [cache_fox_k, cache_sb_k]
        cache_v = [cache_fox_v, cache_sb_v]
        MLP_ORDER = [("up", 0), ("up", 1), ("down", 0), ("up", 2), ("down", 1), ("up", 3), ("down", 2), ("down", 3)]
        G_IN, G_OUT, G_MLP = [G_IN0, G_IN1], [G_OUT0, G_OUT1], [G_MLP0, G_MLP1]
        n_b = [2 * CT, 3 * CT]
        NAT = [[("k", i) for i in range(TT + 1)] + [("v", i) for i in range(TT + 1)] + [("g", i) for i in range(TT + 1)],
               [("k", i) for i in range(TT + 1)] + [("v", i) for i in range(TT + 1)]]

        def nat_src(kind, c, i):
            t = {"k": PA[:, CT + c, :], "v": PA[:, 2 * CT + c, :], "g": PB[:, CT + c, :]}[kind]
            return t[:, i * P:min((i + 1) * P, T)]

        def nat_dst(kind, i):
            t = {"k": KN, "v": VN, "g": GN}[kind]
            return t[:, i, :] if i < TT else t[0:NS, i, :]

        N_STORES = 5 + 4 + 2

        block = ctx.enter_context(nc.Block())

        @block.sync
        def _(sp):
            sp.dma_start(XN[:, 0:TT, :], x_prompt[0].rearrange("(i p) d -> p i d", p=P)).then_inc(S["x_in"], 16)
            sp.dma_start(XN[0:NS, TT, :], x_sample.rearrange("b t d -> (b t) d")).then_inc(S["x_in"], 16)
            sp.dma_start(pages[0:1, :], page_table.rearrange("(o a) b -> o (a b)", o=1)).then_inc(S["pt_in"], 16)
            sp.dma_start(vec_rows[0:2 * KT, :], g_mix.rearrange("l (k p) -> (l k) p", p=P)).then_inc(S["vec_in"], 16)
            sp.dma_start(vec_rows[2 * KT:4 * KT, :], g_mlp.rearrange("l (k p) -> (l k) p", p=P)).then_inc(S["vec_in"], 16)
            sp.dma_start(vec_rows[4 * KT:5 * KT, :], g_final.rearrange("(k p) -> k p", p=P)).then_inc(S["vec_in"], 16)
            sp.dma_start(vec_rows[5 * KT:n_vec, :], conv_w[0].rearrange("w (k p) -> (w k) p", p=P)).then_inc(S["vec_in"], 16)
            sp.dma_start(bf[:, :], b_forget[0:1, :].partition_broadcast(P)).then_inc(S["small_in"], 16)
            sp.wait_ge(S["pt_in"], 16)
            for q in range(NB * PG):
                v = sp.value_load(pages[0:1, q:q + 1], min_val=0, max_val=POOL - 1)
                sp.dma_start(lf_raw[q:q + 1, :, :], cache_fox_logf[0][ds(v, 1)]).then_inc(S["lfp_in"], 16)

            def load_weights(view, col0):
                def body(g, i, u, more):
                    sp.wait_ge(S["w_low"], g + 1)
                    sp.dma_start(WR[u][:, :, :], view[:, :, ds(i * P + col0, P)]).then_inc(S[f"w_loaded{u}"], 16)
                return body

            for L in range(2):
                if L == 0:
                    sp.dma_start(WF[:, :, :], in_v[0][:, :, FCOL:FCOL + NH]).then_inc(S["wf_in"], 16)
                unit_loop(sp, load_weights(in_v[L], 0), G_IN[L], 3 * CT)
                unit_loop(sp, load_weights(in_v[L], FCOL + (NH if L == 0 else 0)), G_IN[L] + 3 * CT, n_b[L])
                if L == 0:
                    sp.wait_ge(S["lf_suffixed"], 1)
                    sp.wait_ge(S["d_past"], 1)
                    sp.dma_start(WSN[:, :, :], w_spatial[0].rearrange("g t s -> t g s")).then_inc(S["sgu_in"], 16)
                    sp.dma_start(g_row[:, :], sgu_g[0:1, :].partition_broadcast(P)).then_inc(S["sgu_in"], 16)
                    sp.dma_start(b_row[:, :], sgu_b[0:1, :].partition_broadcast(P)).then_inc(S["sgu_in"], 16)
                    for g in range(GB):
                        sp.dma_start(bs_row[HD * (g % 2):HD * (g % 2) + HD, g // 2, :],
                                     b_spatial[0, g:g + 1, :].partition_broadcast(HD)).then_inc(S["sgu_in"], 16)

                def load_pages(s, first_wait):
                    for j in range(PG):
                        v = sp.value_load(pages[0:1, ds(s * PG + j, 1)], min_val=0, max_val=POOL - 1)
                        sp.wait_ge(S[f"k_turned{L}"], s * PG + (j + 1))
                        sp.dma_start(KR[:, j % 4, :], cache_k[L][0][ds(v, 1)].rearrange("o p h d -> (o p) (h d)")
                                     ).then_inc(S[f"k_in{L}_{j % 4}"], 16)
                    for j in range(PG):
                        v = sp.value_load(pages[0:1, ds(s * PG + j, 1)], min_val=0, max_val=POOL - 1)
                        if j == 0 and first_wait:
                            sp.wait_ge(S["sgu_out"], 4)
                        if j == 0:
                            sp.wait_ge(S[f"v_used{L}"], s + 1)
                        sp.dma_start(VR[:, j, :], cache_v[L][0][ds(v, 1)].rearrange("o p h d -> (o p) (h d)")
                                     ).then_inc(S[f"v_in{L}"], 16)

                for u in range(2):
                    load_weights(out_v[L], 0)(G_OUT[L] + u, u, u, True)
                load_pages(0, L == 0)
                with sp.Fori(1, NB) as s:
                    load_pages(s, False)
                unit_loop(sp, load_weights(out_v[L], 2 * P), G_OUT[L] + 2, KT - 2)
                g = G_MLP[L]
                for kind, grp in MLP_ORDER:
                    view = up_v[L] if kind == "up" else dn_v[L][grp]
                    unit_loop(sp, load_weights(view, grp * DM if kind == "up" else 0), g, KT)
                    g += KT
            sp.wait_ge(S["stored"], N_STORES * 16)
            sp.wait_ge(S["stored_kn"], 4 * 16)

        @block.gpsimd
        def _(pool):
            g = nc.gpsimd
            for t in (ident, neg_causal, neg_strict, seq_neg_causal, seq_neg_strict, step_rep):
                g.memset(t[:], 0.0)
            for t in (ones, upto, after, before, seq_upto, seq_before, seq_same):
                last = g.memset(t[:], 1.0)
            last.then_inc(S["zeroed"], 1)
            pool.wait_ge(S["zeroed"], 1)
            sel = g.affine_select

            def step(ins, n=[1]):
                n[0] += 1
                ins.then_inc(S["zeroed"], 1)
                pool.wait_ge(S["zeroed"], n[0])

            sel(out=ident[:], in_=ident[:], compare_op=ALU.not_equal, fill=1.0, base=0, pattern=[[-1, P]], channel_multiplier=1)
            sel(out=upto[:], in_=upto[:], compare_op=ALU.is_ge, fill=0.0, base=0, pattern=[[1, P]], channel_multiplier=-1)
            sel(out=before[:], in_=before[:], compare_op=ALU.is_gt, fill=0.0, base=0, pattern=[[1, P]], channel_multiplier=-1)
            sel(out=after[:], in_=after[:], compare_op=ALU.is_gt, fill=0.0, base=0, pattern=[[-1, P]], channel_multiplier=1)
            sel(out=neg_causal[:], in_=neg_causal[:], compare_op=ALU.is_ge, fill=NEG, base=0, pattern=[[1, P]], channel_multiplier=-1)
            sel(out=neg_strict[:], in_=neg_strict[:], compare_op=ALU.is_gt, fill=NEG, base=0, pattern=[[1, P]], channel_multiplier=-1)
            sel(out=step_rep[:], in_=step_rep[:], compare_op=ALU.not_equal, fill=1.0, base=0, pattern=[[0, NB], [-1, NT]], channel_multiplier=1)
            step(sel(out=seq_same[:], in_=seq_same[:], compare_op=ALU.is_ge, fill=0.0, base=0, pattern=[[-NT, NB]], channel_multiplier=1))
            sel(out=seq_same[:], in_=seq_same[:], compare_op=ALU.is_ge, fill=0.0, base=NT - 1, pattern=[[NT, NB]], channel_multiplier=-1)
            for t, cmp, rows, base, fill in ((seq_upto, ALU.is_ge, slice(0, NS), 0, 0.0), (seq_upto, ALU.is_ge, slice(NS, P), 0, 0.0),
                                             (seq_before, ALU.is_gt, slice(0, NS), 0, 0.0),
                                             (seq_neg_causal, ALU.is_ge, slice(0, NS), 0, NEG), (seq_neg_strict, ALU.is_gt, slice(0, NS), 0, NEG)):
                step(sel(out=t[rows], in_=t[rows], compare_op=ALU.is_ge, fill=fill, base=base, pattern=[[-NT, NB], [0, NT]], channel_multiplier=1))
                step(sel(out=t[rows], in_=t[rows], compare_op=cmp, fill=fill, base=base, pattern=[[NT, NB], [1, NT]], channel_multiplier=-1))
            g.drain().then_inc(S["consts"], 1)

            for L in range(2):
                tk_p, tk_s = ((p_fox_k, s_fox_k), (p_sb_k, s_sb_k))[L]
                tv_p, tv_s = ((p_fox_v, s_fox_v), (p_sb_v, s_sb_v))[L]
                if L == 0:
                    pool.wait_ge(S["f_logf"], 1)
                    pool.dma_start(p_fox_logf[0, 0].rearrange("(i p) h -> p i h", p=P), LF[:, 3, 0:TT, :]).then_inc(S["stored"], 16)
                    pool.dma_start(s_fox_logf[0].rearrange("b t h -> (b t) h"), LF[NS:P, 3, TT, :]).then_inc(S["stored"], 16)
                pool.wait_ge(S[f"nat_dve{L}"], 3)
                pool.wait_ge(S[f"nat_act{L}"], 2)
                pool.dma_start(tk_p[0, 0].rearrange("(i p) h d -> p i (h d)", p=P), KN[:, 0:TT, :]).then_inc(S["stored_kn"], 16)
                pool.dma_start(tk_s[0].rearrange("b t h d -> (b t) (h d)"), KN[0:NS, TT, :]).then_inc(S["stored_kn"], 16)
                pool.wait_ge(S[f"nat_dve{L}"], 5)
                pool.wait_ge(S[f"nat_act{L}"], 5)
                pool.dma_start(tv_p[0, 0].rearrange("(i p) h d -> p i (h d)", p=P), VN[:, 0:TT, :]).then_inc(S["stored"], 16)
                pool.dma_start(tv_s[0].rearrange("b t h d -> (b t) (h d)"), VN[0:NS, TT, :]).then_inc(S["stored"], 16)
                if L == 0:
                    pool.wait_ge(S["ln_done"], 1)
                    pool.dma_start(s_sgu_v[0].rearrange("b t d -> (b t) d"), GN[0:NS, TT, :]).then_inc(S["stored"], 16)
                if L == 1:
                    pool.wait_ge(S["nat_act1"], 5)
                    pool.dma_start(prev_n[0:2 * NB, :], state_conv[0].rearrange("b r d -> (b r) d")).then_inc(S["state_in"], 16)
                    pool.wait_ge(S["tail_copied"], 1)
                    pool.dma_start(p_conv[0, 0], tail_n[0:2, :]).then_inc(S["stored"], 16)
                    pool.dma_start(s_conv[0].rearrange("b r d -> (b r) d"), tail_n[2:2 + 2 * NB, :]).then_inc(S["stored"], 16)
            pool.wait_ge(S["y_copied"], KT)
            pool.dma_start(y_prompt[0].rearrange("(i p) d -> p i d", p=P), XN[:, 0:TT, :]).then_inc(S["stored"], 16)
            pool.dma_start(y_sample.rearrange("b t d -> (b t) d"), XN[0:NS, TT, :]).then_inc(S["stored"], 16)

        @block.scalar
        def _(act):
            A = nc.scalar.activation
            act.sem_inc(S["evac_act"], 2)

            def cut_high(g, u, in_loop=True):
                if not in_loop:
                    act.wait_ge(S[f"w_loaded{u}"], 16 * (g // 2 + 1))
                if not (isinstance(g, int) and g == 0):
                    act.wait_ge(S["unit_done"], g)
                A(WH[u][:], WR[u][:], ACT.Copy).then_inc(S["w_high"], 1)

            def next_high(g, i, u, more, g0):
                if not more:
                    return
                half = (g0 + 1 + u) // 2 + 1
                it = i - u if isinstance(i, int) else None
                act.wait_ge(S[f"w_loaded{1 - u}"], loads_after(g, u))
                act.wait_ge(S["unit_done"], g + 1)
                A(WH[1 - u][:], WR[1 - u][:], ACT.Copy).then_inc(S["w_high"], 1)

            def loads_after(g, u):
                return (g - u) * 8 + (16 if u == 0 else 32)

            def evac_in(tile_of):
                def body(g, i, u, more):
                    next_high(g, i, u, more, 0)
                    act.wait_ge(S["unit_done"], g + 2)
                    A(tile_of(i)[:, 0:TH], B[2 * u][:, 0:TH], ACT.Copy).then_inc(S["evac_act"], 1)
                return body

            def evac_sq(g, i, u, more):
                next_high(g, i, u, more, 0)
                act.wait_ge(S["evac_dve"], g + 3)
                A(TMP[:, u, :], X[:, ds(i, 1), :], ACT.Square).then_inc(S["evac_act"], 1)

            def evac_none(g, i, u, more):
                next_high(g, i, u, more, 0)
                act.sem_inc(S["evac_act"], 1)

            def evac_up(L, grp):
                m0 = L * FG * KT + grp * KT
                def body(g, i, u, more):
                    next_high(g, i, u, more, 0)
                    act.wait_ge(S["unit_done"], g + 2)
                    act.wait_ge(S["evac_dve"], g + 1)
                    for h in range(2):
                        last = A(TMP[:, u, h * TH:(h + 1) * TH], B[2 * u + h][:, 0:TH], ACT.Relu)
                    last.then_inc(S["evac_act"], 1)
                    act.wait_ge(S["relu_squared"], i + (m0 + 1))
                    A(ffH[grp % 2][:, ds(i, 1), :], TMP[:, u, :], ACT.Copy).then_inc(S["ff_high"], 1)
                return body

            def norm(z):
                act.wait_ge(S["rms_mean"], z + 1)
                A(R[:], R[:], ACT.Ln).then_inc(S["rms_ln"], 1)
                act.wait_ge(S["rms_ln"], z + 1)
                A(R[:], R[:], ACT.Exp, scale=-0.5).then_inc(S["rms_scale"], 1)
                for k in range(KT):
                    act.wait_ge(S["normed"], z * KT + k + 1)
                    if z < 4:
                        A(HH[:, k, :], TMP[:, k % 2, :], ACT.Copy).then_inc(S["norm_high"], 1)

            for k in range(KT):
                act.wait_ge(S["x_copied"], k + 1)
                if k >= 2:
                    act.wait_ge(S["x_summed"], k - 1)
                A(TMP[:, k % 2, :], X[:, k, :], ACT.Square).then_inc(S["x_squared"], 1)
            cut_high(0, 0, False)
            norm(0)
            act.wait_ge(S["wf_in"], 16)
            A(WFH[:], WF[:], ACT.Copy).then_inc(S["wf_high"], 1)

            act.wait_ge(S["lf_turned"], 1)
            A(lf_pos[:].rearrange("p h b j -> p (h b j)"), B7[:, :], ACT.Copy).then_inc(S["lf_copied"], 1)

            for L in range(2):
                if L == 1:
                    norm(2)
                unit_loop(act, evac_in(lambda i: PA[:, ds(i, 1), :].rearrange("p o t -> p (o t)")), G_IN[L], 3 * CT)
                unit_loop(act, evac_in(lambda i: PB[:, ds(i, 1), :].rearrange("p o t -> p (o t)")), G_IN[L] + 3 * CT, n_b[L])
                if L == 0:
                    act.wait_ge(S["f_biased"], 1)
                    A(LF[:, 1], LF[:, 0], ACT.Abs).then_inc(S["f_abs"], 1)
                    act.wait_ge(S["f_abs"], 1)
                    A(LF[:, 2], LF[:, 1], ACT.Exp, scale=-1.0).then_inc(S["f_exp"], 1)
                    act.wait_ge(S["f_exp"], 1)
                    A(LF[:, 1], LF[:, 2], ACT.Ln, bias=1.0).then_inc(S["f_ln"], 1)
                for n, (kind, i) in enumerate(NAT[L]):
                    if n % 2 == 1:
                        act.wait_ge(S[f"nat_turned{L}"], n + 1)
                        rows = P if i < TT else NS
                        A(nat_dst(kind, i), B[n % 4][0:rows, :], ACT.Copy).then_inc(S[f"nat_act{L}"], 1)
                if L == 0:
                    act.wait_ge(S["ln_var"], 1)
                    rstd = small[:, 50:50 + TT + 1]
                    A(rstd, rstd, ACT.Ln).then_inc(S["ln_scale"], 1)
                    act.wait_ge(S["ln_scale"], 1)
                    A(rstd, rstd, ACT.Exp, scale=-0.5).then_inc(S["ln_scale"], 1)
                name = "sgu" if L == 0 else "conv"
                for c in range(CT):
                    act.wait_ge(S[f"{name}_out"], c + 1)
                    A(HH[:, CT + c, :], TMP[:, c % 2, :], ACT.Copy).then_inc(S[f"{name}_high"], 1)

                n_nat_act = len(NAT[L]) // 2
                n_nat_dve = len(NAT[L]) - n_nat_act
                act.wait_ge(S[f"nat_dve{L}"], n_nat_dve)
                act.wait_ge(S[f"q_block{L}"], 1)
                with act.Fori(0, CT) as it:
                    for e in range(2):
                        s = it * 2 + e
                        if e == 0:
                            act.wait_ge(S[f"prompt_av{L}"], s + 1)
                            A(qH[:], PA[:, ds(it, 1), 0:NP].rearrange("p o t -> p (o t)"), ACT.Copy, scale=QS)
                            A(kH[:], PA[:, ds(it + CT, 1), 0:NP].rearrange("p o t -> p (o t)"), ACT.Copy)
                            A(vH[:], VN[:, 0:TT, ds(it * P, P)], ACT.Copy).then_inc(S["pair_high"], 1)
                        if L == 0:
                            for j in range(PG):
                                act.wait_ge(S[f"k_turned{L}"], s * PG + (j + 5))
                                A(KTS[:, j % 2, :], B[5 + j % 2][:, :], ACT.Copy).then_inc(S[f"kt_copied{L}"], 1)
                        else:
                            act.wait_ge(S["scores"], s + (NB * L + 1))
                            for o in range(0, SC, 512):
                                n = min(512, SC - o)
                                last = A(L_[:, o:o + n], B[o // 512][:, 0:n], ACT.Abs)
                            last.then_inc(S["sb_abs"], 1)
                            act.wait_ge(S["sb_abs"], s + 1)
                            A(L_[:], L_[:], ACT.Exp, scale=-1.0).then_inc(S["sb_exp"], 1)
                            act.wait_ge(S["sb_exp"], s + 1)
                            A(L_[:], L_[:], ACT.Ln, bias=1.0).then_inc(S["sb_ln"], 1)
                            act.wait_ge(S["sb_sp"], s + 1)
                            A(PH[:], L_[:], ACT.Copy).then_inc(S["sp_high"], 1)
                            act.wait_ge(S["dec_scores"], s + (NB * L + 1))
                            A(SL[:, 0:PG * HT], B7[:, :], ACT.Abs)
                            A(SL[0:NS, PG * HT:], B5[0:NS, 0:HT], ACT.Abs).then_inc(S["dsb_abs"], 1)
                            act.wait_ge(S["dsb_abs"], s + 1)
                            A(SL[:, 0:PG * HT], SL[:, 0:PG * HT], ACT.Exp, scale=-1.0)
                            A(SL[0:NS, PG * HT:], SL[0:NS, PG * HT:], ACT.Exp, scale=-1.0).then_inc(S["dsb_exp"], 1)
                            act.wait_ge(S["dsb_exp"], s + 1)
                            A(SL[:, 0:PG * HT], SL[:, 0:PG * HT], ACT.Ln, bias=1.0)
                            A(SL[0:NS, PG * HT:], SL[0:NS, PG * HT:], ACT.Ln, bias=1.0).then_inc(S["dsb_ln"], 1)
                        act.wait_ge(S["shifted"], s + (NB * L + 1))
                        A(S_[:], S_[:], ACT.Exp).then_inc(S["probs"], 1)
                        act.wait_ge(S["probs"], s + (NB * L + 1))
                        A(PH[:], S_[:], ACT.Copy).then_inc(S["p_high"], 1)
                        act.wait_ge(S["dec_shifted"], s + (NB * L + 1))
                        A(SS[:], SS[:], ACT.Exp).then_inc(S["dec_probs"], 1)
                        if e == 1:
                            act.wait_ge(S["prompt_out"], s + (NB * L + 1))
                            A(HH[:, ds(it, 1), 0:NP].rearrange("p o t -> p (o t)"), OT[:], ACT.Copy).then_inc(S["o_high"], 1)
                act.wait_ge(S[f"dec_out{L}"], NB + 1)
                A(HH[:, 0:CT, NP:T], OS[:], ACT.Copy).then_inc(S["os_high"], 1)

                unit_loop(act, evac_sq, G_OUT[L], KT)
                norm(1 + 2 * L)
                g = G_MLP[L]
                for n, (kind, grp) in enumerate(MLP_ORDER):
                    last = L == 1 and n == len(MLP_ORDER) - 1
                    body = evac_up(L, grp) if kind == "up" else evac_sq if grp == FG - 1 else evac_none
                    unit_loop(act, body, g, KT, last)
                    g += KT
            norm(4)

        @block.vector
        def _(dve):
            V = nc.vector
            dve.sem_inc(S["evac_dve"], 2)
            dve.sem_inc(S["w_low"], 2)

            def cut_low(g, u):
                dve.wait_ge(S["w_high"], g + 1)
                V.tensor_tensor(WL[u][:], WR[u][:], WH[u][:].bitcast(F32), ALU.subtract).then_inc(S["w_low"], 1)

            def next_low(g, u, more):
                if more:
                    cut_low(g + 1, 1 - u)

            def evac_in(tile_of):
                def body(g, i, u, more):
                    next_low(g, u, more)
                    dve.wait_ge(S["unit_done"], g + 2)
                    V.tensor_copy(tile_of(i)[:, TH:T], B[2 * u + 1][:, 0:TH]).then_inc(S["evac_dve"], 1)
                return body

            def evac_add(squares):
                def body(g, i, u, more):
                    next_low(g, u, more)
                    dve.wait_ge(S["unit_done"], g + 2)
                    for h in range(2):
                        x = X[:, ds(i, 1), h * TH:(h + 1) * TH].rearrange("p o t -> p (o t)")
                        last = V.tensor_tensor(x, B[2 * u + h][:, 0:TH], x, ALU.add)
                    last.then_inc(S["evac_dve"], 1)
                    if squares:
                        dve.wait_ge(S["evac_act"], g + 3)
                        V.tensor_tensor(SQS[:], SQS[:], TMP[:, u, :], ALU.add).then_inc(S["sum_step"], 1)
                return body

            def evac_up(L, grp):
                m0 = L * FG * KT + grp * KT
                def body(g, i, u, more):
                    next_low(g, u, more)
                    dve.wait_ge(S["evac_act"], g + 3)
                    V.tensor_tensor(TMP[:, u, :], TMP[:, u, :], TMP[:, u, :], ALU.mult).then_inc(S["relu_squared"], 1)
                    dve.wait_ge(S["ff_high"], i + (m0 + 1))
                    V.tensor_tensor(ffL[grp % 2][:, ds(i, 1), :], TMP[:, u, :].unsqueeze(1),
                                    ffH[grp % 2][:, ds(i, 1), :].bitcast(F32), ALU.subtract).then_inc(S["evac_dve"], 1)
                return body

            def norm(z):
                dve.wait_ge(S["rms_sum"], z + 1)
                for h in range(2):
                    last = V.tensor_scalar(R[:, h * TH:(h + 1) * TH], B[h][:, 0:TH], 1.0 / DM, EPS, ALU.mult, ALU.add)
                last.then_inc(S["rms_mean"], 1)
                V.memset(SQS[:], 0.0)
                dve.wait_ge(S["rms_scale"], z + 1)

                def scale(k):
                    gain = vec[:, NORM_G[z] + k:NORM_G[z] + k + 1]
                    dst = TMP[:, k % 2, :] if z < 4 else Y[:, k, :]
                    V.scalar_tensor_tensor(dst, X[:, k, :], gain, R[:], ALU.mult, ALU.mult).then_inc(S["normed"], 1)
                scale(0)
                for k in range(KT):
                    if k + 1 < KT:
                        if 1 <= k and z < 4:
                            dve.wait_ge(S["norm_low"], z * KT + k)
                        scale(k + 1)
                    if z < 4:
                        dve.wait_ge(S["norm_high"], z * KT + k + 1)
                        V.tensor_tensor(HL[:, k, :], TMP[:, k % 2, :], HH[:, k, :].bitcast(F32), ALU.subtract).then_inc(S["norm_low"], 1)

            dve.wait_ge(S["consts"], 1)
            V.tensor_copy(ones_r[:], ones[:])
            V.tensor_copy(after_r[:], after[:]).then_inc(S["ones_r_set"], 1)
            dve.wait_ge(S["vec_turned"], 1)
            V.tensor_copy(vec[:], B[6][:, 0:n_vec]).then_inc(S["vec_set"], 1)
            for k in range(KT):
                dve.wait_ge(S["x_turned"], k + 1)
                V.tensor_copy(X[:, k, 0:NP], B[2 * (k % 2)][:, :])
                V.tensor_copy(X[:, k, NP:T], B[2 * (k % 2) + 1][:, 0:NS]).then_inc(S["x_copied"], 1)
                dve.wait_ge(S["x_squared"], k + 1)
                if k == 0:
                    V.tensor_copy(SQS[:], TMP[:, 0, :]).then_inc(S["x_summed"], 1)
                else:
                    dve.wait_ge(S["x_summed"], k)
                    V.tensor_tensor(SQS[:], SQS[:], TMP[:, k % 2, :], ALU.add).then_inc(S["x_summed"], 1)
            norm(0)
            cut_low(0, 0)
            dve.wait_ge(S["wf_high"], 1)
            V.tensor_tensor(WFL[:], WF[:], WFH[:].bitcast(F32), ALU.subtract).then_inc(S["wf_low"], 1)

            dve.wait_ge(S["lf_copied"], 1)
            V.memset(lf_suf[:, :, :, PG - 1:PG], 0.0).then_inc(S["lf_suffix_step"], 1)
            for j in range(PG - 2, -1, -1):
                dve.wait_ge(S["lf_suffix_step"], PG - 1 - j)
                V.tensor_tensor(lf_suf[:, :, :, j], lf_suf[:, :, :, j + 1], lf_pos[:, :, :, j + 1], ALU.add).then_inc(S["lf_suffix_step"], 1)
            dve.wait_ge(S["lf_suffix_step"], PG)
            V.memset(small[:, 95:96], 0.0).then_inc(S["lf_suffixed"], 1)
            dve.wait_ge(S["lf_tail"], 1)
            V.tensor_copy(D_past[:].rearrange("p b j h -> p (b j) h"),
                          B7[:, :].rearrange("p (h n) -> p n h", h=NH)).then_inc(S["d_past"], 1)

            for L in range(2):
                if L == 1:
                    norm(2)
                if L == 0:
                    dve.wait_ge(S["f_logits"], 1)
                    dve.wait_ge(S["small_in"], 16)
                    V.tensor_tensor(LF[:, 0], B[4][:, 0:(TT + 1) * NH].rearrange("p (i h) -> p i h", h=NH),
                                    bf[:].unsqueeze(1).broadcast_to([P, TT + 1, NH]), ALU.add).then_inc(S["f_biased"], 1)
                unit_loop(dve, evac_in(lambda i: PA[:, ds(i, 1), :].rearrange("p o t -> p (o t)")), G_IN[L], 3 * CT)
                unit_loop(dve, evac_in(lambda i: PB[:, ds(i, 1), :].rearrange("p o t -> p (o t)")), G_IN[L] + 3 * CT, n_b[L])
                if L == 0:
                    dve.wait_ge(S["f_ln"], 1)
                    V.scalar_tensor_tensor(LF[:, 3], LF[:, 0], 0.0, LF[:, 1], ALU.min, ALU.subtract).then_inc(S["f_logf"], 1)
                for n, (kind, i) in enumerate(NAT[L]):
                    if n % 2 == 0:
                        dve.wait_ge(S[f"nat_turned{L}"], n + 1)
                        rows = P if i < TT else NS
                        V.tensor_copy(nat_dst(kind, i), B[n % 4][0:rows, :]).then_inc(S[f"nat_dve{L}"], 1)

                if L == 0:
                    dve.wait_ge(S["F_sums"], 1)
                    V.tensor_scalar(F_neg[:].rearrange("p i h -> p (i h)"), B[5][:, 0:TT * NH], -1.0, None, ALU.mult)
                    V.tensor_scalar(Fn_neg[:], B[5][0:NS, 64:64 + NH], -1.0, None, ALU.mult).then_inc(S["F_set"], 1)
                    dve.wait_ge(S["ws_turned"], 1)
                    for h in range(2):
                        last = V.tensor_tensor(WST[:, 4 * h:4 * h + 4, :], B[6 + h][:, :].rearrange("p (g t) -> p g t", t=P),
                                               upto[:].unsqueeze(1).broadcast_to([P, 4, P]), ALU.mult)
                    last.then_inc(S["ws_masked"], 1)
                    dve.wait_ge(S["rep_done"], 1)
                    rep = B[4][0:NS, 0:GB * NT].rearrange("p (g t) -> p g t", t=NT)
                    for b in range(NB):
                        last = V.tensor_scalar(WBD[:, :, b, :], rep, seq_same[:, b:b + 1], None, ALU.mult)
                    last.then_inc(S["bd_set"], 1)
                    n_ln = 0

                    def ln(ins):
                        nonlocal n_ln
                        n_ln += 1
                        ins.then_inc(S["ln_step"], 1)
                        dve.wait_ge(S["ln_step"], n_ln)

                    ln(V.memset(small[:, 0:96], 1.0))
                    dve.wait_ge(S["nat_act0"], 7)
                    dve.wait_ge(S["sgu_in"], 16 * (3 + GB))
                    for i in range(TT + 1):
                        rows = P if i < TT else NS
                        last = V.bn_stats(small[0:rows, 16 + 6 * i:22 + 6 * i], GN[0:rows, i, :])
                    ln(last)
                    for i in range(TT + 1):
                        rows = P if i < TT else NS
                        last = V.bn_aggr(small[0:rows, 2 * i:2 * i + 2], small[0:rows, 16 + 6 * i:22 + 6 * i])
                    ln(last)
                    var = small[:, 0:2 * TT + 2].rearrange("p (i w) -> p i w", w=2)[:, :, 1]
                    V.tensor_scalar(small[:, 50:50 + TT + 1], var, EPS, None, ALU.add).then_inc(S["ln_var"], 1)
                    dve.wait_ge(S["ln_scale"], 2)
                    for i in range(TT + 1):
                        rows = P if i < TT else NS
                        last = V.tensor_scalar(GN[0:rows, i, :], GN[0:rows, i, :], small[0:rows, 2 * i:2 * i + 1],
                                               small[0:rows, 50 + i:51 + i], ALU.subtract, ALU.mult)
                    ln(last)
                    for i in range(TT + 1):
                        rows = P if i < TT else NS
                        last = V.tensor_tensor(GN[0:rows, i, :], GN[0:rows, i, :], g_row[0:rows, :], ALU.mult)
                    ln(last)
                    for i in range(TT + 1):
                        rows = P if i < TT else NS
                        last = V.tensor_tensor(GN[0:rows, i, :], GN[0:rows, i, :], b_row[0:rows, :], ALU.add)
                    last.then_inc(S["ln_done"], 1)
                    for c in range(CT):
                        dve.wait_ge(S["mixed"], c + 1)
                        t = TMP[:, c % 2, :]
                        V.tensor_tensor(t[:, 0:NP].rearrange("p (i t) -> p i t", t=P), B[c][:, :].rearrange("p (i t) -> p i t", t=P),
                                        bs_row[:, c, :].unsqueeze(1).broadcast_to([P, TT, P]), ALU.add)
                        V.tensor_tensor(t[:, NP:T].rearrange("p (b t) -> p b t", t=NT),
                                        B[5][:, c * NS:(c + 1) * NS].rearrange("p (b t) -> p b t", t=NT),
                                        bs_row[:, c, 0:NT].unsqueeze(1).broadcast_to([P, NB, NT]), ALU.add).then_inc(S["sgu_step"], 1)
                        dve.wait_ge(S["sgu_step"], c + 1)
                        V.tensor_tensor(t, t, PB[:, c, :], ALU.mult).then_inc(S["sgu_out"], 1)
                        dve.wait_ge(S["sgu_high"], c + 1)
                        V.tensor_tensor(HL[:, CT + c, :], t, HH[:, CT + c, :].bitcast(F32), ALU.subtract).then_inc(S["sgu_low"], 1)
                    n_branch = CT
                else:
                    V.memset(UE[:, :, 0:2], 0.0)
                    V.tensor_tensor(UE[:, :, 2:2 + NP], PB[:, CT:2 * CT, 0:NP], PB[:, 2 * CT:3 * CT, 0:NP], ALU.mult)
                    dve.wait_ge(S["state_turned"], 1)
                    for c in range(CT):
                        V.tensor_copy(SE[:, c, :, 0:2], B[4][:, c * 2 * NB:(c + 1) * 2 * NB].rearrange("p (b r) -> p b r", r=2))
                        last = V.tensor_tensor(SE[:, c, :, 2:2 + NT], PB[:, CT + c, NP:T].rearrange("p (b t) -> p b t", t=NT),
                                               PB[:, 2 * CT + c, NP:T].rearrange("p (b t) -> p b t", t=NT), ALU.mult)
                    last.then_inc(S["ue_set"], 1)
                    dve.wait_ge(S["ue_set"], 1)
                    V.tensor_copy(tail[:, :, 0:2], UE[:, :, NP:NP + 2])
                    for c in range(CT):
                        last = V.tensor_copy(tail[:, c, 2:2 + 2 * NB].rearrange("p (b r) -> p b r", r=2), SE[:, c, :, NT:NT + 2])
                    last.then_inc(S["tail_set"], 1)
                    dve.wait_ge(S["tail_turned"], 1)
                    V.tensor_copy(tail_n[:], B[5][0:2 + 2 * NB, :]).then_inc(S["tail_copied"], 1)
                    n_cv = 0
                    for c in range(CT):
                        t = TMP[:, c % 2, :]
                        tp, ts = t[:, 0:NP], t[:, NP:T].rearrange("p (b t) -> p b t", t=NT)
                        for j in range(NCV):
                            w = vec[:, CONV_V + j * CT + c:CONV_V + j * CT + c + 1]
                            up, us = UE[:, c, j:j + NP], SE[:, c, :, j:j + NT]
                            if j == 0:
                                V.tensor_scalar(tp, up, w, None, ALU.mult)
                                V.tensor_scalar(ts, us, w, None, ALU.mult).then_inc(S["conv_step"], 1)
                            else:
                                V.scalar_tensor_tensor(tp, up, w, tp, ALU.mult, ALU.add)
                                V.scalar_tensor_tensor(ts, us, w, ts, ALU.mult, ALU.add).then_inc(S["conv_step"], 1)
                            n_cv += 1
                            dve.wait_ge(S["conv_step"], n_cv)
                        V.tensor_tensor(t, t, PB[:, c, :], ALU.mult).then_inc(S["conv_out"], 1)
                        dve.wait_ge(S["conv_high"], c + 1)
                        V.tensor_tensor(HL[:, CT + c, :], t, HH[:, CT + c, :].bitcast(F32), ALU.subtract).then_inc(S["conv_low"], 1)

                dve.wait_ge(S["stored_kn"], 32 * (L + 1))
                if L == 0:
                    dve.wait_ge(S["stored"], 16 * 5)
                else:
                    dve.wait_ge(S["stored"], 16 * 9)
                V.memset(QB[:], 0.0).then_inc(S["q_block%d" % L], 1)
                V.memset(SL[:], 0.0)
                V.memset(SS[:], NEG)
                V.memset(RD[:], 0.0)
                dve.wait_ge(S[f"q_block{L}"], 1)
                for e in range(2):
                    r = slice(HD * e, HD * e + HD)
                    last = V.tensor_scalar(QB[r, :, :, e, :], PA[r, 0:CT, NP:T].rearrange("p c (b t) -> p c b t", t=NT), QS, None, ALU.mult)
                last.then_inc(S[f"q_block{L}"], 1)
                if L == 0:
                    for b in range(NB):
                        last = V.tensor_tensor(NBI[:, b, :, :], seq_neg_causal[:, b, :].unsqueeze(1).broadcast_to([NS, NH, NT]),
                                               Fn_neg[:].unsqueeze(2).broadcast_to([NS, NH, NT]), ALU.add)
                    last.then_inc(S["nbi_set"], 1)
                    dve.wait_ge(S["nbi_set"], 1)
                ex = PG * HT
                with dve.Fori(0, CT) as it:
                    for e in range(2):
                        s = it * 2 + e
                        r = slice(HD * e, HD * e + HD)
                        if e == 0:
                            dve.wait_ge(S["pair_high"], it + (CT * L + 1))
                            V.scalar_tensor_tensor(qL[:], PA[:, ds(it, 1), 0:NP].rearrange("p o t -> p (o t)"), QS, qH[:].bitcast(F32), ALU.mult, ALU.subtract)
                            V.tensor_tensor(kL[:], PA[:, ds(it + CT, 1), 0:NP].rearrange("p o t -> p (o t)"), kH[:].bitcast(F32), ALU.subtract)
                            V.tensor_tensor(vL[:], VN[:, 0:TT, ds(it * P, P)], vH[:].bitcast(F32), ALU.subtract).then_inc(S["pair_low"], 1)
                        if L == 0:
                            dve.wait_ge(S["scores"], s + 1)
                            for j in range(TT):
                                last = V.tensor_scalar(S_[:, OFF[j]:OFF[j] + WID[j]], sc_bank(j, 0, WID[j]), F_neg[:, j, ds(s, 1)], None, ALU.add)
                            last.then_inc(S["biased"], 1)
                            dve.wait_ge(S["biased"], s + 1)
                            for j in range(TT):
                                d = S_[:, OFF[j]:OFF[j] + P]
                                last = V.tensor_tensor(d, d, neg_causal[:], ALU.add)
                            last.then_inc(S["masked"], 1)
                            dve.wait_ge(S["masked"], s + 1)
                            V.tensor_tensor(MX[:], S_[:, P:NP], S_[:, OFF[1]:OFF[1] + WID[1]], ALU.max).then_inc(S["max_step"], 1)
                            for j in range(2, TT):
                                dve.wait_ge(S["max_step"], s * (TT - 1) + (j - 1))
                                m = MX[:, (j - 1) * P:]
                                V.tensor_tensor(m, m, S_[:, OFF[j]:OFF[j] + WID[j]], ALU.max).then_inc(S["max_step"], 1)
                            dve.wait_ge(S["dec_scores"], s + 1)
                            V.memset(SS[NS:P, ex:], NEG)
                            V.tensor_tensor(SS[:, 0:ex].rearrange("p (n t) -> p n t", t=NT), B7[:, :].rearrange("p (n t) -> p n t", t=NT),
                                            D_past[:, ds(s, 1), :, :].rearrange("p o j h -> p (o j h)").unsqueeze(2).broadcast_to([P, PG * NH, NT]), ALU.add)
                            V.tensor_tensor(SS[0:NS, ex:ex + HT], B5[0:NS, 0:HT], NBI[:, ds(s, 1), :, :].rearrange("p o h t -> p (o h t)"),
                                            ALU.add).then_inc(S["dec_biased"], 1)
                            dve.wait_ge(S["dec_biased"], s + 1)
                            V.tensor_reduce(RD[:, 0:HT], SS[:].rearrange("p (j n) -> p n j", n=HT), AX.X, ALU.max).then_inc(S["dec_max_part"], 1)
                            dve.wait_ge(S["max_turned"], s + 1)
                            V.tensor_reduce(small[:, 0:TT], B[3][:, :].rearrange("p (i k) -> p i k", k=P), AX.X, ALU.max).then_inc(S["max_rows"], 1)
                            dve.wait_ge(S["max_rows"], s + 1)
                            V.tensor_tensor(MD[:], ident[:].unsqueeze(1).broadcast_to([P, TT, P]),
                                            small[:, 0:TT].unsqueeze(2).broadcast_to([P, TT, P]), ALU.mult).then_inc(S["max_diag"], 1)
                            dve.wait_ge(S["dec_max_turned"], s + 1)
                            V.tensor_reduce(small[0:HT, 8:9], B[6][0:HT, 0:P], AX.X, ALU.max).then_inc(S["dec_max_rows"], 1)
                            dve.wait_ge(S["dec_max_rows"], s + 1)
                            V.tensor_scalar(MDD[:], ident[0:HT, 0:HT], small[0:HT, 8:9], None, ALU.mult).then_inc(S["dec_max_diag"], 1)
                            dve.wait_ge(S["max_spread"], s + 1)
                            for j in range(TT):
                                sj = S_[:, OFF[j]:OFF[j] + WID[j]]
                                last = V.tensor_tensor(sj, sj, B[3][:, j * P:NP], ALU.subtract)
                            last.then_inc(S["shifted"], 1)
                            dve.wait_ge(S["dec_max_spread"], s + 1)
                            V.tensor_tensor(SS[:].rearrange("p (j n) -> p j n", n=HT), SS[:].rearrange("p (j n) -> p j n", n=HT),
                                            B[5][:, 0:HT].unsqueeze(1).broadcast_to([P, PG + 1, HT]), ALU.subtract).then_inc(S["dec_shifted"], 1)
                        else:
                            for j in range(PG):
                                dve.wait_ge(S["k_turned1"], s * PG + (j + 5))
                                V.tensor_copy(KTS[:, j % 2, :], B[5 + j % 2][:, :]).then_inc(S["kt_copied1"], 1)
                            dve.wait_ge(S["sb_ln"], s + 1)
                            for o in range(0, SC, 512):
                                n = min(512, SC - o)
                                last = V.scalar_tensor_tensor(S_[:, o:o + n], B[o // 512][:, 0:n], 0.0, L_[:, o:o + n], ALU.min, ALU.subtract)
                            last.then_inc(S["sb_min"], 1)
                            dve.wait_ge(S["sb_min"], s + 1)
                            for o in range(0, SC, 512):
                                n = min(512, SC - o)
                                last = V.scalar_tensor_tensor(L_[:, o:o + n], B[o // 512][:, 0:n], 0.0, L_[:, o:o + n], ALU.max, ALU.add)
                            last.then_inc(S["sb_ls"], 1)
                            dve.wait_ge(S["sb_ls"], s + 1)
                            for j in range(TT):
                                d, l = S_[:, OFF[j]:OFF[j] + P], L_[:, OFF[j]:OFF[j] + P]
                                V.tensor_tensor(d, d, neg_strict[:], ALU.add)
                                last = V.tensor_tensor(l, l, before[:], ALU.mult)
                            last.then_inc(S["sb_sp"], 1)
                            dve.wait_ge(S["sp_high"], s + 1)
                            V.tensor_tensor(PL[:], L_[:], PH[:].bitcast(F32), ALU.subtract).then_inc(S["sp_low"], 1)
                            dve.wait_ge(S["dsb_ln"], s + 1)
                            V.memset(SS[NS:P, ex:], NEG)
                            V.scalar_tensor_tensor(SS[:, 0:ex], B7[:, :], 0.0, SL[:, 0:ex], ALU.min, ALU.subtract)
                            V.scalar_tensor_tensor(SS[0:NS, ex:], B5[0:NS, 0:HT], 0.0, SL[0:NS, ex:], ALU.min, ALU.subtract).then_inc(S["dsb_min"], 1)
                            dve.wait_ge(S["dsb_min"], s + 1)
                            V.scalar_tensor_tensor(SL[:, 0:ex], B7[:, :], 0.0, SL[:, 0:ex], ALU.max, ALU.add)
                            V.scalar_tensor_tensor(SL[0:NS, ex:], B5[0:NS, 0:HT], 0.0, SL[0:NS, ex:], ALU.max, ALU.add).then_inc(S["dsb_sp"], 1)
                            dve.wait_ge(S["dsb_sp"], s + 1)
                            h3 = lambda t: t[0:NS, ex:].rearrange("p (h t) -> p h t", t=NT)
                            V.tensor_tensor(h3(SL), h3(SL), seq_before[:, ds(s, 1), :].broadcast_to([NS, NH, NT]), ALU.mult)
                            V.tensor_tensor(h3(SS), h3(SS), seq_neg_strict[:, ds(s, 1), :].broadcast_to([NS, NH, NT]), ALU.add).then_inc(S["dsb_masked"], 1)
                            dve.wait_ge(S["dsb_masked"], s + 1)
                            V.tensor_copy(SUF[:, PG - 1, :], SL[:, ex:]).then_inc(S["dec_suffix"], 1)
                            for j in range(PG - 2, -1, -1):
                                dve.wait_ge(S["dec_suffix"], s * PG + (PG - 1 - j))
                                V.tensor_tensor(SUF[:, j, :], SUF[:, j + 1, :], SL[:, (j + 1) * HT:(j + 2) * HT], ALU.add).then_inc(S["dec_suffix"], 1)
                            dve.wait_ge(S["cum"], s + 1)
                            for o in range(0, SC, 512):
                                n = min(512, SC - o)
                                last = V.tensor_tensor(S_[:, o:o + n], S_[:, o:o + n], B[o // 512][:, 0:n], ALU.subtract)
                            last.then_inc(S["shifted"], 1)
                            dve.wait_ge(S["dec_cum"], s + 1)
                            V.tensor_tensor(SS[:, 0:ex], SS[:, 0:ex], B[6][:, :], ALU.subtract)
                            V.tensor_tensor(SS[0:NS, ex:], SS[0:NS, ex:], B[5][0:NS, 0:HT], ALU.subtract).then_inc(S["dec_shifted"], 1)
                        dve.wait_ge(S["p_high"], s + (NB * L + 1))
                        V.tensor_tensor(PL[:], S_[:], PH[:].bitcast(F32), ALU.subtract).then_inc(S["p_low"], 1)
                        dve.wait_ge(S[f"prompt_av{L}"], s + 2)
                        if L == 0:
                            V.reciprocal(RD[:], B[3][:, :]).then_inc(S["rden"], 1)
                            dve.wait_ge(S["rden"], s + 1)
                            V.tensor_tensor(OT[r, :], B4[r, :], RD[r, :], ALU.mult).then_inc(S["prompt_out"], 1)
                        else:
                            V.tensor_copy(OT[r, :], B4[r, :]).then_inc(S["prompt_out"], 1)
                        if e == 1:
                            dve.wait_ge(S["o_high"], it + (CT * L + 1))
                            V.tensor_tensor(HL[:, ds(it, 1), 0:NP].rearrange("p o t -> p (o t)"), OT[:],
                                            HH[:, ds(it, 1), 0:NP].rearrange("p o t -> p (o t)").bitcast(F32), ALU.subtract).then_inc(S["o_low"], 1)
                        dve.wait_ge(S["dec_av"], s + (NB * L + 1))
                        if L == 0:
                            dve.wait_ge(S["prompt_out"], s + 1)
                            V.reciprocal(RD[:, 0:HT], B[6][:, 0:HT]).then_inc(S["dec_rden"], 1)
                            dve.wait_ge(S["dec_rden"], s + 1)
                        for f in range(2):
                            rf = slice(HD * f, HD * f + HD)
                            src = B[5][rf, 0:HT].rearrange("p (c h t) -> p c h t", h=2, t=NT)[:, :, f, :]
                            dst = OS[rf, :, ds(s * NT, NT)]
                            if L == 0:
                                last = V.tensor_tensor(dst, src, RD[rf, 0:HT].rearrange("p (c h t) -> p c h t", h=2, t=NT)[:, :, f, :], ALU.mult)
                            else:
                                last = V.tensor_copy(dst, src)
                        last.then_inc(S[f"dec_out{L}"], 1)
                dve.wait_ge(S["os_high"], L + 1)
                V.tensor_tensor(HL[:, 0:CT, NP:T], OS[:], HH[:, 0:CT, NP:T].bitcast(F32), ALU.subtract).then_inc(S["os_low"], 1)

                unit_loop(dve, evac_add(True), G_OUT[L], KT)
                norm(1 + 2 * L)
                g = G_MLP[L]
                for n, (kind, grp) in enumerate(MLP_ORDER):
                    last = L == 1 and n == len(MLP_ORDER) - 1
                    body = evac_up(L, grp) if kind == "up" else evac_add(grp == FG - 1)
                    unit_loop(dve, body, g, KT, last)
                    g += KT
            norm(4)
            for k in range(KT):
                dve.wait_ge(S["y_turned"], k + 1)
                V.tensor_copy(XN[:, 0:TT, k * P:(k + 1) * P], B[2 * (k % 2)][:, :].rearrange("p (i c) -> p i c", c=P))
                V.tensor_copy(XN[0:NS, TT, k * P:(k + 1) * P], B[2 * (k % 2) + 1][0:NS, 0:P]).then_inc(S["y_copied"], 1)

        @block.tensor
        def _(pe):
            M = nc.tensor.matmul
            TR = nc.tensor.transpose
            pe.sem_inc(S["unit_done"], 1)
            for L in range(2):
                pe.sem_inc(S[f"k_turned{L}"], 4)
                pe.sem_inc(S[f"v_used{L}"], 1)
                pe.sem_inc(S[f"prompt_av{L}"], 1)
                pe.sem_inc(S[f"dec_out{L}"], 1)

            def unit(hi, lo, also=None):
                def body(g, i, u, more):
                    pe.wait_ge(S["w_low"], g + 3)
                    pe.wait_ge(S["evac_act"], g + 1)
                    pe.wait_ge(S["evac_dve"], g + 1)
                    for k in range(KT):
                        for n, (w, x) in enumerate(((WH, hi), (WH, lo), (WL, hi))):
                            for h in range(2):
                                last = M(B[2 * u + h][:, 0:TH], w[u][:, k, :], x[:, k, h * TH:(h + 1) * TH],
                                         start=(k == 0 and n == 0), stop=(k == KT - 1 and n == 2))
                    last.then_inc(S["unit_done"], 1)
                return body

            def rms(z, name, value):
                pe.wait_ge(S[name], value)
                for h in range(2):
                    last = M(B[h][:, 0:TH], ones[:], SQS[:, h * TH:(h + 1) * TH], start=True, stop=True)
                last.then_inc(S["rms_sum"], 1)

            pe.wait_ge(S["consts"], 1)
            pe.wait_ge(S["vec_in"], 64)
            TR(B[6][:, 0:n_vec], vec_rows[:], ident[0:n_vec, 0:n_vec]).then_inc(S["vec_turned"], 1)
            pe.wait_ge(S["x_in"], 32)
            for k in range(KT):
                if k >= 2:
                    pe.wait_ge(S["x_copied"], k - 1)
                for i in range(TT):
                    TR(B[2 * (k % 2)][:, i * P:(i + 1) * P], XN[:, i, k * P:(k + 1) * P], ident[:])
                TR(B[2 * (k % 2) + 1][:, 0:NS], XN[0:NS, TT, k * P:(k + 1) * P], ident[0:NS, 0:NS]).then_inc(S["x_turned"], 1)
            rms(0, "x_summed", KT)
            pe.wait_ge(S["lfp_in"], 16 * NB * PG)
            for h in range(NH):
                last = TR(B[7][:, h * NB * PG:(h + 1) * NB * PG], lf_raw[:, :, h], ident[0:NB * PG, 0:NB * PG])
            last.then_inc(S["lf_turned"], 1)
            pe.wait_ge(S["lf_suffixed"], 1)
            flat = lambda t: t[:].rearrange("p h b j -> p (h b j)")
            M(B[7][:, :], after[:], flat(lf_pos), start=True, stop=False)
            M(B[7][:, :], ones[:], flat(lf_suf), start=False, stop=True).then_inc(S["lf_tail"], 1)

            for L in range(2):
                if L == 1:
                    rms(2, "sum_step", 2 * KT)
                pe.wait_ge(S["norm_low"], (2 * L + 1) * KT)
                if L == 0:
                    pe.wait_ge(S["wf_low"], 1)
                    for i in range(TT + 1):
                        c0 = i * P if i < TT else T - P
                        for k in range(KT):
                            for n, (x, w) in enumerate(((HH, WFH), (HL, WFH), (HH, WFL))):
                                last = M(B[4][:, i * NH:(i + 1) * NH], x[:, k, c0:c0 + P], w[:, k, :],
                                         start=(k == 0 and n == 0), stop=(k == KT - 1 and n == 2))
                    last.then_inc(S["f_logits"], 1)
                unit_loop(pe, unit(HH, HL), G_IN[L], 3 * CT + n_b[L])
                g_last = G_IN[L] + 3 * CT + n_b[L] - 1
                pe.wait_ge(S["evac_act"], g_last + 3)
                pe.wait_ge(S["evac_dve"], g_last + 3)
                for n, (kind, i) in enumerate(NAT[L]):
                    if n >= 4:
                        pe.wait_ge(S[f"nat_dve{L}" if n % 2 == 0 else f"nat_act{L}"], (n - 4) // 2 + 1)
                    for c in range(CT):
                        src = nat_src(kind, c, i)
                        rows = P if i < TT else NS
                        last = TR(B[n % 4][0:rows, c * P:(c + 1) * P], src, ident[:])
                    last.then_inc(S[f"nat_turned{L}"], 1)

                if L == 0:
                    pe.wait_ge(S["f_logf"], 1)
                    for i in range(TT):
                        for ii in range(i + 1):
                            M(B[5][:, i * NH:(i + 1) * NH], (upto if ii == i else ones)[:], LF[:, 3, ii, :], start=(ii == 0), stop=(ii == i))
                    M(B[5][0:NS, 64:64 + NH], seq_upto[NS:P].rearrange("p b t -> p (b t)"), LF[NS:P, 3, TT, :],
                      start=True, stop=True).then_inc(S["F_sums"], 1)
                    pe.wait_ge(S["sgu_in"], 16 * (3 + GB))
                    for g in range(GB):
                        last = TR(B[6 + g // 4][:, (g % 4) * P:(g % 4 + 1) * P], WSN[:, g, :], ident[:])
                    last.then_inc(S["ws_turned"], 1)
                    pe.wait_ge(S["ws_masked"], 1)
                    M(B[4][0:NS, 0:GB * NT], step_rep[:].rearrange("p b t -> p (b t)"), WST[0:NT, :, 0:NT], start=True, stop=True).then_inc(S["rep_done"], 1)
                    pe.wait_ge(S["bd_set"], 1)
                    pe.wait_ge(S["ln_done"], 1)
                    for c in range(CT):
                        for e in range(2):
                            g = 2 * c + e
                            r = slice(HD * e, HD * e + HD)
                            for i in range(TT):
                                M(B[c][r, i * P:(i + 1) * P], GN[:, i, g * HD:(g + 1) * HD], WST[:, g, :], start=True, stop=True)
                            last = M(B[5][r, c * NS:(c + 1) * NS], GN[0:NS, TT, g * HD:(g + 1) * HD],
                                     WBD[:, g].rearrange("p b t -> p (b t)"), start=True, stop=True)
                    last.then_inc(S["mixed"], CT)
                else:
                    pe.wait_ge(S["state_in"], 16)
                    for c in range(CT):
                        last = TR(B[4][:, c * 2 * NB:(c + 1) * 2 * NB], prev_n[0:2 * NB, c * P:(c + 1) * P], ident[0:2 * NB, 0:2 * NB])
                    last.then_inc(S["state_turned"], 1)
                    pe.wait_ge(S["tail_set"], 1)
                    for c in range(CT):
                        last = TR(B[5][0:2 + 2 * NB, c * P:(c + 1) * P], tail[:, c, :], ident[:])
                    last.then_inc(S["tail_turned"], 1)

                pe.wait_ge(S[f"q_block{L}"], 2)
                if L == 0:
                    pe.wait_ge(S["sgu_low"], CT)
                else:
                    pe.wait_ge(S["conv_low"], CT)
                with pe.Fori(0, CT) as it:
                    for e in range(2):
                        s = it * 2 + e
                        r = slice(HD * e, HD * e + HD)
                        pe.wait_ge(S[f"dec_out{L}"], s + 1)
                        if e == 0:
                            pe.wait_ge(S["pair_low"], it + (CT * L + 1))
                        for j in (0, 1, 3, 2):
                            for n, (a, b) in enumerate(((kH, qH), (kH, qL), (kL, qH))):
                                last = M(sc_bank(j, 0, WID[j]), a[r, j * P:(j + 1) * P], b[r, j * P:NP], start=(n == 0), stop=(n == 2))
                        last.then_inc(S["scores"], 1)

                        def page_scores(j):
                            pe.wait_ge(S[f"kt_copied{L}"], s * PG + (j + 1))
                            for c in range(CT):
                                M(B7[:, j * HT + c * 2 * NT:j * HT + (c + 1) * 2 * NT], KTS[:, j % 2, c * P:(c + 1) * P],
                                  QB[:, c, ds(s, 1), :, :].rearrange("p o h t -> p (o h t)"), start=True, stop=True)

                        for j in range(PG):
                            pe.wait_ge(S[f"k_in{L}_{j % 4}"], s * (16 * PG // 4) + 16 * (j // 4 + 1))
                            if j >= 2:
                                pe.wait_ge(S[f"kt_copied{L}"], s * PG + (j - 1))
                            for c in range(CT):
                                last = TR(B[5 + j % 2][:, c * P:(c + 1) * P], KR[:, j % 4, c * P:(c + 1) * P], ident[:])
                            last.then_inc(S[f"k_turned{L}"], 1)
                            if j >= 1:
                                page_scores(j - 1)
                        page_scores(PG - 1)
                        for c in range(CT):
                            last = M(B5[0:NS, c * 2 * NT:(c + 1) * 2 * NT], PA[:, CT + c, NP:T],
                                     QB[:, c, ds(s, 1), :, :].rearrange("p o h t -> p (o h t)"), start=True, stop=True)
                        last.then_inc(S["dec_scores"], 1)

                        if L == 0:
                            pe.wait_ge(S["max_step"], s * (TT - 1) + (TT - 1))
                            for i in range(TT):
                                src = S_[:, 0:P] if i == 0 else MX[:, (i - 1) * P:i * P]
                                last = TR(B[3][:, i * P:(i + 1) * P], src, ident[:])
                            last.then_inc(S["max_turned"], 1)
                            pe.wait_ge(S["dec_max_part"], s + 1)
                            TR(B[6][:, 0:P], RD[:, 0:P], ident[:]).then_inc(S["dec_max_turned"], 1)
                            pe.wait_ge(S["max_diag"], s + 1)
                            M(B[3][:, :], ones_r[:], MD[:].rearrange("p i q -> p (i q)"), start=True, stop=True).then_inc(S["max_spread"], 1)
                            pe.wait_ge(S["dec_max_diag"], s + 1)
                            M(B[5][:, 0:HT], ones_r[0:HT, :], MDD[:], start=True, stop=True).then_inc(S["dec_max_spread"], 1)
                        else:
                            pe.wait_ge(S["sp_low"], s + 1)
                            for j in (0, 1, 3, 2):
                                for jj in range(j, TT):
                                    d = (jj - j) * P
                                    for n, x in enumerate((PH, PL)):
                                        last = M(sc_bank(j, d, WID[jj]), (after_r if jj == j else ones_r)[:], x[:, OFF[jj]:OFF[jj] + WID[jj]],
                                                 start=(jj == j and n == 0), stop=(jj == TT - 1 and n == 1))
                            last.then_inc(S["cum"], 1)
                            pe.wait_ge(S["dec_suffix"], s * PG + PG)
                            ex = PG * HT
                            M(B[6][:, :], after[:], SL[:, 0:ex], start=True, stop=False)
                            M(B[6][:, :], ones[:], SUF[:].rearrange("p j n -> p (j n)"), start=False, stop=True)
                            M(B[5][0:NS, 0:HT], after[0:NS, 0:NS], SL[0:NS, ex:ex + HT], start=True, stop=True).then_inc(S["dec_cum"], 1)

                        pe.wait_ge(S["p_low"], s + (NB * L + 1))
                        if L == 0:
                            for j in range(TT):
                                for n, x in enumerate((PH, PL)):
                                    M(B[3][:, j * P:NP], ones_r[:], x[:, OFF[j]:OFF[j] + WID[j]], start=(j == 0 and n == 0), stop=(j == TT - 1 and n == 1))
                        for j in range(TT):
                            for n, (a, b) in enumerate(((vH, PH), (vH, PL), (vL, PH))):
                                last = M(B4[:, j * P:NP], a[:, j, :], b[:, OFF[j]:OFF[j] + WID[j]], start=(j == 0 and n == 0), stop=(j == TT - 1 and n == 2))
                        last.then_inc(S[f"prompt_av{L}"], 1)
                        pe.wait_ge(S["dec_probs"], s + (NB * L + 1))
                        if L == 0:
                            for j in range(PG + 1):
                                M(B[6][:, 0:HT], ones[:], SS[:, j * HT:(j + 1) * HT], start=(j == 0), stop=(j == PG))
                        pe.wait_ge(S[f"v_in{L}"], s * (16 * PG) + 16 * PG)
                        for c in range(CT):
                            o = c * 2 * NT
                            for j in range(PG):
                                last = M(B[5][:, o:o + 2 * NT], VR[:, j, c * P:(c + 1) * P], SS[:, j * HT + o:j * HT + o + 2 * NT], start=(j == 0), stop=False)
                            if c == CT - 1:
                                last.then_inc(S[f"v_used{L}"], 1)
                            last = M(B[5][:, o:o + 2 * NT], VN[0:NS, TT, c * P:(c + 1) * P], SS[0:NS, PG * HT + o:PG * HT + o + 2 * NT], start=False, stop=True)
                        last.then_inc(S["dec_av"], 1)

                pe.wait_ge(S["o_low"], CT * (L + 1))
                pe.wait_ge(S["os_low"], L + 1)
                unit_loop(pe, unit(HH, HL), G_OUT[L], KT)
                rms(1 + 2 * L, "sum_step", (2 * L + 1) * KT)
                pe.wait_ge(S["norm_low"], (2 * L + 2) * KT)
                g = G_MLP[L]
                up_end = {}
                for n, (kind, grp) in enumerate(MLP_ORDER):
                    if kind == "up":
                        unit_loop(pe, unit(HH, HL), g, KT)
                        up_end[grp] = g + KT - 1
                    else:
                        pe.wait_ge(S["evac_dve"], up_end[grp] + 3)
                        unit_loop(pe, unit(ffH[grp % 2], ffL[grp % 2]), g, KT)
                    g += KT
            rms(4, "sum_step", 4 * KT)
            for k in range(KT):
                pe.wait_ge(S["normed"], 4 * KT + k + 1)
                if k >= 2:
                    pe.wait_ge(S["y_copied"], k - 1)
                for i in range(TT):
                    TR(B[2 * (k % 2)][:, i * P:(i + 1) * P], Y[:, k, i * P:(i + 1) * P], ident[:])
                TR(B[2 * (k % 2) + 1][0:NS, 0:P], Y[:, k, NP:T], ident[:]).then_inc(S["y_turned"], 1)


_INS = ["x_prompt", "x_sample", "cache_fox_k", "cache_fox_v", "cache_fox_logf", "cache_sb_k", "cache_sb_v", "state_conv",
        "page_table", "g_mix", "g_mlp", "g_final", "w_up", "w_down", "w_in_even", "b_forget", "sgu_g", "sgu_b",
        "w_spatial", "b_spatial", "w_out_even", "w_in_odd", "conv_w", "w_out_odd"]
_OUTS = [(1, 512, 1024), (8, 8, 1024), (1, 1, 512, 8, 64), (1, 1, 512, 8, 64), (1, 1, 512, 8), (1, 1, 512, 8, 64),
         (1, 1, 512, 8, 64), (1, 1, 2, 512), (1, 8, 8, 8, 64), (1, 8, 8, 8, 64), (1, 8, 8, 8), (1, 8, 8, 8, 64),
         (1, 8, 8, 8, 64), (1, 8, 2, 512), (1, 8, 8, 512)]


def kernel(**inputs):
    import numpy as _np
    import concourse.bacc as _bacc
    from concourse import mybir as _mybir
    from concourse.bass_utils import run_bass_kernel_spmd as _run

    nc = _bacc.Bacc("TRN2", target_bir_lowering=False, num_devices=1)
    arrays, args = {}, []
    for name in _INS:
        a = _np.ascontiguousarray(inputs[name])
        arrays[f"in_{name}_dram"] = a
        args.append(nc.dram_tensor(f"in_{name}_dram", a.shape, _mybir.dt.from_np(a.dtype), kind="ExternalInput").ap())
    for i, shape in enumerate(_OUTS):
        args.append(nc.dram_tensor(f"out_{i}_dram", shape, _mybir.dt.float32, kind="ExternalOutput").ap())
    trunk(nc, *args)
    r = _run(nc, [arrays], core_ids=[0])
    return tuple(r.results[0][f"out_{i}_dram"] for i in range(len(_OUTS)))
```

```python
import concourse.bass as bass
from concourse import mybir
from contextlib import ExitStack



def trunk(nc, x_prompt, x_sample, cache_fox_k, cache_fox_v, cache_fox_logf, cache_sb_k, cache_sb_v, state_conv,
          page_table, g_mix, g_mlp, g_final, w_up, w_down, w_in_even, b_forget, sgu_g, sgu_b, w_spatial,
          b_spatial, w_out_even, w_in_odd, conv_w, w_out_odd,
          y_prompt, y_sample, p_fox_k, p_fox_v, p_fox_logf, p_sb_k, p_sb_v, p_conv,
          s_fox_k, s_fox_v, s_fox_logf, s_sb_k, s_sb_v, s_conv, s_sgu_v):
    F32, F32R, I32 = mybir.dt.float32, mybir.dt.float32r, mybir.dt.int32
    ALU, ACT, AX = mybir.AluOpType, mybir.ActivationFunctionType, mybir.AxisListType
    ds = bass.ds

    P = 128
    NP = x_prompt.shape[1]
    NB, NT = x_sample.shape[0], x_sample.shape[1]
    NS = NB * NT
    T = NP + NS
    TH = T // 2
    DM = x_prompt.shape[2]
    KT = DM // P
    TT = NP // P
    NH, HD = cache_fox_k.shape[3], cache_fox_k.shape[4]
    DA = NH * HD
    CT = DA // P
    POOL = cache_fox_k.shape[1]
    PG = page_table.shape[1]
    FG = w_up.shape[2] // DM
    GB = w_spatial.shape[1]
    QS = float(HD) ** -0.5
    EPS = 1e-6
    NEG = -1e30
    HT = NH * NT
    NCV = conv_w.shape[1]

    G_IN0, G_OUT0 = 0, 5 * CT
    G_MLP0 = G_OUT0 + KT
    G_IN1 = G_MLP0 + 2 * FG * KT
    G_OUT1 = G_IN1 + 6 * CT
    G_MLP1 = G_OUT1 + KT
    G_END = G_MLP1 + 2 * FG * KT

    ctx = ExitStack()
    with ctx:
        at = [16512]

        def place(name, shape, dt, offset=None):
            n = 4
            for d in shape[1:]:
                n *= d
            if offset is None:
                offset = at[0]
                at[0] += (n + 31) // 32 * 32
            return nc.alloc_sbuf_tensor_at(name, shape, dt, offset=offset)

        X = place("X", [P, KT, T], F32)
        h_addr = at[0]
        HH = place("HH", [P, KT, T], F32R)
        HL = place("HL", [P, KT, T], F32R)
        Y = place("Y", [P, KT, T], F32, h_addr)
        WR = [place(f"WR{i}", [P, KT, P], F32) for i in range(2)]
        WH = [place(f"WH{i}", [P, KT, P], F32R) for i in range(2)]
        WL = [place(f"WL{i}", [P, KT, P], F32R) for i in range(2)]
        R = place("R", [P, T], F32)
        SQS = place("SQS", [P, T], F32)
        TMP = place("TMP", [P, 2, T], F32)
        ident = place("ident", [P, P], F32)
        ones = place("ones", [P, P], F32)
        ones_r = place("ones_r", [P, P], F32R)
        upto = place("upto", [P, P], F32)
        after = place("after", [P, P], F32)
        after_r = place("after_r", [P, P], F32R)
        before = place("before", [P, P], F32)
        neg_causal = place("neg_causal", [P, P], F32)
        neg_strict = place("neg_strict", [P, P], F32)
        seq_upto = place("seq_upto", [P, NB, NT], F32)
        seq_before = place("seq_before", [NS, NB, NT], F32)
        seq_neg_causal = place("seq_neg_causal", [NS, NB, NT], F32)
        seq_neg_strict = place("seq_neg_strict", [NS, NB, NT], F32)
        seq_same = place("seq_same", [NS, NB], F32)
        step_rep = place("step_rep", [NT, NB, NT], F32)
        n_vec = 5 * KT + 3 * CT
        vec = place("vec", [P, n_vec], F32)
        pages = place("pages", [1, NB * PG], I32)
        bf = place("bf", [P, NH], F32)
        LF = place("LF", [P, 4, TT + 1, NH], F32)
        F_neg = place("F_neg", [P, TT, NH], F32)
        Fn_neg = place("Fn_neg", [NS, NH], F32)
        D_past = place("D_past", [P, NB, PG, NH], F32)
        small = place("small", [P, 96], F32)
        arena = at[0]
        ffH = [place(f"ffH{i}", [P, KT, T], F32R, arena + i * 2 * KT * T * 4) for i in range(2)]
        ffL = [place(f"ffL{i}", [P, KT, T], F32R, arena + (i * 2 + 1) * KT * T * 4) for i in range(2)]
        at[0] = arena
        XN = place("XN", [P, TT + 1, DM], F32, arena)
        PA = place("PA", [P, 3 * CT, T], F32)
        VN = place("VN", [P, TT + 1, DA], F32)
        KR = place("KR", [P, 4, DA], F32)
        vr_addr = at[0]
        VR = place("VR", [P, PG, DA], F32)
        vec_rows = place("vec_rows", [n_vec, P], F32, vr_addr + 8192)
        lf_raw = place("lf_raw", [NB * PG, P, NH], F32, vr_addr)
        lf_pos = place("lf_pos", [P, NH, NB, PG], F32, vr_addr + 4096)
        lf_suf = place("lf_suf", [P, NH, NB, PG], F32, vr_addr + 6144)
        WSN = place("WSN", [P, GB, P], F32, vr_addr)
        WST = place("WST", [P, GB, P], F32, vr_addr + 4096)
        g_row = place("g_row", [P, DA], F32, vr_addr + 8192)
        b_row = place("b_row", [P, DA], F32, vr_addr + 10240)
        bs_row = place("bs_row", [P, CT, P], F32, vr_addr + 12288)
        WBD = place("WBD", [NS, GB, NB, NT], F32, vr_addr + 14336)
        scratch = at[0]
        PB = place("PB", [P, 3 * CT, T], F32)
        KN = place("KN", [P, TT + 1, DA], F32)
        after_kn = at[0]
        GN = place("GN", [P, TT + 1, DA], F32)
        wf_addr = after_kn - (TT + 1) * DA * 4
        WF = place("WF", [P, KT, P], F32, wf_addr)
        WFH = place("WFH", [P, KT, P], F32R, wf_addr + KT * P * 4)
        WFL = place("WFL", [P, KT, P], F32R, wf_addr + 2 * KT * P * 4)
        FT = place("FT", [NH, T], F32, wf_addr + 3 * KT * P * 4)
        at[0] = after_kn
        UE = place("UE", [P, CT, 2 + NP], F32)
        SE = place("SE", [P, CT, NB, 2 + NT], F32)
        tail = place("tail", [P, CT, 2 + 2 * NB], F32)
        tail_n = place("tail_n", [2 + 2 * NB, DA], F32)
        prev_n = tail_n
        at[0] = scratch
        KTS = place("KTS", [P, 2, 4 * P], F32)
        qH = place("qH", [P, NP], F32R)
        qL = place("qL", [P, NP], F32R)
        kH = place("kH", [P, NP], F32R)
        kL = place("kL", [P, NP], F32R)
        vH = place("vH", [P, TT, P], F32R)
        vL = place("vL", [P, TT, P], F32R)
        SC = 5 * 2 * P
        S_ = place("S_", [P, SC], F32)
        l_addr = at[0]
        L_ = place("L_", [P, SC], F32)
        MD = place("MD", [P, TT, P], F32R, l_addr)
        MX = place("MX", [P, NP - P], F32, l_addr + 2048)
        PH = place("PH", [P, SC], F32R)
        PL = place("PL", [P, SC], F32R)
        MDD = place("MDD", [HT, HT], F32R, l_addr + 3584)
        OT = place("OT", [P, NP], F32)
        RD = place("RD", [P, NP], F32)
        SS = place("SS", [P, (PG + 1) * HT + 2 * NT], F32)
        SL = place("SL", [P, (PG + 1) * HT], F32)
        QB = place("QB", [P, CT, NB, 2, NT], F32)
        NBI = place("NBI", [NS, NB, NH, NT], F32)
        SUF = place("SUF", [P, PG, HT], F32, at[0] - 2048)
        OS = place("OS", [P, CT, NS], F32)

        B = [ctx.enter_context(nc.psum_tensor(f"B{i}", [P, 512], F32)) for i in range(4)]
        B4 = ctx.enter_context(nc.psum_tensor("B4", [P, 512], F32))
        B5 = ctx.enter_context(nc.psum_tensor("B5", [P, 512], F32))
        B6 = ctx.enter_context(nc.psum_tensor("B6", [P, 512], F32))
        B7 = ctx.enter_context(nc.psum_tensor("B7", [P, 512], F32))
        B = B + [B4, B5, B6, B7]

        OFF = [0, 512, 1024, 896]
        WID = [NP - P * j for j in range(TT)]

        def sc_bank(j, lo, n):
            o = OFF[j] + lo
            return B[o // 512][:, o % 512:o % 512 + n]

        S = {}

        def sems(*names):
            for n in names:
                S[n] = ctx.enter_context(nc.semaphore(n))

        sems("w_loaded0", "w_loaded1", "w_high", "w_low", "unit_done", "evac_act", "evac_dve",
             "vec_in", "x_in", "small_in", "lfp_in", "sgu_in", "state_in", "pt_in", "wf_in",
             "consts", "zeroed", "vec_turned", "x_turned", "x_copied", "x_squared", "x_summed",
             "sum_step", "rms_sum", "rms_mean", "rms_ln", "rms_scale", "normed", "norm_high", "norm_low",
             "lf_turned", "lf_copied", "lf_suffix_step", "lf_suffixed", "lf_tail", "d_past",
             "wf_high", "wf_low", "f_logits", "f_copied", "f_turned", "f_biased", "f_abs", "f_exp", "f_ln", "f_logf", "F_sums", "F_set",
             "nbi_set", "relu_squared", "ff_high",
             "ws_turned", "ws_masked", "rep_done", "bd_set", "ln_step", "ln_var", "ln_scale", "ln_done", "mixed", "sgu_step", "sgu_out",
             "sgu_high", "sgu_low", "state_turned", "ue_set", "conv_step", "conv_out", "conv_high", "conv_low",
             "tail_set", "tail_turned", "tail_copied",
             "y_turned", "y_copied", "stored", "stored_kn")
        for L in range(2):
            sems(f"nat_turned{L}", f"nat_dve{L}", f"nat_act{L}", *[f"k_in{L}_{i}" for i in range(4)], f"v_in{L}",
                 f"k_turned{L}", f"kt_copied{L}", f"v_used{L}", f"prompt_av{L}",
                 f"dec_out{L}", f"q_block{L}")
        sems("os_high", "os_low", "qk_high", "qk_low", "v_high", "v_low", "o_high", "o_low", "scores", "shifted", "probs", "p_high", "p_low", "dec_shifted", "dec_probs", "dec_av", "av_copied", "av_turned", "prompt_out",
             "biased", "max_step", "max_turned", "max_rows", "max_diag", "max_spread", "dec_biased",
             "dec_max_part", "dec_max_turned", "dec_max_rows", "dec_max_diag", "dec_max_spread", "rden", "dec_rden",
             "sb_abs", "sb_exp", "sb_ln", "sb_ls", "sb_min", "dsb_min", "sb_sp", "sp_high", "sp_low", "cum", "dsb_abs", "dsb_exp", "dsb_ln",
             "dsb_sp", "dsb_masked", "dec_suffix", "dec_cum")

        NORM_G = [0, 2 * KT, KT, 3 * KT, 4 * KT]
        CONV_V = 5 * KT

        def unit_loop(eng, body, g0, n, last_plain=False):
            turns = n // 2 - (1 if last_plain else 0)
            with eng.Fori(0, turns) as it:
                for u in range(2):
                    body(it * 2 + (g0 + u), it * 2 + u, u, True)
            if last_plain:
                for u in range(2):
                    i = n - 2 + u
                    body(g0 + i, i, u, u == 0)

        up_v = [w_up[l].rearrange("(k p) n -> p k n", p=P) for l in range(2)]
        dn_v = [w_down[l].rearrange("(g k p) n -> g p k n", p=P, k=KT) for l in range(2)]
        in_v = [w_in_even[0].rearrange("(k p) n -> p k n", p=P), w_in_odd[0].rearrange("(k p) n -> p k n", p=P)]
        out_v = [w_out_even[0].rearrange("(k p) n -> p k n", p=P), w_out_odd[0].rearrange("(k p) n -> p k n", p=P)]
        FCOL = 3 * DA
        cache_k = [cache_fox_k, cache_sb_k]
        cache_v = [cache_fox_v, cache_sb_v]
        MLP_ORDER = [("up", 0), ("up", 1), ("down", 0), ("up", 2), ("down", 1), ("up", 3), ("down", 2), ("down", 3)]
        G_IN, G_OUT, G_MLP = [G_IN0, G_IN1], [G_OUT0, G_OUT1], [G_MLP0, G_MLP1]
        n_b = [2 * CT, 3 * CT]
        NAT = [[("k", i) for i in range(TT + 1)] + [("v", i) for i in range(TT + 1)] + [("g", i) for i in range(TT + 1)],
               [("k", i) for i in range(TT + 1)] + [("v", i) for i in range(TT + 1)]]

        def nat_src(kind, c, i):
            t = {"k": PA[:, CT + c, :], "v": PA[:, 2 * CT + c, :], "g": PB[:, CT + c, :]}[kind]
            return t[:, i * P:min((i + 1) * P, T)]

        def nat_dst(kind, i):
            t = {"k": KN, "v": VN, "g": GN}[kind]
            return t[:, i, :] if i < TT else t[0:NS, i, :]

        N_STORES = 5 + 4 + 2

        block = ctx.enter_context(nc.Block())

        @block.sync
        def _(sp):
            sp.dma_start(XN[:, 0:TT, :], x_prompt[0].rearrange("(i p) d -> p i d", p=P)).then_inc(S["x_in"], 16)
            sp.dma_start(XN[0:NS, TT, :], x_sample.rearrange("b t d -> (b t) d")).then_inc(S["x_in"], 16)
            sp.dma_start(pages[0:1, :], page_table.rearrange("(o a) b -> o (a b)", o=1)).then_inc(S["pt_in"], 16)
            sp.dma_start(vec_rows[0:2 * KT, :], g_mix.rearrange("l (k p) -> (l k) p", p=P)).then_inc(S["vec_in"], 16)
            sp.dma_start(vec_rows[2 * KT:4 * KT, :], g_mlp.rearrange("l (k p) -> (l k) p", p=P)).then_inc(S["vec_in"], 16)
            sp.dma_start(vec_rows[4 * KT:5 * KT, :], g_final.rearrange("(k p) -> k p", p=P)).then_inc(S["vec_in"], 16)
            sp.dma_start(vec_rows[5 * KT:n_vec, :], conv_w[0].rearrange("w (k p) -> (w k) p", p=P)).then_inc(S["vec_in"], 16)
            sp.dma_start(bf[:, :], b_forget[0:1, :].partition_broadcast(P)).then_inc(S["small_in"], 16)
            def load_weights(view, col0):
                def body(g, i, u, more):
                    sp.wait_ge(S["w_low"], g + 1)
                    sp.dma_start(WR[u][:, :, :], view[:, :, ds(i * P + col0, P)]).then_inc(S[f"w_loaded{u}"], 16)
                return body

            for L in range(2):
                if L == 0:
                    for u in range(2):
                        load_weights(in_v[L], 0)(G_IN[L] + u, u, u, True)
                    sp.dma_start(WF[:, :, :], in_v[0][:, :, FCOL:FCOL + P]).then_inc(S["wf_in"], 16)
                    unit_loop(sp, load_weights(in_v[L], 2 * P), G_IN[L] + 2, 3 * CT - 2)
                else:
                    unit_loop(sp, load_weights(in_v[L], 0), G_IN[L], 3 * CT)
                unit_loop(sp, load_weights(in_v[L], FCOL + (NH if L == 0 else 0)), G_IN[L] + 3 * CT, n_b[L])
                if L == 0:
                    sp.wait_ge(S["lf_suffixed"], 1)
                    sp.wait_ge(S["d_past"], 1)
                    sp.dma_start(WSN[:, :, :], w_spatial[0].rearrange("g t s -> t g s")).then_inc(S["sgu_in"], 16)
                    sp.dma_start(g_row[:, :], sgu_g[0:1, :].partition_broadcast(P)).then_inc(S["sgu_in"], 16)
                    sp.dma_start(b_row[:, :], sgu_b[0:1, :].partition_broadcast(P)).then_inc(S["sgu_in"], 16)
                    for g in range(GB):
                        sp.dma_start(bs_row[HD * (g % 2):HD * (g % 2) + HD, g // 2, :],
                                     b_spatial[0, g:g + 1, :].partition_broadcast(HD)).then_inc(S["sgu_in"], 16)

                def load_k(s, j):
                    v = sp.value_load(pages[0:1, ds(s * PG + j, 1)], min_val=0, max_val=POOL - 1)
                    sp.wait_ge(S[f"k_turned{L}"], s * PG + (j + 1))
                    sp.dma_start(KR[:, j % 4, :], cache_k[L][0][ds(v, 1)].rearrange("o p h d -> (o p) (h d)")
                                 ).then_inc(S[f"k_in{L}_{j % 4}"], 16)

                def load_v(s, first_wait):
                    for j in range(PG):
                        v = sp.value_load(pages[0:1, ds(s * PG + j, 1)], min_val=0, max_val=POOL - 1)
                        if j == 0 and first_wait:
                            sp.wait_ge(S["sgu_out"], 4)
                        if j == 0:
                            sp.wait_ge(S[f"v_used{L}"], s + 1)
                        sp.dma_start(VR[:, j, :], cache_v[L][0][ds(v, 1)].rearrange("o p h d -> (o p) (h d)")
                                     ).then_inc(S[f"v_in{L}"], 16)

                for u in range(2):
                    load_weights(out_v[L], 0)(G_OUT[L] + u, u, u, True)
                for j in range(PG + 4):
                    load_k(j // PG, j % PG)
                load_v(0, L == 0)
                with sp.Fori(1, NB - 1) as s:
                    for j in range(4, PG):
                        load_k(s, j)
                    for j in range(4):
                        load_k(s + 1, j)
                    load_v(s, False)
                for j in range(4, PG):
                    load_k(NB - 1, j)
                load_v(NB - 1, False)
                unit_loop(sp, load_weights(out_v[L], 2 * P), G_OUT[L] + 2, KT - 2)
                g = G_MLP[L]
                for kind, grp in MLP_ORDER:
                    view = up_v[L] if kind == "up" else dn_v[L][grp]
                    unit_loop(sp, load_weights(view, grp * DM if kind == "up" else 0), g, KT)
                    g += KT
            sp.wait_ge(S["stored"], N_STORES * 16)
            sp.wait_ge(S["stored_kn"], 4 * 16)

        @block.gpsimd
        def _(pool):
            g = nc.gpsimd
            for t in (ident, neg_causal, neg_strict, seq_neg_causal, seq_neg_strict, step_rep):
                g.memset(t[:], 0.0)
            for t in (ones, upto, after, before, seq_upto, seq_before, seq_same):
                last = g.memset(t[:], 1.0)
            last.then_inc(S["zeroed"], 1)
            pool.wait_ge(S["zeroed"], 1)
            sel = g.affine_select

            def step(ins, n=[1]):
                n[0] += 1
                ins.then_inc(S["zeroed"], 1)
                pool.wait_ge(S["zeroed"], n[0])

            sel(out=ident[:], in_=ident[:], compare_op=ALU.not_equal, fill=1.0, base=0, pattern=[[-1, P]], channel_multiplier=1)
            sel(out=upto[:], in_=upto[:], compare_op=ALU.is_ge, fill=0.0, base=0, pattern=[[1, P]], channel_multiplier=-1)
            sel(out=before[:], in_=before[:], compare_op=ALU.is_gt, fill=0.0, base=0, pattern=[[1, P]], channel_multiplier=-1)
            sel(out=after[:], in_=after[:], compare_op=ALU.is_gt, fill=0.0, base=0, pattern=[[-1, P]], channel_multiplier=1)
            sel(out=neg_causal[:], in_=neg_causal[:], compare_op=ALU.is_ge, fill=NEG, base=0, pattern=[[1, P]], channel_multiplier=-1)
            sel(out=neg_strict[:], in_=neg_strict[:], compare_op=ALU.is_gt, fill=NEG, base=0, pattern=[[1, P]], channel_multiplier=-1)
            sel(out=step_rep[:], in_=step_rep[:], compare_op=ALU.not_equal, fill=1.0, base=0, pattern=[[0, NB], [-1, NT]], channel_multiplier=1)
            step(sel(out=seq_same[:], in_=seq_same[:], compare_op=ALU.is_ge, fill=0.0, base=0, pattern=[[-NT, NB]], channel_multiplier=1))
            sel(out=seq_same[:], in_=seq_same[:], compare_op=ALU.is_ge, fill=0.0, base=NT - 1, pattern=[[NT, NB]], channel_multiplier=-1)
            for t, cmp, rows, base, fill in ((seq_upto, ALU.is_ge, slice(0, NS), 0, 0.0), (seq_upto, ALU.is_ge, slice(NS, P), 0, 0.0),
                                             (seq_before, ALU.is_gt, slice(0, NS), 0, 0.0),
                                             (seq_neg_causal, ALU.is_ge, slice(0, NS), 0, NEG), (seq_neg_strict, ALU.is_gt, slice(0, NS), 0, NEG)):
                step(sel(out=t[rows], in_=t[rows], compare_op=ALU.is_ge, fill=fill, base=base, pattern=[[-NT, NB], [0, NT]], channel_multiplier=1))
                step(sel(out=t[rows], in_=t[rows], compare_op=cmp, fill=fill, base=base, pattern=[[NT, NB], [1, NT]], channel_multiplier=-1))
            g.drain().then_inc(S["consts"], 1)
            pool.wait_ge(S["pt_in"], 16)
            for q in range(NB * PG):
                v = pool.value_load(pages[0:1, q:q + 1], min_val=0, max_val=POOL - 1)
                pool.dma_start(lf_raw[q:q + 1, :, :], cache_fox_logf[0][ds(v, 1)]).then_inc(S["lfp_in"], 16)

            for L in range(2):
                tk_p, tk_s = ((p_fox_k, s_fox_k), (p_sb_k, s_sb_k))[L]
                tv_p, tv_s = ((p_fox_v, s_fox_v), (p_sb_v, s_sb_v))[L]
                if L == 0:
                    pool.wait_ge(S["f_logf"], 1)
                    pool.dma_start(p_fox_logf[0, 0].rearrange("(i p) h -> p i h", p=P), LF[:, 3, 0:TT, :]).then_inc(S["stored"], 16)
                    pool.dma_start(s_fox_logf[0].rearrange("b t h -> (b t) h"), LF[NS:P, 3, TT, :]).then_inc(S["stored"], 16)
                pool.wait_ge(S[f"nat_dve{L}"], 3)
                pool.wait_ge(S[f"nat_act{L}"], 2)
                pool.dma_start(tk_p[0, 0].rearrange("(i p) h d -> p i (h d)", p=P), KN[:, 0:TT, :]).then_inc(S["stored_kn"], 16)
                pool.dma_start(tk_s[0].rearrange("b t h d -> (b t) (h d)"), KN[0:NS, TT, :]).then_inc(S["stored_kn"], 16)
                pool.wait_ge(S[f"nat_dve{L}"], 5)
                pool.wait_ge(S[f"nat_act{L}"], 5)
                pool.dma_start(tv_p[0, 0].rearrange("(i p) h d -> p i (h d)", p=P), VN[:, 0:TT, :]).then_inc(S["stored"], 16)
                pool.dma_start(tv_s[0].rearrange("b t h d -> (b t) (h d)"), VN[0:NS, TT, :]).then_inc(S["stored"], 16)
                if L == 0:
                    pool.wait_ge(S["ln_done"], 1)
                    pool.dma_start(s_sgu_v[0].rearrange("b t d -> (b t) d"), GN[0:NS, TT, :]).then_inc(S["stored"], 16)
                if L == 1:
                    pool.wait_ge(S["nat_act1"], 5)
                    pool.dma_start(prev_n[0:2 * NB, :], state_conv[0].rearrange("b r d -> (b r) d")).then_inc(S["state_in"], 16)
                    pool.wait_ge(S["tail_copied"], 1)
                    pool.dma_start(p_conv[0, 0], tail_n[0:2, :]).then_inc(S["stored"], 16)
                    pool.dma_start(s_conv[0].rearrange("b r d -> (b r) d"), tail_n[2:2 + 2 * NB, :]).then_inc(S["stored"], 16)
            pool.wait_ge(S["y_copied"], KT)
            pool.dma_start(y_prompt[0].rearrange("(i p) d -> p i d", p=P), XN[:, 0:TT, :]).then_inc(S["stored"], 16)
            pool.dma_start(y_sample.rearrange("b t d -> (b t) d"), XN[0:NS, TT, :]).then_inc(S["stored"], 16)

        @block.scalar
        def _(act):
            A = nc.scalar.activation
            nc.scalar.preload_act_table_set("natural_log_exp_and_others")
            act.sem_inc(S["evac_act"], 2)

            def cut_high(g, u, in_loop=True):
                if not in_loop:
                    act.wait_ge(S[f"w_loaded{u}"], 16 * (g // 2 + 1))
                if not (isinstance(g, int) and g == 0):
                    act.wait_ge(S["unit_done"], g)
                A(WH[u][:], WR[u][:], ACT.Copy).then_inc(S["w_high"], 1)

            def next_high(g, i, u, more, g0):
                if not more:
                    return
                half = (g0 + 1 + u) // 2 + 1
                it = i - u if isinstance(i, int) else None
                act.wait_ge(S[f"w_loaded{1 - u}"], loads_after(g, u))
                act.wait_ge(S["unit_done"], g + 1)
                A(WH[1 - u][:], WR[1 - u][:], ACT.Copy).then_inc(S["w_high"], 1)

            def loads_after(g, u):
                return (g - u) * 8 + (16 if u == 0 else 32)

            def evac_in(tile_of):
                def body(g, i, u, more):
                    next_high(g, i, u, more, 0)
                    act.wait_ge(S["unit_done"], g + 2)
                    A(tile_of(i)[:, 0:TH], B[2 * u][:, 0:TH], ACT.Copy).then_inc(S["evac_act"], 1)
                return body

            def evac_sq(g, i, u, more):
                next_high(g, i, u, more, 0)
                act.wait_ge(S["evac_dve"], g + 3)
                A(TMP[:, u, :], X[:, ds(i, 1), :], ACT.Square).then_inc(S["evac_act"], 1)

            def evac_none(g, i, u, more):
                next_high(g, i, u, more, 0)
                act.sem_inc(S["evac_act"], 1)

            def evac_up(L, grp):
                m0 = L * FG * KT + grp * KT
                def body(g, i, u, more):
                    next_high(g, i, u, more, 0)
                    act.wait_ge(S["unit_done"], g + 2)
                    act.wait_ge(S["evac_dve"], g + 1)
                    for h in range(2):
                        last = A(TMP[:, u, h * TH:(h + 1) * TH], B[2 * u + h][:, 0:TH], ACT.Relu)
                    last.then_inc(S["evac_act"], 1)
                    act.wait_ge(S["relu_squared"], i + (m0 + 1))
                    A(ffH[grp % 2][:, ds(i, 1), :], TMP[:, u, :], ACT.Copy).then_inc(S["ff_high"], 1)
                return body

            def norm(z):
                act.wait_ge(S["rms_mean"], z + 1)
                A(R[:], R[:], ACT.Ln).then_inc(S["rms_ln"], 1)
                act.wait_ge(S["rms_ln"], z + 1)
                A(R[:], R[:], ACT.Exp, scale=-0.5).then_inc(S["rms_scale"], 1)
                for k in range(KT):
                    act.wait_ge(S["normed"], z * KT + k + 1)
                    if z < 4:
                        A(HH[:, k, :], TMP[:, k % 2, :], ACT.Copy).then_inc(S["norm_high"], 1)

            for k in range(KT):
                act.wait_ge(S["x_copied"], k + 1)
                if k >= 2:
                    act.wait_ge(S["x_summed"], k - 1)
                A(TMP[:, k % 2, :], X[:, k, :], ACT.Square).then_inc(S["x_squared"], 1)
            cut_high(0, 0, False)
            norm(0)
            act.wait_ge(S["wf_in"], 16)
            A(WFH[:], WF[:], ACT.Copy).then_inc(S["wf_high"], 1)

            for L in range(2):
                if L == 1:
                    norm(2)
                unit_loop(act, evac_in(lambda i: PA[:, ds(i, 1), :].rearrange("p o t -> p (o t)")), G_IN[L], 3 * CT)
                if L == 0:
                    act.wait_ge(S["lf_turned"], 1)
                    A(lf_pos[:].rearrange("p h b j -> p (h b j)"), B7[:, :], ACT.Copy).then_inc(S["lf_copied"], 1)
                    act.wait_ge(S["f_logits"], 1)
                    A(FT[:, 0:TH], B4[0:NH, 0:TH], ACT.Copy)
                    A(FT[:, TH:T], B5[0:NH, 0:TH], ACT.Copy).then_inc(S["f_copied"], 1)
                unit_loop(act, evac_in(lambda i: PB[:, ds(i, 1), :].rearrange("p o t -> p (o t)")), G_IN[L] + 3 * CT, n_b[L])
                if L == 0:
                    act.wait_ge(S["f_biased"], 1)
                    A(LF[:, 1], LF[:, 0], ACT.Abs).then_inc(S["f_abs"], 1)
                    act.wait_ge(S["f_abs"], 1)
                    A(LF[:, 2], LF[:, 1], ACT.Exp, scale=-1.0).then_inc(S["f_exp"], 1)
                    act.wait_ge(S["f_exp"], 1)
                    A(LF[:, 1], LF[:, 2], ACT.Ln, bias=1.0).then_inc(S["f_ln"], 1)
                for n, (kind, i) in enumerate(NAT[L]):
                    if n % 2 == 1:
                        act.wait_ge(S[f"nat_turned{L}"], n + 1)
                        rows = P if i < TT else NS
                        A(nat_dst(kind, i), B[n % 4][0:rows, :], ACT.Copy).then_inc(S[f"nat_act{L}"], 1)
                if L == 0:
                    act.wait_ge(S["ln_var"], 1)
                    rstd = small[:, 50:50 + TT + 1]
                    A(rstd, rstd, ACT.Ln).then_inc(S["ln_scale"], 1)
                    act.wait_ge(S["ln_scale"], 1)
                    A(rstd, rstd, ACT.Exp, scale=-0.5).then_inc(S["ln_scale"], 1)
                name = "sgu" if L == 0 else "conv"
                for c in range(CT):
                    act.wait_ge(S[f"{name}_out"], c + 1)
                    A(HH[:, CT + c, :], TMP[:, c % 2, :], ACT.Copy).then_inc(S[f"{name}_high"], 1)

                n_nat_act = len(NAT[L]) // 2
                n_nat_dve = len(NAT[L]) - n_nat_act
                act.wait_ge(S[f"nat_dve{L}"], n_nat_dve)
                act.wait_ge(S[f"q_block{L}"], 1)
                def stage_qk(it):
                    A(qH[:], PA[:, ds(it, 1), 0:NP].rearrange("p o t -> p (o t)"), ACT.Copy, scale=QS)
                    A(kH[:], PA[:, ds(it + CT, 1), 0:NP].rearrange("p o t -> p (o t)"), ACT.Copy).then_inc(S["qk_high"], 1)

                def copy_page(s, j):
                    act.wait_ge(S[f"k_turned{L}"], s * PG + (j + 5))
                    A(KTS[:, j % 2, :], B[6 - j % 2][:, :], ACT.Copy).then_inc(S[f"kt_copied{L}"], 1)

                def prompt_exp(s):
                    act.wait_ge(S["shifted"], s + (NB * L + 1))
                    A(S_[:], S_[:], ACT.Exp).then_inc(S["probs"], 1)

                def prompt_high(s):
                    act.wait_ge(S["probs"], s + (NB * L + 1))
                    act.wait_ge(S[f"prompt_av{L}"], s + 1)
                    A(PH[:], S_[:], ACT.Copy).then_inc(S["p_high"], 1)

                def sample_exp(s):
                    act.wait_ge(S["dec_shifted"], s + (NB * L + 1))
                    A(SS[:, 0:ex + HT], SS[:, 0:ex + HT], ACT.Exp).then_inc(S["dec_probs"], 1)

                ex = PG * HT

                def step(s, it, e, more):
                    if e == 0:
                        act.wait_ge(S[f"prompt_av{L}"], s + 1)
                        A(vH[:], VN[:, 0:TT, ds(it * P, P)], ACT.Copy).then_inc(S["v_high"], 1)
                    if e == 1 and more:
                        act.wait_ge(S["scores"], s + (NB * L + 1))
                        stage_qk(it + 1)

                    def copy_pages(*js):
                        for j in js if more else ():
                            copy_page(s + 1, j)

                    def o_high():
                        if e == 1:
                            act.wait_ge(S["prompt_out"], s + (NB * L + 1))
                            A(HH[:, ds(it, 1), 0:NP].rearrange("p o t -> p (o t)"), OT[:], ACT.Copy).then_inc(S["o_high"], 1)

                    if L == 0:
                        copy_pages(0, 1, 2)
                        prompt_exp(s)
                        prompt_high(s)
                        copy_pages(3)
                        sample_exp(s)
                        copy_pages(4, 5)
                        o_high()
                        copy_pages(6, 7)
                    else:
                        act.wait_ge(S["dec_av"], s + ((NB + 1) * L + 1))
                        act.wait_ge(S["av_copied"], s + (NB * L))
                        A(SL[:, 0:ex], B7[:, :], ACT.Abs)
                        A(SL[0:NS, ex:], B5[0:NS, P:P + HT], ACT.Abs).then_inc(S["dsb_abs"], 1)
                        act.wait_ge(S["dsb_abs"], s + 1)
                        A(SL[:, 0:ex], SL[:, 0:ex], ACT.Exp, scale=-1.0)
                        A(SL[0:NS, ex:], SL[0:NS, ex:], ACT.Exp, scale=-1.0).then_inc(S["dsb_exp"], 1)
                        act.wait_ge(S["dsb_exp"], s + 1)
                        A(SL[:, 0:ex], SL[:, 0:ex], ACT.Ln, bias=1.0)
                        A(SL[0:NS, ex:], SL[0:NS, ex:], ACT.Ln, bias=1.0).then_inc(S["dsb_ln"], 1)
                        copy_pages(0, 1)
                        prompt_exp(s)
                        prompt_high(s)
                        copy_pages(2)
                        sample_exp(s)
                        copy_pages(3)
                        if more:
                            sb_abs(s + 1)
                        copy_pages(4)
                        o_high()
                        if more:
                            sb_ln(s + 1)
                        copy_pages(5, 6, 7)
                        if more:
                            sb_high(s + 1)

                def sb_abs(s):
                    act.wait_ge(S["scores"], s + (NB * L + 1))
                    for o in range(0, SC, 512):
                        n = min(512, SC - o)
                        last = A(L_[:, o:o + n], B[o // 512][:, 0:n], ACT.Abs)
                    last.then_inc(S["sb_abs"], 1)
                    act.wait_ge(S["sb_abs"], s + 1)
                    A(L_[:], L_[:], ACT.Exp, scale=-1.0).then_inc(S["sb_exp"], 1)

                def sb_ln(s):
                    act.wait_ge(S["sb_exp"], s + 1)
                    A(L_[:], L_[:], ACT.Ln, bias=1.0).then_inc(S["sb_ln"], 1)

                def sb_high(s):
                    act.wait_ge(S["sb_sp"], s + 1)
                    act.wait_ge(S["prompt_av1"], s + 1)
                    A(PH[:], L_[:], ACT.Copy).then_inc(S["sp_high"], 1)

                stage_qk(0)
                for j in range(PG):
                    copy_page(0, j)
                if L == 1:
                    sb_abs(0)
                    sb_ln(0)
                    sb_high(0)
                with act.Fori(0, CT - 1) as it:
                    for e in range(2):
                        step(it * 2 + e, it, e, True)
                for e in range(2):
                    step(NB - 2 + e, CT - 1, e, e == 0)
                act.wait_ge(S[f"dec_out{L}"], NB + 1)
                A(HH[:, 0:CT, NP:T], OS[:], ACT.Copy).then_inc(S["os_high"], 1)

                unit_loop(act, evac_sq, G_OUT[L], KT)
                norm(1 + 2 * L)
                g = G_MLP[L]
                for n, (kind, grp) in enumerate(MLP_ORDER):
                    last = L == 1 and n == len(MLP_ORDER) - 1
                    body = evac_up(L, grp) if kind == "up" else evac_sq if grp == FG - 1 else evac_none
                    unit_loop(act, body, g, KT, last)
                    g += KT
            norm(4)

        @block.vector
        def _(dve):
            V = nc.vector
            dve.sem_inc(S["evac_dve"], 2)
            dve.sem_inc(S["w_low"], 2)

            def cut_low(g, u):
                dve.wait_ge(S["w_high"], g + 1)
                V.tensor_tensor(WL[u][:], WR[u][:], WH[u][:].bitcast(F32), ALU.subtract).then_inc(S["w_low"], 1)

            def next_low(g, u, more):
                if more:
                    cut_low(g + 1, 1 - u)

            def evac_in(tile_of):
                def body(g, i, u, more):
                    next_low(g, u, more)
                    dve.wait_ge(S["unit_done"], g + 2)
                    V.tensor_copy(tile_of(i)[:, TH:T], B[2 * u + 1][:, 0:TH]).then_inc(S["evac_dve"], 1)
                return body

            def evac_add(squares):
                def body(g, i, u, more):
                    next_low(g, u, more)
                    dve.wait_ge(S["unit_done"], g + 2)
                    for h in range(2):
                        x = X[:, ds(i, 1), h * TH:(h + 1) * TH].rearrange("p o t -> p (o t)")
                        last = V.tensor_tensor(x, B[2 * u + h][:, 0:TH], x, ALU.add)
                    last.then_inc(S["evac_dve"], 1)
                    if squares:
                        dve.wait_ge(S["evac_act"], g + 3)
                        V.tensor_tensor(SQS[:], SQS[:], TMP[:, u, :], ALU.add).then_inc(S["sum_step"], 1)
                return body

            def evac_up(L, grp):
                m0 = L * FG * KT + grp * KT
                def body(g, i, u, more):
                    next_low(g, u, more)
                    dve.wait_ge(S["evac_act"], g + 3)
                    V.tensor_tensor(TMP[:, u, :], TMP[:, u, :], TMP[:, u, :], ALU.mult).then_inc(S["relu_squared"], 1)
                    dve.wait_ge(S["ff_high"], i + (m0 + 1))
                    V.tensor_tensor(ffL[grp % 2][:, ds(i, 1), :], TMP[:, u, :].unsqueeze(1),
                                    ffH[grp % 2][:, ds(i, 1), :].bitcast(F32), ALU.subtract).then_inc(S["evac_dve"], 1)
                return body

            def norm(z):
                dve.wait_ge(S["rms_sum"], z + 1)
                for h in range(2):
                    last = V.tensor_scalar(R[:, h * TH:(h + 1) * TH], B[h][:, 0:TH], 1.0 / DM, EPS, ALU.mult, ALU.add)
                last.then_inc(S["rms_mean"], 1)
                V.memset(SQS[:], 0.0)
                dve.wait_ge(S["rms_scale"], z + 1)

                def scale(k):
                    gain = vec[:, NORM_G[z] + k:NORM_G[z] + k + 1]
                    dst = TMP[:, k % 2, :] if z < 4 else Y[:, k, :]
                    V.scalar_tensor_tensor(dst, X[:, k, :], gain, R[:], ALU.mult, ALU.mult).then_inc(S["normed"], 1)
                scale(0)
                for k in range(KT):
                    if k + 1 < KT:
                        if 1 <= k and z < 4:
                            dve.wait_ge(S["norm_low"], z * KT + k)
                        scale(k + 1)
                    if z < 4:
                        dve.wait_ge(S["norm_high"], z * KT + k + 1)
                        V.tensor_tensor(HL[:, k, :], TMP[:, k % 2, :], HH[:, k, :].bitcast(F32), ALU.subtract).then_inc(S["norm_low"], 1)

            dve.wait_ge(S["consts"], 1)
            V.tensor_copy(ones_r[:], ones[:])
            V.tensor_copy(after_r[:], after[:])
            dve.wait_ge(S["vec_turned"], 1)
            V.tensor_copy(vec[:], B[6][:, 0:n_vec])
            for k in range(KT):
                dve.wait_ge(S["x_turned"], k + 1)
                V.tensor_copy(X[:, k, 0:NP], B[2 * (k % 2)][:, :])
                V.tensor_copy(X[:, k, NP:T], B[2 * (k % 2) + 1][:, 0:NS]).then_inc(S["x_copied"], 1)
                dve.wait_ge(S["x_squared"], k + 1)
                if k == 0:
                    V.tensor_copy(SQS[:], TMP[:, 0, :]).then_inc(S["x_summed"], 1)
                else:
                    dve.wait_ge(S["x_summed"], k)
                    V.tensor_tensor(SQS[:], SQS[:], TMP[:, k % 2, :], ALU.add).then_inc(S["x_summed"], 1)
            cut_low(0, 0)
            norm(0)
            dve.wait_ge(S["wf_high"], 1)
            V.tensor_tensor(WFL[:], WF[:], WFH[:].bitcast(F32), ALU.subtract).then_inc(S["wf_low"], 1)

            for L in range(2):
                if L == 1:
                    norm(2)
                unit_loop(dve, evac_in(lambda i: PA[:, ds(i, 1), :].rearrange("p o t -> p (o t)")), G_IN[L], 3 * CT)
                if L == 0:
                    dve.wait_ge(S["lf_copied"], 1)
                    V.memset(lf_suf[:, :, :, PG - 1:PG], 0.0).then_inc(S["lf_suffix_step"], 1)
                    for j in range(PG - 2, -1, -1):
                        dve.wait_ge(S["lf_suffix_step"], PG - 1 - j)
                        V.tensor_tensor(lf_suf[:, :, :, j], lf_suf[:, :, :, j + 1], lf_pos[:, :, :, j + 1], ALU.add).then_inc(S["lf_suffix_step"], 1)
                    dve.wait_ge(S["lf_suffix_step"], PG)
                    V.memset(small[:, 95:96], 0.0).then_inc(S["lf_suffixed"], 1)
                    dve.wait_ge(S["f_turned"], 1)
                    dve.wait_ge(S["small_in"], 16)
                    V.tensor_tensor(LF[:, 0], B[6][:, 0:(TT + 1) * NH].rearrange("p (i h) -> p i h", h=NH),
                                    bf[:].unsqueeze(1).broadcast_to([P, TT + 1, NH]), ALU.add).then_inc(S["f_biased"], 1)
                    dve.wait_ge(S["lf_tail"], 1)
                    V.tensor_copy(D_past[:].rearrange("p b j h -> p (b j) h"),
                                  B7[:, :].rearrange("p (h n) -> p n h", h=NH)).then_inc(S["d_past"], 1)
                unit_loop(dve, evac_in(lambda i: PB[:, ds(i, 1), :].rearrange("p o t -> p (o t)")), G_IN[L] + 3 * CT, n_b[L])
                if L == 0:
                    dve.wait_ge(S["f_ln"], 1)
                    V.scalar_tensor_tensor(LF[:, 3], LF[:, 0], 0.0, LF[:, 1], ALU.min, ALU.subtract).then_inc(S["f_logf"], 1)
                for n, (kind, i) in enumerate(NAT[L]):
                    if n % 2 == 0:
                        dve.wait_ge(S[f"nat_turned{L}"], n + 1)
                        rows = P if i < TT else NS
                        V.tensor_copy(nat_dst(kind, i), B[n % 4][0:rows, :]).then_inc(S[f"nat_dve{L}"], 1)

                if L == 0:
                    dve.wait_ge(S["F_sums"], 1)
                    V.tensor_scalar(F_neg[:].rearrange("p i h -> p (i h)"), B[5][:, 0:TT * NH], -1.0, None, ALU.mult)
                    V.tensor_scalar(Fn_neg[:], B[5][0:NS, 64:64 + NH], -1.0, None, ALU.mult).then_inc(S["F_set"], 1)
                    dve.wait_ge(S["ws_turned"], 1)
                    for h in range(2):
                        last = V.tensor_tensor(WST[:, 4 * h:4 * h + 4, :], B[6 + h][:, :].rearrange("p (g t) -> p g t", t=P),
                                               upto[:].unsqueeze(1).broadcast_to([P, 4, P]), ALU.mult)
                    last.then_inc(S["ws_masked"], 1)
                    dve.wait_ge(S["rep_done"], 1)
                    rep = B[4][0:NS, 0:GB * NT].rearrange("p (g t) -> p g t", t=NT)
                    for b in range(NB):
                        last = V.tensor_scalar(WBD[:, :, b, :], rep, seq_same[:, b:b + 1], None, ALU.mult)
                    last.then_inc(S["bd_set"], 1)
                    n_ln = 0

                    def ln(ins):
                        nonlocal n_ln
                        n_ln += 1
                        ins.then_inc(S["ln_step"], 1)
                        dve.wait_ge(S["ln_step"], n_ln)

                    ln(V.memset(small[:, 0:96], 1.0))
                    dve.wait_ge(S["nat_act0"], 7)
                    dve.wait_ge(S["sgu_in"], 16 * (3 + GB))
                    for i in range(TT + 1):
                        rows = P if i < TT else NS
                        last = V.bn_stats(small[0:rows, 16 + 6 * i:22 + 6 * i], GN[0:rows, i, :])
                    ln(last)
                    for i in range(TT + 1):
                        rows = P if i < TT else NS
                        last = V.bn_aggr(small[0:rows, 2 * i:2 * i + 2], small[0:rows, 16 + 6 * i:22 + 6 * i])
                    ln(last)
                    var = small[:, 0:2 * TT + 2].rearrange("p (i w) -> p i w", w=2)[:, :, 1]
                    V.tensor_scalar(small[:, 50:50 + TT + 1], var, EPS, None, ALU.add).then_inc(S["ln_var"], 1)
                    dve.wait_ge(S["ln_scale"], 2)
                    for i in range(TT + 1):
                        rows = P if i < TT else NS
                        last = V.tensor_scalar(GN[0:rows, i, :], GN[0:rows, i, :], small[0:rows, 2 * i:2 * i + 1],
                                               small[0:rows, 50 + i:51 + i], ALU.subtract, ALU.mult)
                    ln(last)
                    for i in range(TT + 1):
                        rows = P if i < TT else NS
                        last = V.tensor_tensor(GN[0:rows, i, :], GN[0:rows, i, :], g_row[0:rows, :], ALU.mult)
                    ln(last)
                    for i in range(TT + 1):
                        rows = P if i < TT else NS
                        last = V.tensor_tensor(GN[0:rows, i, :], GN[0:rows, i, :], b_row[0:rows, :], ALU.add)
                    last.then_inc(S["ln_done"], 1)
                    for c in range(CT):
                        dve.wait_ge(S["mixed"], c + 1)
                        t = TMP[:, c % 2, :]
                        V.tensor_tensor(t[:, 0:NP].rearrange("p (i t) -> p i t", t=P), B[c][:, :].rearrange("p (i t) -> p i t", t=P),
                                        bs_row[:, c, :].unsqueeze(1).broadcast_to([P, TT, P]), ALU.add)
                        V.tensor_tensor(t[:, NP:T].rearrange("p (b t) -> p b t", t=NT),
                                        B[5][:, c * NS:(c + 1) * NS].rearrange("p (b t) -> p b t", t=NT),
                                        bs_row[:, c, 0:NT].unsqueeze(1).broadcast_to([P, NB, NT]), ALU.add).then_inc(S["sgu_step"], 1)
                        dve.wait_ge(S["sgu_step"], c + 1)
                        V.tensor_tensor(t, t, PB[:, c, :], ALU.mult).then_inc(S["sgu_out"], 1)
                        dve.wait_ge(S["sgu_high"], c + 1)
                        V.tensor_tensor(HL[:, CT + c, :], t, HH[:, CT + c, :].bitcast(F32), ALU.subtract).then_inc(S["sgu_low"], 1)
                    n_branch = CT
                else:
                    V.memset(UE[:, :, 0:2], 0.0)
                    V.tensor_tensor(UE[:, :, 2:2 + NP], PB[:, CT:2 * CT, 0:NP], PB[:, 2 * CT:3 * CT, 0:NP], ALU.mult)
                    dve.wait_ge(S["state_turned"], 1)
                    for c in range(CT):
                        V.tensor_copy(SE[:, c, :, 0:2], B[4][:, c * 2 * NB:(c + 1) * 2 * NB].rearrange("p (b r) -> p b r", r=2))
                        last = V.tensor_tensor(SE[:, c, :, 2:2 + NT], PB[:, CT + c, NP:T].rearrange("p (b t) -> p b t", t=NT),
                                               PB[:, 2 * CT + c, NP:T].rearrange("p (b t) -> p b t", t=NT), ALU.mult)
                    last.then_inc(S["ue_set"], 1)
                    dve.wait_ge(S["ue_set"], 1)
                    V.tensor_copy(tail[:, :, 0:2], UE[:, :, NP:NP + 2])
                    for c in range(CT):
                        last = V.tensor_copy(tail[:, c, 2:2 + 2 * NB].rearrange("p (b r) -> p b r", r=2), SE[:, c, :, NT:NT + 2])
                    last.then_inc(S["tail_set"], 1)
                    dve.wait_ge(S["tail_turned"], 1)
                    V.tensor_copy(tail_n[:], B[5][0:2 + 2 * NB, :]).then_inc(S["tail_copied"], 1)
                    n_cv = 0
                    for c in range(CT):
                        t = TMP[:, c % 2, :]
                        tp, ts = t[:, 0:NP], t[:, NP:T].rearrange("p (b t) -> p b t", t=NT)
                        for j in range(NCV):
                            w = vec[:, CONV_V + j * CT + c:CONV_V + j * CT + c + 1]
                            up, us = UE[:, c, j:j + NP], SE[:, c, :, j:j + NT]
                            if j == 0:
                                V.tensor_scalar(tp, up, w, None, ALU.mult)
                                V.tensor_scalar(ts, us, w, None, ALU.mult).then_inc(S["conv_step"], 1)
                            else:
                                V.scalar_tensor_tensor(tp, up, w, tp, ALU.mult, ALU.add)
                                V.scalar_tensor_tensor(ts, us, w, ts, ALU.mult, ALU.add).then_inc(S["conv_step"], 1)
                            n_cv += 1
                            dve.wait_ge(S["conv_step"], n_cv)
                        V.tensor_tensor(t, t, PB[:, c, :], ALU.mult).then_inc(S["conv_out"], 1)
                        dve.wait_ge(S["conv_high"], c + 1)
                        V.tensor_tensor(HL[:, CT + c, :], t, HH[:, CT + c, :].bitcast(F32), ALU.subtract).then_inc(S["conv_low"], 1)

                dve.wait_ge(S["stored_kn"], 32 * (L + 1))
                if L == 0:
                    dve.wait_ge(S["stored"], 16 * 5)
                else:
                    dve.wait_ge(S["stored"], 16 * 9)
                V.memset(QB[:], 0.0).then_inc(S["q_block%d" % L], 1)
                V.memset(SL[:], 0.0)
                V.memset(SS[:, 0:(PG + 1) * HT], NEG)
                V.memset(RD[:], 0.0)
                V.memset(SS[:, (PG + 1) * HT:], 0.0)
                dve.wait_ge(S[f"q_block{L}"], 1)
                for e in range(2):
                    r = slice(HD * e, HD * e + HD)
                    last = V.tensor_scalar(QB[r, :, :, e, :], PA[r, 0:CT, NP:T].rearrange("p c (b t) -> p c b t", t=NT), QS, None, ALU.mult)
                last.then_inc(S[f"q_block{L}"], 1)
                if L == 0:
                    for b in range(NB):
                        last = V.tensor_tensor(NBI[:, b, :, :], seq_neg_causal[:, b, :].unsqueeze(1).broadcast_to([NS, NH, NT]),
                                               Fn_neg[:].unsqueeze(2).broadcast_to([NS, NH, NT]), ALU.add)
                    last.then_inc(S["nbi_set"], 1)
                    dve.wait_ge(S["nbi_set"], 1)
                ex = PG * HT
                flat1 = lambda t: t.rearrange("p o t -> p (o t)")

                def stage_qk(it):
                    dve.wait_ge(S["qk_high"], it + (CT * L + 1))
                    V.scalar_tensor_tensor(qL[:], flat1(PA[:, ds(it, 1), 0:NP]), QS, qH[:].bitcast(F32), ALU.mult, ALU.subtract)
                    V.tensor_tensor(kL[:], flat1(PA[:, ds(it + CT, 1), 0:NP]), kH[:].bitcast(F32), ALU.subtract).then_inc(S["qk_low"], 1)

                def fox_bias(s):
                    dve.wait_ge(S["scores"], s + 1)
                    for j in range(TT):
                        f = F_neg[:, j, ds(s, 1)]
                        last = V.scalar_tensor_tensor(S_[:, OFF[j]:OFF[j] + P], sc_bank(j, 0, P), f, neg_causal[:], ALU.add, ALU.add)
                        if WID[j] > P:
                            last = V.tensor_scalar(S_[:, OFF[j] + P:OFF[j] + WID[j]], sc_bank(j, P, WID[j] - P), f, None, ALU.add)
                    last.then_inc(S["biased"], 1)
                    dve.wait_ge(S["biased"], s + 1)
                    V.tensor_tensor(MX[:], S_[:, P:NP], S_[:, OFF[1]:OFF[1] + WID[1]], ALU.max).then_inc(S["max_step"], 1)
                    for j in range(2, TT):
                        dve.wait_ge(S["max_step"], s * (TT - 1) + (j - 1))
                        m = MX[:, (j - 1) * P:]
                        V.tensor_tensor(m, m, S_[:, OFF[j]:OFF[j] + WID[j]], ALU.max).then_inc(S["max_step"], 1)

                def fox_sample_bias(s):
                    dve.wait_ge(S["dec_av"], s + 1)
                    V.memset(SS[NS:P, ex:ex + HT], NEG)
                    V.tensor_tensor(SS[:, 0:ex].rearrange("p (n t) -> p n t", t=NT), B7[:, :].rearrange("p (n t) -> p n t", t=NT),
                                    D_past[:, ds(s, 1), :, :].rearrange("p o j h -> p (o j h)").unsqueeze(2).broadcast_to([P, PG * NH, NT]), ALU.add)
                    V.tensor_tensor(SS[0:NS, ex:ex + HT], B5[0:NS, P:P + HT], NBI[:, ds(s, 1), :, :].rearrange("p o h t -> p (o h t)"),
                                    ALU.add).then_inc(S["dec_biased"], 1)
                    dve.wait_ge(S["dec_biased"], s + 1)
                    V.tensor_reduce(RD[:, 2 * P:2 * P + HT], SS[:, 0:ex + HT].rearrange("p (j n) -> p n j", n=HT), AX.X, ALU.max).then_inc(S["dec_max_part"], 1)

                def fox_shift(s):
                    dve.wait_ge(S["max_turned"], s + 1)
                    V.tensor_reduce(small[:, 0:TT], B[3][:, :].rearrange("p (i k) -> p i k", k=P), AX.X, ALU.max).then_inc(S["max_rows"], 1)
                    dve.wait_ge(S["max_rows"], s + 1)
                    V.tensor_tensor(MD[:], ident[:].unsqueeze(1).broadcast_to([P, TT, P]),
                                    small[:, 0:TT].unsqueeze(2).broadcast_to([P, TT, P]), ALU.mult).then_inc(S["max_diag"], 1)
                    dve.wait_ge(S["dec_max_turned"], s + 1)
                    V.tensor_reduce(small[0:HT, 8:9], B4[0:HT, 0:P], AX.X, ALU.max).then_inc(S["dec_max_rows"], 1)
                    dve.wait_ge(S["dec_max_rows"], s + 1)
                    V.tensor_scalar(MDD[:], ident[0:HT, 0:HT], small[0:HT, 8:9], None, ALU.mult).then_inc(S["dec_max_diag"], 1)
                    dve.wait_ge(S["max_spread"], s + 1)
                    for j in range(TT):
                        sj = S_[:, OFF[j]:OFF[j] + WID[j]]
                        last = V.tensor_tensor(sj, sj, B[3][:, j * P:NP], ALU.subtract)
                    last.then_inc(S["shifted"], 1)
                    dve.wait_ge(S["dec_max_spread"], s + 1)
                    V.tensor_tensor(SS[:, 0:ex + HT].rearrange("p (j n) -> p j n", n=HT), SS[:, 0:ex + HT].rearrange("p (j n) -> p j n", n=HT),
                                    B4[:, P:P + HT].unsqueeze(1).broadcast_to([P, PG + 1, HT]), ALU.subtract).then_inc(S["dec_shifted"], 1)

                def sb_prompt_weights(s):
                    dve.wait_ge(S["sb_ln"], s + 1)
                    for o in range(0, SC, 512):
                        n = min(512, SC - o)
                        last = V.scalar_tensor_tensor(S_[:, o:o + n], B[o // 512][:, 0:n], 0.0, L_[:, o:o + n], ALU.min, ALU.subtract)
                    last.then_inc(S["sb_min"], 1)
                    dve.wait_ge(S["sb_min"], s + 1)
                    for o in range(0, SC, 512):
                        n = min(512, SC - o)
                        last = V.scalar_tensor_tensor(L_[:, o:o + n], B[o // 512][:, 0:n], 0.0, L_[:, o:o + n], ALU.max, ALU.add)
                    last.then_inc(S["sb_ls"], 1)
                    dve.wait_ge(S["sb_ls"], s + 1)
                    d, l = S_[:, OFF[3]:OFF[3] + P], L_[:, OFF[3]:OFF[3] + P]
                    V.tensor_tensor(l, l, before[:], ALU.mult)
                    d2, l2 = (t[:, 0:1024].rearrange("p (j c) -> p j c", c=512)[:, :, 0:P] for t in (S_, L_))
                    V.tensor_tensor(l2, l2, before[:].unsqueeze(1).broadcast_to([P, 2, P]), ALU.mult)
                    e, m = S_[:, OFF[2]:OFF[2] + P], L_[:, OFF[2]:OFF[2] + P]
                    V.tensor_tensor(m, m, before[:], ALU.mult).then_inc(S["sb_sp"], 1)
                    V.tensor_tensor(d, d, neg_strict[:], ALU.add)
                    V.tensor_tensor(e, e, neg_strict[:], ALU.add)
                    V.tensor_tensor(d2, d2, neg_strict[:].unsqueeze(1).broadcast_to([P, 2, P]), ALU.add)
                    dve.wait_ge(S["sp_high"], s + 1)
                    V.tensor_tensor(PL[:], L_[:], PH[:].bitcast(F32), ALU.subtract).then_inc(S["sp_low"], 1)

                def sb_weights(s):
                    dve.wait_ge(S["dsb_ln"], s + 1)
                    V.memset(SS[NS:P, ex:ex + HT], NEG)
                    V.scalar_tensor_tensor(SS[:, 0:ex], B7[:, :], 0.0, SL[:, 0:ex], ALU.min, ALU.subtract)
                    V.scalar_tensor_tensor(SS[0:NS, ex:ex + HT], B5[0:NS, P:P + HT], 0.0, SL[0:NS, ex:], ALU.min, ALU.subtract).then_inc(S["dsb_min"], 1)
                    dve.wait_ge(S["dsb_min"], s + 1)
                    V.scalar_tensor_tensor(SL[:, 0:ex], B7[:, :], 0.0, SL[:, 0:ex], ALU.max, ALU.add)
                    V.scalar_tensor_tensor(SL[0:NS, ex:], B5[0:NS, P:P + HT], 0.0, SL[0:NS, ex:], ALU.max, ALU.add).then_inc(S["dsb_sp"], 1)
                    dve.wait_ge(S["dsb_sp"], s + 1)
                    h3 = lambda t: t[0:NS, ex:ex + HT].rearrange("p (h t) -> p h t", t=NT)
                    V.tensor_tensor(h3(SL), h3(SL), seq_before[:, ds(s, 1), :].broadcast_to([NS, NH, NT]), ALU.mult)
                    V.tensor_tensor(h3(SS), h3(SS), seq_neg_strict[:, ds(s, 1), :].broadcast_to([NS, NH, NT]), ALU.add).then_inc(S["dsb_masked"], 1)
                    dve.wait_ge(S["cum"], s + 1)
                    for o in range(0, SC, 512):
                        n = min(512, SC - o)
                        last = V.tensor_tensor(S_[:, o:o + n], S_[:, o:o + n], B[o // 512][:, 0:n], ALU.subtract)
                    last.then_inc(S["shifted"], 1)
                    dve.wait_ge(S["dsb_masked"], s + 1)
                    V.tensor_copy(SUF[:, PG - 1, :], SL[:, ex:]).then_inc(S["dec_suffix"], 1)
                    for j in range(PG - 2, -1, -1):
                        dve.wait_ge(S["dec_suffix"], s * PG + (PG - 1 - j))
                        V.tensor_tensor(SUF[:, j, :], SUF[:, j + 1, :], SL[:, (j + 1) * HT:(j + 2) * HT], ALU.add).then_inc(S["dec_suffix"], 1)
                    dve.wait_ge(S["dec_cum"], s + 1)
                    V.tensor_tensor(SS[:, 0:ex], SS[:, 0:ex], B[3][:, :], ALU.subtract)
                    V.tensor_tensor(SS[0:NS, ex:ex + HT], SS[0:NS, ex:ex + HT], B4[0:NS, 0:HT], ALU.subtract).then_inc(S["dec_shifted"], 1)

                def step(s, it, e, more):
                    r = slice(HD * e, HD * e + HD)
                    if L == 0:
                        fox_shift(s)
                    else:
                        sb_weights(s)
                    if e == 0:
                        dve.wait_ge(S["v_high"], it + (CT * L + 1))
                        V.tensor_tensor(vL[:], VN[:, 0:TT, ds(it * P, P)], vH[:].bitcast(F32), ALU.subtract).then_inc(S["v_low"], 1)
                    if e == 1 and more:
                        stage_qk(it + 1)
                    dve.wait_ge(S["p_high"], s + (NB * L + 1))
                    V.tensor_tensor(PL[:], S_[:], PH[:].bitcast(F32), ALU.subtract).then_inc(S["p_low"], 1)
                    dve.wait_ge(S[f"prompt_av{L}"], s + 2)
                    if L == 0:
                        V.reciprocal(RD[:], B[3][:, :]).then_inc(S["rden"], 1)
                        dve.wait_ge(S["rden"], s + 1)
                        V.tensor_tensor(OT[r, :], B4[r, :], RD[r, :], ALU.mult).then_inc(S["prompt_out"], 1)
                    else:
                        V.tensor_copy(OT[r, :], B4[r, :]).then_inc(S["prompt_out"], 1)
                    if e == 1:
                        dve.wait_ge(S["o_high"], it + (CT * L + 1))
                        V.tensor_tensor(flat1(HL[:, ds(it, 1), 0:NP]), OT[:], flat1(HH[:, ds(it, 1), 0:NP]).bitcast(F32), ALU.subtract).then_inc(S["o_low"], 1)
                    if L == 0 and more:
                        fox_bias(s + 1)
                    if L == 1 and more:
                        sb_prompt_weights(s + 1)
                    dve.wait_ge(S["dec_av"], s + ((NB + 1) * L + 2))
                    V.tensor_copy(RD[:, P:2 * P], B5[:, 0:P]).then_inc(S["av_copied"], 1)
                    if L == 0:
                        V.reciprocal(RD[:, 0:HT], B5[:, P + HT:P + 2 * HT]).then_inc(S["dec_rden"], 1)
                        if more:
                            fox_sample_bias(s + 1)
                        dve.wait_ge(S["dec_rden"], s + 1)
                    dve.wait_ge(S["av_turned"], s + (NB * L + 1))
                    for f in range(2):
                        rf = slice(HD * f, HD * f + HD)
                        src = B4[rf, 2 * P:3 * P].rearrange("p (c r) -> p c r", c=CT)[:, :, f * NT:(f + 1) * NT]
                        dst = OS[rf, :, ds(s * NT, NT)]
                        if L == 0:
                            last = V.tensor_tensor(dst, src, RD[rf, 0:HT].rearrange("p (c h t) -> p c h t", h=2, t=NT)[:, :, f, :], ALU.mult)
                        else:
                            last = V.tensor_copy(dst, src)
                    last.then_inc(S[f"dec_out{L}"], 1)

                stage_qk(0)
                if L == 0:
                    fox_bias(0)
                    fox_sample_bias(0)
                else:
                    sb_prompt_weights(0)
                with dve.Fori(0, CT - 1) as it:
                    for e in range(2):
                        step(it * 2 + e, it, e, True)
                for e in range(2):
                    step(NB - 2 + e, CT - 1, e, e == 0)
                dve.wait_ge(S["os_high"], L + 1)
                V.tensor_tensor(HL[:, 0:CT, NP:T], OS[:], HH[:, 0:CT, NP:T].bitcast(F32), ALU.subtract).then_inc(S["os_low"], 1)

                unit_loop(dve, evac_add(True), G_OUT[L], KT)
                norm(1 + 2 * L)
                g = G_MLP[L]
                for n, (kind, grp) in enumerate(MLP_ORDER):
                    last = L == 1 and n == len(MLP_ORDER) - 1
                    body = evac_up(L, grp) if kind == "up" else evac_add(grp == FG - 1)
                    unit_loop(dve, body, g, KT, last)
                    g += KT
            norm(4)
            for k in range(KT):
                dve.wait_ge(S["y_turned"], k + 1)
                V.tensor_copy(XN[:, 0:TT, k * P:(k + 1) * P], B[2 * (k % 2)][:, :].rearrange("p (i c) -> p i c", c=P))
                V.tensor_copy(XN[0:NS, TT, k * P:(k + 1) * P], B[2 * (k % 2) + 1][0:NS, 0:P]).then_inc(S["y_copied"], 1)

        @block.tensor
        def _(pe):
            M = nc.tensor.matmul
            TR = nc.tensor.transpose
            pe.sem_inc(S["unit_done"], 1)
            for L in range(2):
                pe.sem_inc(S[f"k_turned{L}"], 4)
                pe.sem_inc(S[f"v_used{L}"], 1)
                pe.sem_inc(S[f"prompt_av{L}"], 1)
                pe.sem_inc(S[f"dec_out{L}"], 1)

            def unit(hi, lo, also=None):
                def body(g, i, u, more):
                    pe.wait_ge(S["w_low"], g + 3)
                    pe.wait_ge(S["evac_act"], g + 1)
                    pe.wait_ge(S["evac_dve"], g + 1)
                    for k in range(KT):
                        for n, (w, x) in enumerate(((WH, hi), (WH, lo), (WL, hi))):
                            for h in range(2):
                                last = M(B[2 * u + h][:, 0:TH], w[u][:, k, :], x[:, k, h * TH:(h + 1) * TH],
                                         start=(k == 0 and n == 0), stop=(k == KT - 1 and n == 2))
                    last.then_inc(S["unit_done"], 1)
                return body

            def rms(z, name, value):
                pe.wait_ge(S[name], value)
                for h in range(2):
                    last = M(B[h][:, 0:TH], ones[:], SQS[:, h * TH:(h + 1) * TH], start=True, stop=True)
                last.then_inc(S["rms_sum"], 1)

            pe.wait_ge(S["consts"], 1)
            pe.wait_ge(S["vec_in"], 64)
            TR(B[6][:, 0:n_vec], vec_rows[:], ident[0:n_vec, 0:n_vec]).then_inc(S["vec_turned"], 1)
            pe.wait_ge(S["x_in"], 32)
            for k in range(KT):
                if k >= 2:
                    pe.wait_ge(S["x_copied"], k - 1)
                for i in range(TT):
                    TR(B[2 * (k % 2)][:, i * P:(i + 1) * P], XN[:, i, k * P:(k + 1) * P], ident[:])
                TR(B[2 * (k % 2) + 1][:, 0:NS], XN[0:NS, TT, k * P:(k + 1) * P], ident[0:NS, 0:NS]).then_inc(S["x_turned"], 1)
            rms(0, "x_summed", KT)
            for L in range(2):
                if L == 1:
                    rms(2, "sum_step", 2 * KT)
                pe.wait_ge(S["norm_low"], (2 * L + 1) * KT)
                unit_loop(pe, unit(HH, HL), G_IN[L], 3 * CT)
                if L == 0:
                    pe.wait_ge(S["lfp_in"], 16 * NB * PG)
                    for h in range(NH):
                        last = TR(B[7][:, h * NB * PG:(h + 1) * NB * PG], lf_raw[:, :, h], ident[0:NB * PG, 0:NB * PG])
                    last.then_inc(S["lf_turned"], 1)
                    pe.wait_ge(S["wf_low"], 1)
                    for k in range(KT):
                        for n, (w, x) in enumerate(((WFH, HH), (WFH, HL), (WFL, HH))):
                            for h in range(2):
                                last = M(B[4 + h][:, 0:TH], w[:, k, :], x[:, k, h * TH:(h + 1) * TH],
                                         start=(k == 0 and n == 0), stop=(k == KT - 1 and n == 2))
                    last.then_inc(S["f_logits"], 1)
                    pe.wait_ge(S["lf_suffixed"], 1)
                    flat = lambda t: t[:].rearrange("p h b j -> p (h b j)")
                    M(B[7][:, :], after[:], flat(lf_pos), start=True, stop=False)
                    M(B[7][:, :], ones[:], flat(lf_suf), start=False, stop=True).then_inc(S["lf_tail"], 1)
                    pe.wait_ge(S["f_copied"], 1)
                    for i in range(TT + 1):
                        c0 = i * P if i < TT else T - P
                        last = TR(B[6][:, i * NH:(i + 1) * NH], FT[:, c0:c0 + P], ident[0:NH, 0:NH])
                    last.then_inc(S["f_turned"], 1)
                unit_loop(pe, unit(HH, HL), G_IN[L] + 3 * CT, n_b[L])
                g_last = G_IN[L] + 3 * CT + n_b[L] - 1
                pe.wait_ge(S["evac_act"], g_last + 3)
                pe.wait_ge(S["evac_dve"], g_last + 3)
                for n, (kind, i) in enumerate(NAT[L]):
                    if n >= 4:
                        pe.wait_ge(S[f"nat_dve{L}" if n % 2 == 0 else f"nat_act{L}"], (n - 4) // 2 + 1)
                    for c in range(CT):
                        src = nat_src(kind, c, i)
                        rows = P if i < TT else NS
                        last = TR(B[n % 4][0:rows, c * P:(c + 1) * P], src, ident[:])
                    last.then_inc(S[f"nat_turned{L}"], 1)

                if L == 0:
                    pe.wait_ge(S["f_logf"], 1)
                    for i in range(TT):
                        for ii in range(i + 1):
                            M(B[5][:, i * NH:(i + 1) * NH], (upto if ii == i else ones)[:], LF[:, 3, ii, :], start=(ii == 0), stop=(ii == i))
                    M(B[5][0:NS, 64:64 + NH], seq_upto[NS:P].rearrange("p b t -> p (b t)"), LF[NS:P, 3, TT, :],
                      start=True, stop=True).then_inc(S["F_sums"], 1)
                    pe.wait_ge(S["sgu_in"], 16 * (3 + GB))
                    for g in range(GB):
                        last = TR(B[6 + g // 4][:, (g % 4) * P:(g % 4 + 1) * P], WSN[:, g, :], ident[:])
                    last.then_inc(S["ws_turned"], 1)
                    pe.wait_ge(S["ws_masked"], 1)
                    M(B[4][0:NS, 0:GB * NT], step_rep[:].rearrange("p b t -> p (b t)"), WST[0:NT, :, 0:NT], start=True, stop=True).then_inc(S["rep_done"], 1)
                    pe.wait_ge(S["bd_set"], 1)
                    pe.wait_ge(S["ln_done"], 1)
                    for c in range(CT):
                        for e in range(2):
                            g = 2 * c + e
                            r = slice(HD * e, HD * e + HD)
                            for i in range(TT):
                                M(B[c][r, i * P:(i + 1) * P], GN[:, i, g * HD:(g + 1) * HD], WST[:, g, :], start=True, stop=True)
                            last = M(B[5][r, c * NS:(c + 1) * NS], GN[0:NS, TT, g * HD:(g + 1) * HD],
                                     WBD[:, g].rearrange("p b t -> p (b t)"), start=True, stop=True)
                    last.then_inc(S["mixed"], CT)
                else:
                    pe.wait_ge(S["state_in"], 16)
                    for c in range(CT):
                        last = TR(B[4][:, c * 2 * NB:(c + 1) * 2 * NB], prev_n[0:2 * NB, c * P:(c + 1) * P], ident[0:2 * NB, 0:2 * NB])
                    last.then_inc(S["state_turned"], 1)
                    pe.wait_ge(S["tail_set"], 1)
                    for c in range(CT):
                        last = TR(B[5][0:2 + 2 * NB, c * P:(c + 1) * P], tail[:, c, :], ident[:])
                    last.then_inc(S["tail_turned"], 1)

                pe.wait_ge(S[f"q_block{L}"], 2)
                if L == 0:
                    pe.wait_ge(S["sgu_low"], CT)
                else:
                    pe.wait_ge(S["conv_low"], CT)
                ex = PG * HT
                new_s, den_s = B5[0:NS, P:P + HT], B5[:, P + HT:P + 2 * HT]
                QW = 2 * NT
                QR = 32

                def page_scores(s, j):
                    pe.wait_ge(S[f"kt_copied{L}"], s * PG + (j + 1))
                    for c in range(CT):
                        M(B7[:, j * HT + c * 2 * NT:j * HT + (c + 1) * 2 * NT], KTS[:, j % 2, c * P:(c + 1) * P],
                          QB[:, c, ds(s, 1), :, :].rearrange("p o h t -> p (o h t)"), start=True, stop=True)

                def page(s, j, first):
                    pe.wait_ge(S[f"k_in{L}_{j % 4}"], s * (16 * PG // 4) + 16 * (j // 4 + 1))
                    if j >= 2:
                        pe.wait_ge(S[f"kt_copied{L}"], s * PG + (j - 1))
                    if j == 1 and not first:
                        pe.wait_ge(S["dec_biased" if L == 0 else "dsb_sp"], s)
                    for c in range(CT):
                        last = TR(B[6 - j % 2][:, c * P:(c + 1) * P], KR[:, j % 4, c * P:(c + 1) * P], ident[:])
                    last.then_inc(S[f"k_turned{L}"], 1)
                    if j >= 1:
                        page_scores(s, j - 1)
                    if j == PG - 1:
                        page_scores(s, j)

                def prompt_scores(s, e, it):
                    r = slice(HD * e, HD * e + HD)
                    if e == 0:
                        pe.wait_ge(S["qk_low"], it + (CT * L + 1))
                    for j in range(TT):
                        for n, (a, b) in enumerate(((kH, qH), (kH, qL), (kL, qH))):
                            last = M(sc_bank(j, 0, WID[j]), a[r, j * P:(j + 1) * P], b[r, j * P:NP], start=(n == 0), stop=(n == 2))
                    last.then_inc(S["scores"], 1)

                def new_scores(s):
                    for c in range(CT):
                        last = M(new_s[:, c * 2 * NT:(c + 1) * 2 * NT], PA[:, CT + c, NP:T],
                                 QB[:, c, ds(s, 1), :, :].rearrange("p o h t -> p (o h t)"), start=True, stop=True)
                    return last

                def ahead(s):
                    if L == 0:
                        pe.wait_ge(S["max_step"], s * (TT - 1) + (TT - 1))
                        for i in range(TT):
                            src = S_[:, 0:P] if i == 0 else MX[:, (i - 1) * P:i * P]
                            last = TR(B[3][:, i * P:(i + 1) * P], src, ident[:])
                        last.then_inc(S["max_turned"], 1)
                    else:
                        pe.wait_ge(S["sp_low"], s + 1)
                        for j in range(TT):
                            for jj in range(j, TT):
                                d = (jj - j) * P
                                for n, x in enumerate((PH, PL)):
                                    last = M(sc_bank(j, d, WID[jj]), (after_r if jj == j else ones_r)[:], x[:, OFF[jj]:OFF[jj] + WID[jj]],
                                             start=(jj == j and n == 0), stop=(jj == TT - 1 and n == 1))
                        last.then_inc(S["cum"], 1)

                def step(s, it, e, more):
                    def pages_after(*js):
                        for j in js if more else ():
                            page(s + 1, j, False)

                    if L == 0:
                        pages_after(0)
                        pe.wait_ge(S["max_diag"], s + 1)
                        M(B[3][:, :], ones_r[:], MD[:].rearrange("p i q -> p (i q)"), start=True, stop=True).then_inc(S["max_spread"], 1)
                        pages_after(1)
                        pe.wait_ge(S["dec_max_part"], s + 1)
                        pe.wait_ge(S["dec_out0"], s + 1)
                        TR(B4[:, 0:P], RD[:, 2 * P:3 * P], ident[:]).then_inc(S["dec_max_turned"], 1)
                        pages_after(2)
                        pe.wait_ge(S["dec_max_diag"], s + 1)
                        M(B4[:, P:P + HT], ones_r[0:HT, :], MDD[:], start=True, stop=True).then_inc(S["dec_max_spread"], 1)
                        pages_after(3)
                    else:
                        pages_after(0, 1)
                        pe.wait_ge(S["dec_suffix"], s * PG + PG)
                        pe.wait_ge(S["dec_out1"], s + 1)
                        M(B[3][:, :], after[:], SL[:, 0:ex], start=True, stop=False)
                        M(B[3][:, :], ones[:], SUF[:].rearrange("p j n -> p (j n)"), start=False, stop=True)
                        M(B4[0:NS, 0:HT], after[0:NS, 0:NS], SL[0:NS, ex:ex + HT], start=True, stop=True).then_inc(S["dec_cum"], 1)
                        pages_after(2, 3)
                    pe.wait_ge(S["v_low"], it + (CT * L + 1))
                    pe.wait_ge(S["p_low"], s + (NB * L + 1))
                    if L == 0:
                        for j in range(TT):
                            for n, x in enumerate((PH, PL)):
                                M(B[3][:, j * P:NP], ones_r[:], x[:, OFF[j]:OFF[j] + WID[j]], start=(j == 0 and n == 0), stop=(j == TT - 1 and n == 1))
                    for j in range(TT):
                        for n, (a, b) in enumerate(((vH, PH), (vH, PL), (vL, PH))):
                            last = M(B4[:, j * P:NP], a[:, j, :], b[:, OFF[j]:OFF[j] + WID[j]], start=(j == 0 and n == 0), stop=(j == TT - 1 and n == 2))
                    last.then_inc(S[f"prompt_av{L}"], 1)
                    if more:
                        prompt_scores(s + 1, 1 - e, it + e)
                        pages_after(4, 5, 6, 7)
                        new_scores(s + 1)
                    pe.wait_ge(S["dec_probs"], s + (NB * L + 1))
                    if L == 0:
                        for j in range(PG + 1):
                            M(den_s, ones[:], SS[:, j * HT:(j + 1) * HT], start=(j == 0), stop=(j == PG))
                    pe.wait_ge(S[f"v_in{L}"], s * (16 * PG) + 16 * PG)
                    for c in range(CT):
                        o = c * QW
                        rows = slice(c * QR, (c + 1) * QR)
                        for j in range(PG):
                            last = M(B5[rows, 0:P], SS[:, j * HT + o:j * HT + o + QR], VR[:, j, c * P:(c + 1) * P], start=(j == 0), stop=False)
                        if c == CT - 1:
                            last.then_inc(S[f"v_used{L}"], 1)
                        last = M(B5[rows, 0:P], SS[0:NS, ex + o:ex + o + QR], VN[0:NS, TT, c * P:(c + 1) * P], start=False, stop=True)
                    last.then_inc(S["dec_av"], 1)
                    if more:
                        ahead(s + 1)
                    pe.wait_ge(S["av_copied"], s + (NB * L + 1))
                    TR(B4[:, 2 * P:3 * P], RD[:, P:2 * P], ident[:]).then_inc(S["av_turned"], 1)

                for j in range(PG):
                    page(0, j, True)
                prompt_scores(0, 0, 0)
                new_scores(0).then_inc(S["dec_av"], 1)
                ahead(0)
                with pe.Fori(0, CT - 1) as it:
                    for e in range(2):
                        step(it * 2 + e, it, e, True)
                for e in range(2):
                    step(NB - 2 + e, CT - 1, e, e == 0)
                pe.wait_ge(S["o_low"], CT * (L + 1))
                pe.wait_ge(S["os_low"], L + 1)
                unit_loop(pe, unit(HH, HL), G_OUT[L], KT)
                rms(1 + 2 * L, "sum_step", (2 * L + 1) * KT)
                pe.wait_ge(S["norm_low"], (2 * L + 2) * KT)
                g = G_MLP[L]
                up_end = {}
                for n, (kind, grp) in enumerate(MLP_ORDER):
                    if kind == "up":
                        unit_loop(pe, unit(HH, HL), g, KT)
                        up_end[grp] = g + KT - 1
                    else:
                        pe.wait_ge(S["evac_dve"], up_end[grp] + 3)
                        unit_loop(pe, unit(ffH[grp % 2], ffL[grp % 2]), g, KT)
                    g += KT
            rms(4, "sum_step", 4 * KT)
            for k in range(KT):
                pe.wait_ge(S["normed"], 4 * KT + k + 1)
                if k >= 2:
                    pe.wait_ge(S["y_copied"], k - 1)
                for i in range(TT):
                    TR(B[2 * (k % 2)][:, i * P:(i + 1) * P], Y[:, k, i * P:(i + 1) * P], ident[:])
                TR(B[2 * (k % 2) + 1][0:NS, 0:P], Y[:, k, NP:T], ident[:]).then_inc(S["y_turned"], 1)


_INS = ["x_prompt", "x_sample", "cache_fox_k", "cache_fox_v", "cache_fox_logf", "cache_sb_k", "cache_sb_v", "state_conv",
        "page_table", "g_mix", "g_mlp", "g_final", "w_up", "w_down", "w_in_even", "b_forget", "sgu_g", "sgu_b",
        "w_spatial", "b_spatial", "w_out_even", "w_in_odd", "conv_w", "w_out_odd"]
_OUTS = [(1, 512, 1024), (8, 8, 1024), (1, 1, 512, 8, 64), (1, 1, 512, 8, 64), (1, 1, 512, 8), (1, 1, 512, 8, 64),
         (1, 1, 512, 8, 64), (1, 1, 2, 512), (1, 8, 8, 8, 64), (1, 8, 8, 8, 64), (1, 8, 8, 8), (1, 8, 8, 8, 64),
         (1, 8, 8, 8, 64), (1, 8, 2, 512), (1, 8, 8, 512)]


def kernel(**inputs):
    import numpy as _np
    import concourse.bacc as _bacc
    from concourse import mybir as _mybir
    from concourse.bass_utils import run_bass_kernel_spmd as _run

    nc = _bacc.Bacc("TRN2", target_bir_lowering=False, num_devices=1)
    arrays, args = {}, []
    for name in _INS:
        a = _np.ascontiguousarray(inputs[name])
        arrays[f"in_{name}_dram"] = a
        args.append(nc.dram_tensor(f"in_{name}_dram", a.shape, _mybir.dt.from_np(a.dtype), kind="ExternalInput").ap())
    for i, shape in enumerate(_OUTS):
        args.append(nc.dram_tensor(f"out_{i}_dram", shape, _mybir.dt.float32, kind="ExternalOutput").ap())
    trunk(nc, *args)
    r = _run(nc, [arrays], core_ids=[0])
    return tuple(r.results[0][f"out_{i}_dram"] for i in range(len(_OUTS)))
```

```python
import concourse.bass as bass
from concourse import mybir
from contextlib import ExitStack



def trunk(nc, x_prompt, x_sample, cache_fox_k, cache_fox_v, cache_fox_logf, cache_sb_k, cache_sb_v, state_conv,
          page_table, g_mix, g_mlp, g_final, w_up, w_down, w_in_even, b_forget, sgu_g, sgu_b, w_spatial,
          b_spatial, w_out_even, w_in_odd, conv_w, w_out_odd,
          y_prompt, y_sample, p_fox_k, p_fox_v, p_fox_logf, p_sb_k, p_sb_v, p_conv,
          s_fox_k, s_fox_v, s_fox_logf, s_sb_k, s_sb_v, s_conv, s_sgu_v):
    F32, F32R, I32 = mybir.dt.float32, mybir.dt.float32r, mybir.dt.int32
    ALU, ACT, AX = mybir.AluOpType, mybir.ActivationFunctionType, mybir.AxisListType
    ds = bass.ds

    P = 128
    NP = x_prompt.shape[1]
    NB, NT = x_sample.shape[0], x_sample.shape[1]
    NS = NB * NT
    T = NP + NS
    TH = T // 2
    DM = x_prompt.shape[2]
    KT = DM // P
    TT = NP // P
    NH, HD = cache_fox_k.shape[3], cache_fox_k.shape[4]
    DA = NH * HD
    CT = DA // P
    POOL = cache_fox_k.shape[1]
    PG = page_table.shape[1]
    FG = w_up.shape[2] // DM
    GB = w_spatial.shape[1]
    QS = float(HD) ** -0.5
    EPS = 1e-6
    NEG = -1e30
    HT = NH * NT
    NCV = conv_w.shape[1]

    G_IN0, G_OUT0 = 0, 5 * CT
    G_MLP0 = G_OUT0 + KT
    G_IN1 = G_MLP0 + 2 * FG * KT
    G_OUT1 = G_IN1 + 6 * CT
    G_MLP1 = G_OUT1 + KT
    G_END = G_MLP1 + 2 * FG * KT

    ctx = ExitStack()
    with ctx:
        at = [16512]

        def place(name, shape, dt, offset=None):
            n = 4
            for d in shape[1:]:
                n *= d
            if offset is None:
                offset = at[0]
                at[0] += (n + 31) // 32 * 32
            return nc.alloc_sbuf_tensor_at(name, shape, dt, offset=offset)

        X = place("X", [P, KT, T], F32)
        h_addr = at[0]
        HH = place("HH", [P, KT, T], F32R)
        HL = place("HL", [P, KT, T], F32R)
        Y = place("Y", [P, KT, T], F32, h_addr)
        WR = [place(f"WR{i}", [P, KT, P], F32) for i in range(2)]
        WH = [place(f"WH{i}", [P, KT, P], F32R) for i in range(2)]
        WL = [place(f"WL{i}", [P, KT, P], F32R) for i in range(2)]
        R = place("R", [P, T], F32)
        SQS = place("SQS", [P, T], F32)
        TMP = place("TMP", [P, 2, T], F32)
        ident = place("ident", [P, P], F32)
        ones = place("ones", [P, P], F32)
        ones_r = place("ones_r", [P, P], F32R)
        upto = place("upto", [P, P], F32)
        after = place("after", [P, P], F32)
        after_r = place("after_r", [P, P], F32R)
        before = place("before", [P, P], F32)
        neg_causal = place("neg_causal", [P, P], F32)
        neg_strict = place("neg_strict", [P, P], F32)
        seq_upto = place("seq_upto", [P, NB, NT], F32)
        seq_before = place("seq_before", [NS, NB, NT], F32)
        seq_neg_causal = place("seq_neg_causal", [NS, NB, NT], F32)
        seq_neg_strict = place("seq_neg_strict", [NS, NB, NT], F32)
        seq_same = place("seq_same", [NS, NB], F32)
        step_rep = place("step_rep", [NT, NB, NT], F32)
        n_vec = 5 * KT + 3 * CT
        vec = place("vec", [P, n_vec], F32)
        pages = place("pages", [1, NB * PG], I32)
        bf = place("bf", [P, NH], F32)
        LF = place("LF", [P, 4, TT + 1, NH], F32)
        F_neg = place("F_neg", [P, TT, NH], F32)
        Fn_neg = place("Fn_neg", [NS, NH], F32)
        D_past = place("D_past", [P, NB, PG, NH], F32)
        small = place("small", [P, 96], F32)
        arena = at[0]
        ffH = [place(f"ffH{i}", [P, KT, T], F32R, arena + i * 2 * KT * T * 4) for i in range(2)]
        ffL = [place(f"ffL{i}", [P, KT, T], F32R, arena + (i * 2 + 1) * KT * T * 4) for i in range(2)]
        at[0] = arena
        XN = place("XN", [P, TT + 1, DM], F32, arena)
        PA = place("PA", [P, 3 * CT, T], F32)
        VN = place("VN", [P, TT + 1, DA], F32)
        KR = place("KR", [P, 4, DA], F32)
        vr_addr = at[0]
        VR = place("VR", [P, PG, DA], F32)
        vec_rows = place("vec_rows", [n_vec, P], F32, vr_addr + 8192)
        lf_raw = place("lf_raw", [NB * PG, P, NH], F32, vr_addr)
        lf_pos = place("lf_pos", [P, NH, NB, PG], F32, vr_addr + 4096)
        lf_suf = place("lf_suf", [P, NH, NB, PG], F32, vr_addr + 6144)
        WSN = place("WSN", [P, GB, P], F32, vr_addr)
        WST = place("WST", [P, GB, P], F32, vr_addr + 4096)
        g_row = place("g_row", [P, DA], F32, vr_addr + 8192)
        b_row = place("b_row", [P, DA], F32, vr_addr + 10240)
        bs_row = place("bs_row", [P, CT, P], F32, vr_addr + 12288)
        WBD = place("WBD", [NS, GB, NB, NT], F32, vr_addr + 14336)
        scratch = at[0]
        PB = place("PB", [P, 3 * CT, T], F32)
        KN = place("KN", [P, TT + 1, DA], F32)
        after_kn = at[0]
        GN = place("GN", [P, TT + 1, DA], F32)
        wf_addr = after_kn - (TT + 1) * DA * 4
        WF = place("WF", [P, KT, P], F32, wf_addr)
        WFH = place("WFH", [P, KT, P], F32R, wf_addr + KT * P * 4)
        WFL = place("WFL", [P, KT, P], F32R, wf_addr + 2 * KT * P * 4)
        FT = place("FT", [NH, T], F32, wf_addr + 3 * KT * P * 4)
        at[0] = after_kn
        UE = place("UE", [P, CT, 2 + NP], F32)
        SE = place("SE", [P, CT, NB, 2 + NT], F32)
        tail = place("tail", [P, CT, 2 + 2 * NB], F32)
        tail_n = place("tail_n", [2 + 2 * NB, DA], F32)
        prev_n = tail_n
        at[0] = scratch
        KTS = place("KTS", [P, 2, 4 * P], F32)
        qH = place("qH", [P, NP], F32R)
        qL = place("qL", [P, NP], F32R)
        kH = place("kH", [P, NP], F32R)
        kL = place("kL", [P, NP], F32R)
        vH = place("vH", [P, TT, P], F32R)
        vL = place("vL", [P, TT, P], F32R)
        SC = 5 * 2 * P
        S_ = place("S_", [P, SC], F32)
        l_addr = at[0]
        L_ = place("L_", [P, SC], F32)
        MD = place("MD", [P, TT, P], F32R, l_addr)
        MX = place("MX", [P, NP - P], F32, l_addr + 2048)
        PH = place("PH", [P, SC], F32R)
        PL = place("PL", [P, SC], F32R)
        MDD = place("MDD", [HT, HT], F32R, l_addr + 3584)
        OT = place("OT", [P, NP], F32)
        RD = place("RD", [P, NP], F32)
        SS = place("SS", [P, (PG + 1) * HT + 2 * NT], F32)
        SL = place("SL", [P, (PG + 1) * HT], F32)
        QB = place("QB", [P, CT, NB, 2, NT], F32)
        NBI = place("NBI", [NS, NB, NH, NT], F32)
        SUF = place("SUF", [P, PG, HT], F32, at[0] - 2048)
        OS = place("OS", [P, CT, NS], F32)

        B = [ctx.enter_context(nc.psum_tensor(f"B{i}", [P, 512], F32)) for i in range(4)]
        B4 = ctx.enter_context(nc.psum_tensor("B4", [P, 512], F32))
        B5 = ctx.enter_context(nc.psum_tensor("B5", [P, 512], F32))
        B6 = ctx.enter_context(nc.psum_tensor("B6", [P, 512], F32))
        B7 = ctx.enter_context(nc.psum_tensor("B7", [P, 512], F32))
        B = B + [B4, B5, B6, B7]

        OFF = [0, 512, 1024, 896]
        WID = [NP - P * j for j in range(TT)]

        def sc_bank(j, lo, n):
            o = OFF[j] + lo
            return B[o // 512][:, o % 512:o % 512 + n]

        S = {}

        def sems(*names):
            for n in names:
                S[n] = ctx.enter_context(nc.semaphore(n))

        sems("w_loaded0", "w_loaded1", "w_high", "w_low", "unit_done", "evac_act", "evac_dve",
             "vec_in", "x_in", "small_in", "lfp_in", "sgu_in", "state_in", "pt_in", "wf_in",
             "consts", "zeroed", "vec_turned", "x_turned", "x_copied", "x_squared", "x_summed",
             "sum_step", "rms_sum", "rms_mean", "rms_ln", "rms_scale", "normed", "norm_high", "norm_low",
             "lf_turned", "lf_copied", "lf_suffix_step", "lf_suffixed", "lf_tail", "d_past",
             "wf_high", "wf_low", "f_logits", "f_copied", "f_turned", "f_biased", "f_abs", "f_exp", "f_ln", "f_logf", "F_sums", 
             "nbi_set", "relu_squared", "ff_high",
             "ws_turned", "ws_masked", "rep_done", "bd_set", "ln_step", "ln_var", "ln_scale", "ln_done", "mixed", "sgu_step", "sgu_out",
             "sgu_high", "sgu_low", "state_turned", "ue_set", "conv_step", "conv_out", "conv_high", "conv_low",
             "tail_set", "tail_turned", "tail_copied",
             "y_turned", "y_copied", "stored", "stored_kn")
        for L in range(2):
            sems(f"nat_turned{L}", f"nat_dve{L}", f"nat_act{L}", *[f"k_in{L}_{i}" for i in range(4)], f"v_in{L}",
                 f"k_turned{L}", f"kt_copied{L}", f"v_used{L}", f"prompt_av{L}",
                 f"dec_out{L}", f"q_block{L}")
        sems("os_high", "os_low", "qk_high", "qk_low", "v_high", "v_low", "o_high", "o_low", "scores", "shifted", "probs", "p_high", "p_low", "dec_shifted", "dec_probs", "dec_av", "av_copied", "den_summed", "stored_v", "av_turned", "prompt_out",
             "biased", "max_step", "max_turned", "max_rows", "max_diag", "max_spread", "dec_biased",
             "dec_max_part", "dec_max_turned", "dec_max_rows", "dec_max_diag", "dec_max_spread", "rden", "dec_rden",
             "sb_abs", "sb_exp", "sb_ln", "sb_ls", "sb_min", "dsb_min", "sb_sp", "sp_high", "sp_low", "cum", "dsb_abs", "dsb_exp", "dsb_ln",
             "dsb_sp", "dsb_masked", "dec_suffix", "dec_cum")

        NORM_G = [0, 2 * KT, KT, 3 * KT, 4 * KT]
        CONV_V = 5 * KT

        def unit_loop(eng, body, g0, n, last_plain=False, first_plain=False, i0=0):
            first = 2 if first_plain else 0
            for u in range(first):
                body(g0 + u, i0 + u, u, "second" if u == 0 else None)
            turns = (n - first) // 2 - (1 if last_plain else 0)
            with eng.Fori(0, turns) as it:
                for u in range(2):
                    body(it * 2 + (g0 + first + u), it * 2 + (i0 + first + u), u, "next")
            if last_plain:
                for u in range(2):
                    i = n - 2 + u
                    body(g0 + i, i0 + i, u, "next" if u == 0 else None)

        up_v = [w_up[l].rearrange("(k p) n -> p k n", p=P) for l in range(2)]
        dn_v = [w_down[l].rearrange("(g k p) n -> g p k n", p=P, k=KT) for l in range(2)]
        in_v = [w_in_even[0].rearrange("(k p) n -> p k n", p=P), w_in_odd[0].rearrange("(k p) n -> p k n", p=P)]
        out_v = [w_out_even[0].rearrange("(k p) n -> p k n", p=P), w_out_odd[0].rearrange("(k p) n -> p k n", p=P)]
        FCOL = 3 * DA
        cache_k = [cache_fox_k, cache_sb_k]
        cache_v = [cache_fox_v, cache_sb_v]
        MLP_ORDER = [("up", 0), ("up", 1), ("down", 0), ("up", 2), ("down", 1), ("up", 3), ("down", 2), ("down", 3)]
        G_IN, G_OUT, G_MLP = [G_IN0, G_IN1], [G_OUT0, G_OUT1], [G_MLP0, G_MLP1]
        n_b = [2 * CT, 3 * CT]
        G_QKV = [G_IN[L] + n_b[L] for L in range(2)]
        NG = TT + 1
        NAT = [[("g", i) for i in range(TT + 1)] + [("k", i) for i in range(TT + 1)] + [("v", i) for i in range(TT + 1)],
               [("k", i) for i in range(TT + 1)] + [("v", i) for i in range(TT + 1)]]

        def pa_tile(i):
            return PA[:, ds(i, 1), :].rearrange("p o t -> p (o t)")

        def pb_tile(i):
            return PB[:, ds(i, 1), :].rearrange("p o t -> p (o t)")

        def nat_counts(L, kind):
            n = max(n for n, (k, i) in enumerate(NAT[L]) if k == kind) + 1
            return (n + 1) // 2, n // 2

        def nat_src(kind, c, i):
            t = {"k": PA[:, CT + c, :], "v": PA[:, 2 * CT + c, :], "g": PB[:, CT + c, :]}[kind]
            return t[:, i * P:min((i + 1) * P, T)]

        def nat_bank(L, n):
            return B[4 + n % 2] if L == 0 and n < NG else B[n % 4]

        def nat_dst(kind, i):
            t = {"k": KN, "v": VN, "g": GN}[kind]
            return t[:, i, :] if i < TT else t[0:NS, i, :]

        N_STORES = 3 + 2 + 2

        block = ctx.enter_context(nc.Block())

        @block.sync
        def _(sp):
            sp.dma_start(XN[:, 0:TT, :], x_prompt[0].rearrange("(i p) d -> p i d", p=P)).then_inc(S["x_in"], 16)
            sp.dma_start(XN[0:NS, TT, :], x_sample.rearrange("b t d -> (b t) d")).then_inc(S["x_in"], 16)
            sp.dma_start(pages[0:1, :], page_table.rearrange("(o a) b -> o (a b)", o=1)).then_inc(S["pt_in"], 16)
            sp.dma_start(vec_rows[0:2 * KT, :], g_mix.rearrange("l (k p) -> (l k) p", p=P)).then_inc(S["vec_in"], 16)
            sp.dma_start(vec_rows[2 * KT:4 * KT, :], g_mlp.rearrange("l (k p) -> (l k) p", p=P)).then_inc(S["vec_in"], 16)
            sp.dma_start(vec_rows[4 * KT:5 * KT, :], g_final.rearrange("(k p) -> k p", p=P)).then_inc(S["vec_in"], 16)
            sp.dma_start(vec_rows[5 * KT:n_vec, :], conv_w[0].rearrange("w (k p) -> (w k) p", p=P)).then_inc(S["vec_in"], 16)
            sp.dma_start(bf[:, :], b_forget[0:1, :].partition_broadcast(P)).then_inc(S["small_in"], 16)
            def load_weights(view, col0):
                def body(g, i, u, more):
                    sp.wait_ge(S["w_low"], g + 1)
                    sp.dma_start(WR[u][:, :, :], view[:, :, ds(i * P + col0, P)]).then_inc(S[f"w_loaded{u}"], 16)
                return body

            for L in range(2):
                side = FCOL + (NH if L == 0 else 0)
                for u in range(2):
                    load_weights(in_v[L], side)(G_IN[L] + u, u, u, None)
                if L == 0:
                    sp.dma_start(WF[:, :, :], in_v[0][:, :, FCOL:FCOL + P]).then_inc(S["wf_in"], 16)
                unit_loop(sp, load_weights(in_v[L], side + 2 * P), G_IN[L] + 2, n_b[L] - 2)
                unit_loop(sp, load_weights(in_v[L], 0), G_QKV[L], 3 * CT)

                def load_k(s, j):
                    v = sp.value_load(pages[0:1, ds(s * PG + j, 1)], min_val=0, max_val=POOL - 1)
                    sp.wait_ge(S[f"k_turned{L}"], s * PG + (j + 1))
                    sp.dma_start(KR[:, j % 4, :], cache_k[L][0][ds(v, 1)].rearrange("o p h d -> (o p) (h d)")
                                 ).then_inc(S[f"k_in{L}_{j % 4}"], 16)

                def load_v(s, first_wait):
                    for j in range(PG):
                        v = sp.value_load(pages[0:1, ds(s * PG + j, 1)], min_val=0, max_val=POOL - 1)
                        if j == 0 and first_wait:
                            sp.wait_ge(S["sgu_out"], 4)
                        if j == 0:
                            sp.wait_ge(S[f"v_used{L}"], s + 1)
                        sp.dma_start(VR[:, j, :], cache_v[L][0][ds(v, 1)].rearrange("o p h d -> (o p) (h d)")
                                     ).then_inc(S[f"v_in{L}"], 16)

                for u in range(2):
                    load_weights(out_v[L], 0)(G_OUT[L] + u, u, u, None)
                for j in range(PG + 4):
                    load_k(j // PG, j % PG)
                load_v(0, L == 0)
                with sp.Fori(1, NB - 1) as s:
                    for j in range(4, PG):
                        load_k(s, j)
                    for j in range(4):
                        load_k(s + 1, j)
                    load_v(s, False)
                for j in range(4, PG):
                    load_k(NB - 1, j)
                load_v(NB - 1, False)
                unit_loop(sp, load_weights(out_v[L], 2 * P), G_OUT[L] + 2, KT - 2)
                g = G_MLP[L]
                for kind, grp in MLP_ORDER:
                    view = up_v[L] if kind == "up" else dn_v[L][grp]
                    unit_loop(sp, load_weights(view, grp * DM if kind == "up" else 0), g, KT)
                    g += KT
            sp.wait_ge(S["stored"], N_STORES * 16)
            sp.wait_ge(S["stored_kn"], 4 * 16)
            sp.wait_ge(S["stored_v"], 4 * 16)

        @block.gpsimd
        def _(pool):
            g = nc.gpsimd
            for t in (ident, neg_causal, neg_strict, seq_neg_causal, seq_neg_strict, step_rep):
                g.memset(t[:], 0.0)
            for t in (ones, upto, after, before, seq_upto, seq_before, seq_same):
                last = g.memset(t[:], 1.0)
            last.then_inc(S["zeroed"], 1)
            pool.wait_ge(S["zeroed"], 1)
            sel = g.affine_select

            def step(ins, n=[1]):
                n[0] += 1
                ins.then_inc(S["zeroed"], 1)
                pool.wait_ge(S["zeroed"], n[0])

            sel(out=ident[:], in_=ident[:], compare_op=ALU.not_equal, fill=1.0, base=0, pattern=[[-1, P]], channel_multiplier=1)
            sel(out=upto[:], in_=upto[:], compare_op=ALU.is_ge, fill=0.0, base=0, pattern=[[1, P]], channel_multiplier=-1)
            sel(out=before[:], in_=before[:], compare_op=ALU.is_gt, fill=0.0, base=0, pattern=[[1, P]], channel_multiplier=-1)
            sel(out=after[:], in_=after[:], compare_op=ALU.is_gt, fill=0.0, base=0, pattern=[[-1, P]], channel_multiplier=1)
            sel(out=neg_causal[:], in_=neg_causal[:], compare_op=ALU.is_ge, fill=NEG, base=0, pattern=[[1, P]], channel_multiplier=-1)
            sel(out=neg_strict[:], in_=neg_strict[:], compare_op=ALU.is_gt, fill=NEG, base=0, pattern=[[1, P]], channel_multiplier=-1)
            sel(out=step_rep[:], in_=step_rep[:], compare_op=ALU.not_equal, fill=1.0, base=0, pattern=[[0, NB], [-1, NT]], channel_multiplier=1)
            step(sel(out=seq_same[:], in_=seq_same[:], compare_op=ALU.is_ge, fill=0.0, base=0, pattern=[[-NT, NB]], channel_multiplier=1))
            sel(out=seq_same[:], in_=seq_same[:], compare_op=ALU.is_ge, fill=0.0, base=NT - 1, pattern=[[NT, NB]], channel_multiplier=-1)
            for t, cmp, rows, base, fill in ((seq_upto, ALU.is_ge, slice(0, NS), 0, 0.0), (seq_upto, ALU.is_ge, slice(NS, P), 0, 0.0),
                                             (seq_before, ALU.is_gt, slice(0, NS), 0, 0.0),
                                             (seq_neg_causal, ALU.is_ge, slice(0, NS), 0, NEG), (seq_neg_strict, ALU.is_gt, slice(0, NS), 0, NEG)):
                step(sel(out=t[rows], in_=t[rows], compare_op=ALU.is_ge, fill=fill, base=base, pattern=[[-NT, NB], [0, NT]], channel_multiplier=1))
                step(sel(out=t[rows], in_=t[rows], compare_op=cmp, fill=fill, base=base, pattern=[[NT, NB], [1, NT]], channel_multiplier=-1))
            g.drain().then_inc(S["consts"], 1)
            pool.wait_ge(S["pt_in"], 16)
            for q in range(NB * PG):
                v = pool.value_load(pages[0:1, q:q + 1], min_val=0, max_val=POOL - 1)
                pool.dma_start(lf_raw[q:q + 1, :, :], cache_fox_logf[0][ds(v, 1)]).then_inc(S["lfp_in"], 16)

            for L in range(2):
                tk_p, tk_s = ((p_fox_k, s_fox_k), (p_sb_k, s_sb_k))[L]
                tv_p, tv_s = ((p_fox_v, s_fox_v), (p_sb_v, s_sb_v))[L]
                if L == 0:
                    pool.wait_ge(S["lf_suffixed"], 1)
                    pool.wait_ge(S["d_past"], 1)
                    pool.dma_start(WSN[:, :, :], w_spatial[0].rearrange("g t s -> t g s")).then_inc(S["sgu_in"], 16)
                    pool.dma_start(g_row[:, :], sgu_g[0:1, :].partition_broadcast(P)).then_inc(S["sgu_in"], 16)
                    pool.dma_start(b_row[:, :], sgu_b[0:1, :].partition_broadcast(P)).then_inc(S["sgu_in"], 16)
                    for g8 in range(GB):
                        pool.dma_start(bs_row[HD * (g8 % 2):HD * (g8 % 2) + HD, g8 // 2, :],
                                       b_spatial[0, g8:g8 + 1, :].partition_broadcast(HD)).then_inc(S["sgu_in"], 16)
                    pool.wait_ge(S["f_logf"], 1)
                    pool.dma_start(p_fox_logf[0, 0].rearrange("(i p) h -> p i h", p=P), LF[:, 3, 0:TT, :]).then_inc(S["stored"], 16)
                    pool.dma_start(s_fox_logf[0].rearrange("b t h -> (b t) h"), LF[NS:P, 3, TT, :]).then_inc(S["stored"], 16)
                    pool.wait_ge(S["ln_done"], 1)
                    pool.dma_start(s_sgu_v[0].rearrange("b t d -> (b t) d"), GN[0:NS, TT, :]).then_inc(S["stored"], 16)
                else:
                    pool.wait_ge(S["unit_done"], G_IN1 + 1)
                    pool.dma_start(prev_n[0:2 * NB, :], state_conv[0].rearrange("b r d -> (b r) d")).then_inc(S["state_in"], 16)
                    pool.wait_ge(S["tail_copied"], 1)
                    pool.dma_start(p_conv[0, 0], tail_n[0:2, :]).then_inc(S["stored"], 16)
                    pool.dma_start(s_conv[0].rearrange("b r d -> (b r) d"), tail_n[2:2 + 2 * NB, :]).then_inc(S["stored"], 16)
                pool.wait_ge(S[f"nat_dve{L}"], nat_counts(L, "k")[0])
                pool.wait_ge(S[f"nat_act{L}"], nat_counts(L, "k")[1])
                pool.dma_start(tk_p[0, 0].rearrange("(i p) h d -> p i (h d)", p=P), KN[:, 0:TT, :]).then_inc(S["stored_kn"], 16)
                pool.dma_start(tk_s[0].rearrange("b t h d -> (b t) (h d)"), KN[0:NS, TT, :]).then_inc(S["stored_kn"], 16)
                pool.wait_ge(S[f"nat_dve{L}"], nat_counts(L, "v")[0])
                pool.wait_ge(S[f"nat_act{L}"], nat_counts(L, "v")[1])
                pool.dma_start(tv_p[0, 0].rearrange("(i p) h d -> p i (h d)", p=P), VN[:, 0:TT, :]).then_inc(S["stored_v"], 16)
                pool.dma_start(tv_s[0].rearrange("b t h d -> (b t) (h d)"), VN[0:NS, TT, :]).then_inc(S["stored_v"], 16)

            pool.wait_ge(S["y_copied"], KT)
            pool.dma_start(y_prompt[0].rearrange("(i p) d -> p i d", p=P), XN[:, 0:TT, :]).then_inc(S["stored"], 16)
            pool.dma_start(y_sample.rearrange("b t d -> (b t) d"), XN[0:NS, TT, :]).then_inc(S["stored"], 16)

        @block.scalar
        def _(act):
            A = nc.scalar.activation
            nc.scalar.preload_act_table_set("natural_log_exp_and_others")
            act.sem_inc(S["evac_act"], 2)

            def cut_high(g):
                act.wait_ge(S[f"w_loaded{g % 2}"], 16 * (g // 2 + 1))
                if g > 1:
                    act.wait_ge(S["unit_done"], g)
                A(WH[g % 2][:], WR[g % 2][:], ACT.Copy).then_inc(S["w_high"], 1)

            def next_high(g, u, more):
                if more == "second":
                    cut_high(g + 2)
                if more != "next":
                    return
                act.wait_ge(S[f"w_loaded{1 - u}"], loads_after(g, u))
                act.wait_ge(S["unit_done"], g + 1)
                A(WH[1 - u][:], WR[1 - u][:], ACT.Copy).then_inc(S["w_high"], 1)

            def loads_after(g, u):
                return (g - u) * 8 + (16 if u == 0 else 32)

            def evac_in(tile_of):
                def body(g, i, u, more):
                    next_high(g, u, more)
                    act.wait_ge(S["unit_done"], g + 2)
                    A(tile_of(i)[:, 0:TH], B[2 * u][:, 0:TH], ACT.Copy).then_inc(S["evac_act"], 1)
                return body

            def evac_sq(g, i, u, more):
                next_high(g, u, more)
                act.wait_ge(S["evac_dve"], g + 3)
                A(TMP[:, u, :], X[:, ds(i, 1), :], ACT.Square).then_inc(S["evac_act"], 1)

            def evac_none(g, i, u, more):
                next_high(g, u, more)
                act.sem_inc(S["evac_act"], 1)

            def evac_up(L, grp):
                m0 = L * FG * KT + grp * KT
                def body(g, i, u, more):
                    next_high(g, u, more)
                    act.wait_ge(S["unit_done"], g + 2)
                    act.wait_ge(S["evac_dve"], g + 1)
                    for h in range(2):
                        last = A(TMP[:, u, h * TH:(h + 1) * TH], B[2 * u + h][:, 0:TH], ACT.Relu)
                    last.then_inc(S["evac_act"], 1)
                    act.wait_ge(S["relu_squared"], i + (m0 + 1))
                    A(ffH[grp % 2][:, ds(i, 1), :], TMP[:, u, :], ACT.Copy).then_inc(S["ff_high"], 1)
                return body

            def norm(z):
                act.wait_ge(S["rms_mean"], z + 1)
                A(R[:], R[:], ACT.Ln).then_inc(S["rms_ln"], 1)
                act.wait_ge(S["rms_ln"], z + 1)
                A(R[:], R[:], ACT.Exp, scale=-0.5).then_inc(S["rms_scale"], 1)
                for k in range(KT):
                    act.wait_ge(S["normed"], z * KT + k + 1)
                    if z < 4:
                        A(HH[:, k, :], TMP[:, k % 2, :], ACT.Copy).then_inc(S["norm_high"], 1)

            for k in range(KT):
                act.wait_ge(S["x_copied"], k + 1)
                if k >= 2:
                    act.wait_ge(S["x_summed"], k - 1)
                A(TMP[:, k % 2, :], X[:, k, :], ACT.Square).then_inc(S["x_squared"], 1)
            cut_high(0)
            cut_high(1)
            norm(0)
            act.wait_ge(S["wf_in"], 16)
            A(WFH[:], WF[:], ACT.Copy).then_inc(S["wf_high"], 1)

            for L in range(2):
                if L == 1:
                    cut_high(G_IN[1] + 1)
                    norm(2)
                def copy_natural(n0, n1):
                    for n in range(n0, n1):
                        if n % 2 == 1:
                            kind, i = NAT[L][n]
                            act.wait_ge(S[f"nat_turned{L}"], n + 1)
                            rows = P if i < TT else NS
                            A(nat_dst(kind, i), nat_bank(L, n)[0:rows, :], ACT.Copy).then_inc(S[f"nat_act{L}"], 1)

                unit_loop(act, evac_in(pb_tile), G_IN[L], n_b[L], first_plain=True)
                if L == 0:
                    act.wait_ge(S["lf_turned"], 1)
                    A(lf_pos[:].rearrange("p h b j -> p (h b j)"), B7[:, :], ACT.Copy).then_inc(S["lf_copied"], 1)
                    act.wait_ge(S["f_logits"], 1)
                    A(FT[:, 0:TH], B4[0:NH, 0:TH], ACT.Copy)
                    A(FT[:, TH:T], B5[0:NH, 0:TH], ACT.Copy).then_inc(S["f_copied"], 1)
                    act.wait_ge(S["f_biased"], 1)
                    A(LF[:, 1], LF[:, 0], ACT.Abs).then_inc(S["f_abs"], 1)
                    act.wait_ge(S["f_abs"], 1)
                    A(LF[:, 2], LF[:, 1], ACT.Exp, scale=-1.0).then_inc(S["f_exp"], 1)
                    act.wait_ge(S["f_exp"], 1)
                    A(LF[:, 1], LF[:, 2], ACT.Ln, bias=1.0).then_inc(S["f_ln"], 1)
                    copy_natural(0, NG)
                    unit_loop(act, evac_in(pa_tile), G_QKV[L], 2)
                    act.wait_ge(S["ln_var"], 1)
                    rstd = small[:, 50:50 + TT + 1]
                    A(rstd, rstd, ACT.Ln).then_inc(S["ln_scale"], 1)
                    act.wait_ge(S["ln_scale"], 1)
                    A(rstd, rstd, ACT.Exp, scale=-0.5).then_inc(S["ln_scale"], 1)
                    unit_loop(act, evac_in(pa_tile), G_QKV[L] + 2, 3 * CT - 2, i0=2)
                else:
                    unit_loop(act, evac_in(pa_tile), G_QKV[L], 3 * CT)
                name = "sgu" if L == 0 else "conv"
                for c in range(CT):
                    act.wait_ge(S[f"{name}_out"], c + 1)
                    A(HH[:, CT + c, :], PB[:, c, :], ACT.Copy).then_inc(S[f"{name}_high"], 1)
                    if c == 1:
                        copy_natural(NG if L == 0 else 0, len(NAT[L]))
                cut_high(G_OUT[L] + 1)

                act.wait_ge(S[f"nat_dve{L}"], nat_counts(L, "v")[0])
                act.wait_ge(S[f"q_block{L}"], 1)

                def stage_qk(it):
                    A(qH[:], PA[:, ds(it, 1), 0:NP].rearrange("p o t -> p (o t)"), ACT.Copy, scale=QS)
                    A(kH[:], PA[:, ds(it + CT, 1), 0:NP].rearrange("p o t -> p (o t)"), ACT.Copy).then_inc(S["qk_high"], 1)

                def copy_page(s, j):
                    act.wait_ge(S[f"k_turned{L}"], s * PG + (j + 5))
                    A(KTS[:, j % 2, :], B[6 - j % 2][:, :], ACT.Copy).then_inc(S[f"kt_copied{L}"], 1)

                def prompt_exp(s):
                    act.wait_ge(S["shifted"], s + (NB * L + 1))
                    A(S_[:], S_[:], ACT.Exp).then_inc(S["probs"], 1)

                def prompt_high(s):
                    act.wait_ge(S["probs"], s + (NB * L + 1))
                    act.wait_ge(S[f"prompt_av{L}"], s + 1)
                    A(PH[:], S_[:], ACT.Copy).then_inc(S["p_high"], 1)

                def sample_exp(s):
                    act.wait_ge(S["dec_shifted"], s + (NB * L + 1))
                    A(SS[:, 0:ex + HT], SS[:, 0:ex + HT], ACT.Exp).then_inc(S["dec_probs"], 1)

                ex = PG * HT

                def step(s, it, e, more):
                    if e == 0:
                        act.wait_ge(S[f"prompt_av{L}"], s + 1)
                        A(vH[:], VN[:, 0:TT, ds(it * P, P)], ACT.Copy).then_inc(S["v_high"], 1)
                    if e == 1 and more:
                        act.wait_ge(S["scores"], s + (NB * L + 1))
                        stage_qk(it + 1)

                    def copy_pages(*js):
                        for j in js if more else ():
                            copy_page(s + 1, j)

                    def o_high():
                        if e == 1:
                            act.wait_ge(S["prompt_out"], s + (NB * L + 1))
                            A(HH[:, ds(it, 1), 0:NP].rearrange("p o t -> p (o t)"), OT[:], ACT.Copy).then_inc(S["o_high"], 1)

                    if L == 0:
                        copy_pages(0, 1)
                        sample_exp(s)
                        copy_pages(2, 3, 4, 5)
                        o_high()
                        copy_pages(6, 7)
                        if more:
                            prompt_exp(s + 1)
                            prompt_high(s + 1)
                    else:
                        act.wait_ge(S["dec_av"], s + ((NB + 1) * L + 1))
                        act.wait_ge(S["av_copied"], s + (NB * L))
                        A(SL[:, 0:ex], B7[:, :], ACT.Abs)
                        A(SL[0:NS, ex:], B5[0:NS, P:P + HT], ACT.Abs).then_inc(S["dsb_abs"], 1)
                        act.wait_ge(S["dsb_abs"], s + 1)
                        A(SL[:, 0:ex], SL[:, 0:ex], ACT.Exp, scale=-1.0)
                        A(SL[0:NS, ex:], SL[0:NS, ex:], ACT.Exp, scale=-1.0).then_inc(S["dsb_exp"], 1)
                        act.wait_ge(S["dsb_exp"], s + 1)
                        A(SL[:, 0:ex], SL[:, 0:ex], ACT.Ln, bias=1.0)
                        A(SL[0:NS, ex:], SL[0:NS, ex:], ACT.Ln, bias=1.0).then_inc(S["dsb_ln"], 1)
                        copy_pages(0)
                        prompt_exp(s)
                        prompt_high(s)
                        copy_pages(1, 2)
                        sample_exp(s)
                        if more:
                            sb_abs(s + 1)
                        copy_pages(3, 4)
                        if more:
                            sb_exp(s + 1)
                        copy_pages(5)
                        if more:
                            sb_ln(s + 1)
                        copy_pages(6)
                        o_high()
                        copy_pages(7)
                        if more:
                            sb_high(s + 1)

                def sb_abs(s):
                    act.wait_ge(S["scores"], s + (NB * L + 1))
                    for o in range(0, SC, 512):
                        n = min(512, SC - o)
                        last = A(L_[:, o:o + n], B[o // 512][:, 0:n], ACT.Abs)
                    last.then_inc(S["sb_abs"], 1)

                def sb_exp(s):
                    act.wait_ge(S["sb_abs"], s + 1)
                    A(L_[:], L_[:], ACT.Exp, scale=-1.0).then_inc(S["sb_exp"], 1)

                def sb_ln(s):
                    act.wait_ge(S["sb_exp"], s + 1)
                    A(L_[:], L_[:], ACT.Ln, bias=1.0).then_inc(S["sb_ln"], 1)

                def sb_high(s):
                    act.wait_ge(S["sb_sp"], s + 1)
                    act.wait_ge(S["prompt_av1"], s + 1)
                    A(PH[:], L_[:], ACT.Copy).then_inc(S["sp_high"], 1)

                stage_qk(0)
                for j in range(PG):
                    copy_page(0, j)
                if L == 0:
                    prompt_exp(0)
                    prompt_high(0)
                else:
                    sb_abs(0)
                    sb_exp(0)
                    sb_ln(0)
                    sb_high(0)
                with act.Fori(0, CT - 1) as it:
                    for e in range(2):
                        step(it * 2 + e, it, e, True)
                for e in range(2):
                    step(NB - 2 + e, CT - 1, e, e == 0)
                act.wait_ge(S[f"dec_out{L}"], NB + 1)
                A(HH[:, 0:CT, NP:T], OS[:], ACT.Copy).then_inc(S["os_high"], 1)

                unit_loop(act, evac_sq, G_OUT[L], KT, first_plain=True)
                cut_high(G_MLP[L] + 1)
                norm(1 + 2 * L)
                g = G_MLP[L]
                for n, (kind, grp) in enumerate(MLP_ORDER):
                    last = L == 1 and n == len(MLP_ORDER) - 1
                    body = evac_up(L, grp) if kind == "up" else evac_sq if grp == FG - 1 else evac_none
                    unit_loop(act, body, g, KT, last, n == 0)
                    g += KT
            norm(4)

        @block.vector
        def _(dve):
            V = nc.vector
            dve.sem_inc(S["evac_dve"], 2)
            dve.sem_inc(S["w_low"], 2)

            def cut_low(g, u):
                dve.wait_ge(S["w_high"], g + 1)
                V.tensor_tensor(WL[u][:], WR[u][:], WH[u][:].bitcast(F32), ALU.subtract).then_inc(S["w_low"], 1)

            def next_low(g, u, more):
                if more == "second":
                    cut_low(g + 2, u)
                if more == "next":
                    cut_low(g + 1, 1 - u)

            def evac_in(tile_of):
                def body(g, i, u, more):
                    next_low(g, u, more)
                    dve.wait_ge(S["unit_done"], g + 2)
                    V.tensor_copy(tile_of(i)[:, TH:T], B[2 * u + 1][:, 0:TH]).then_inc(S["evac_dve"], 1)
                return body

            def evac_add(squares):
                def body(g, i, u, more):
                    next_low(g, u, more)
                    dve.wait_ge(S["unit_done"], g + 2)
                    for h in range(2):
                        x = X[:, ds(i, 1), h * TH:(h + 1) * TH].rearrange("p o t -> p (o t)")
                        last = V.tensor_tensor(x, B[2 * u + h][:, 0:TH], x, ALU.add)
                    last.then_inc(S["evac_dve"], 1)
                    if squares:
                        dve.wait_ge(S["evac_act"], g + 3)
                        V.tensor_tensor(SQS[:], SQS[:], TMP[:, u, :], ALU.add).then_inc(S["sum_step"], 1)
                return body

            def evac_up(L, grp):
                m0 = L * FG * KT + grp * KT
                def body(g, i, u, more):
                    next_low(g, u, more)
                    dve.wait_ge(S["evac_act"], g + 3)
                    V.tensor_tensor(TMP[:, u, :], TMP[:, u, :], TMP[:, u, :], ALU.mult).then_inc(S["relu_squared"], 1)
                    dve.wait_ge(S["ff_high"], i + (m0 + 1))
                    V.tensor_tensor(ffL[grp % 2][:, ds(i, 1), :], TMP[:, u, :].unsqueeze(1),
                                    ffH[grp % 2][:, ds(i, 1), :].bitcast(F32), ALU.subtract).then_inc(S["evac_dve"], 1)
                return body

            def norm(z):
                dve.wait_ge(S["rms_sum"], z + 1)
                for h in range(2):
                    last = V.tensor_scalar(R[:, h * TH:(h + 1) * TH], B[h][:, 0:TH], 1.0 / DM, EPS, ALU.mult, ALU.add)
                last.then_inc(S["rms_mean"], 1)
                V.memset(SQS[:], 0.0)
                dve.wait_ge(S["rms_scale"], z + 1)

                def scale(k):
                    gain = vec[:, NORM_G[z] + k:NORM_G[z] + k + 1]
                    dst = TMP[:, k % 2, :] if z < 4 else Y[:, k, :]
                    V.scalar_tensor_tensor(dst, X[:, k, :], gain, R[:], ALU.mult, ALU.mult).then_inc(S["normed"], 1)
                scale(0)
                for k in range(KT):
                    if k + 1 < KT:
                        if 1 <= k and z < 4:
                            dve.wait_ge(S["norm_low"], z * KT + k)
                        scale(k + 1)
                    if z < 4:
                        dve.wait_ge(S["norm_high"], z * KT + k + 1)
                        V.tensor_tensor(HL[:, k, :], TMP[:, k % 2, :], HH[:, k, :].bitcast(F32), ALU.subtract).then_inc(S["norm_low"], 1)

            dve.wait_ge(S["consts"], 1)
            V.tensor_copy(ones_r[:], ones[:])
            V.tensor_copy(after_r[:], after[:])
            dve.wait_ge(S["vec_turned"], 1)
            V.tensor_copy(vec[:], B[6][:, 0:n_vec])
            for k in range(KT):
                dve.wait_ge(S["x_turned"], k + 1)
                V.tensor_copy(X[:, k, 0:NP], B[2 * (k % 2)][:, :])
                V.tensor_copy(X[:, k, NP:T], B[2 * (k % 2) + 1][:, 0:NS]).then_inc(S["x_copied"], 1)
                dve.wait_ge(S["x_squared"], k + 1)
                if k == 0:
                    V.tensor_copy(SQS[:], TMP[:, 0, :]).then_inc(S["x_summed"], 1)
                else:
                    dve.wait_ge(S["x_summed"], k)
                    V.tensor_tensor(SQS[:], SQS[:], TMP[:, k % 2, :], ALU.add).then_inc(S["x_summed"], 1)
            cut_low(0, 0)
            cut_low(1, 1)
            norm(0)
            dve.wait_ge(S["wf_high"], 1)
            V.tensor_tensor(WFL[:], WF[:], WFH[:].bitcast(F32), ALU.subtract).then_inc(S["wf_low"], 1)

            for L in range(2):
                if L == 1:
                    cut_low(G_IN[1] + 1, 1)
                    norm(2)
                unit_loop(dve, evac_in(pb_tile), G_IN[L], n_b[L], first_plain=True)

                def copy_natural(n0, n1):
                    for n in range(n0, n1):
                        if n % 2 == 0:
                            kind, i = NAT[L][n]
                            dve.wait_ge(S[f"nat_turned{L}"], n + 1)
                            rows = P if i < TT else NS
                            V.tensor_copy(nat_dst(kind, i), nat_bank(L, n)[0:rows, :]).then_inc(S[f"nat_dve{L}"], 1)

                if L == 0:
                    dve.wait_ge(S["lf_copied"], 1)
                    V.memset(lf_suf[:, :, :, PG - 1:PG], 0.0).then_inc(S["lf_suffix_step"], 1)
                    for j in range(PG - 2, -1, -1):
                        dve.wait_ge(S["lf_suffix_step"], PG - 1 - j)
                        V.tensor_tensor(lf_suf[:, :, :, j], lf_suf[:, :, :, j + 1], lf_pos[:, :, :, j + 1], ALU.add).then_inc(S["lf_suffix_step"], 1)
                    dve.wait_ge(S["lf_suffix_step"], PG)
                    V.memset(small[:, 95:96], 0.0).then_inc(S["lf_suffixed"], 1)
                    dve.wait_ge(S["f_turned"], 1)
                    dve.wait_ge(S["small_in"], 16)
                    V.tensor_tensor(LF[:, 0], B[6][:, 0:(TT + 1) * NH].rearrange("p (i h) -> p i h", h=NH),
                                    bf[:].unsqueeze(1).broadcast_to([P, TT + 1, NH]), ALU.add).then_inc(S["f_biased"], 1)
                    dve.wait_ge(S["lf_tail"], 1)
                    V.tensor_copy(D_past[:].rearrange("p b j h -> p (b j) h"),
                                  B7[:, :].rearrange("p (h n) -> p n h", h=NH)).then_inc(S["d_past"], 1)
                if L == 0:
                    dve.wait_ge(S["f_ln"], 1)
                    V.scalar_tensor_tensor(LF[:, 3], LF[:, 0], 0.0, LF[:, 1], ALU.min, ALU.subtract).then_inc(S["f_logf"], 1)
                    copy_natural(0, NG)

                tiles = [(i, P if i < TT else NS) for i in range(TT + 1)]

                def ln_stats():
                    V.memset(small[:, 0:96], 1.0).then_inc(S["ln_step"], 1)
                    dve.wait_ge(S["ln_step"], 1)
                    dve.wait_ge(S["nat_act0"], NG // 2)
                    for i, rows in tiles:
                        last = V.bn_stats(small[0:rows, 16 + 6 * i:22 + 6 * i], GN[0:rows, i, :])
                    last.then_inc(S["ln_step"], 1)

                def ln_moments():
                    dve.wait_ge(S["ln_step"], 2)
                    for i, rows in tiles:
                        last = V.bn_aggr(small[0:rows, 2 * i:2 * i + 2], small[0:rows, 16 + 6 * i:22 + 6 * i])
                    last.then_inc(S["ln_step"], 1)
                    dve.wait_ge(S["ln_step"], 3)
                    var = small[:, 0:2 * TT + 2].rearrange("p (i w) -> p i w", w=2)[:, :, 1]
                    V.tensor_scalar(small[:, 50:50 + TT + 1], var, EPS, None, ALU.add).then_inc(S["ln_var"], 1)

                def ln_scale():
                    dve.wait_ge(S["ln_scale"], 2)
                    for i, rows in tiles:
                        last = V.tensor_scalar(GN[0:rows, i, :], GN[0:rows, i, :], small[0:rows, 2 * i:2 * i + 1],
                                               small[0:rows, 50 + i:51 + i], ALU.subtract, ALU.mult)
                    last.then_inc(S["ln_step"], 1)

                def ln_gain():
                    dve.wait_ge(S["ln_step"], 4)
                    dve.wait_ge(S["sgu_in"], 16 * (3 + GB))
                    for i, rows in tiles:
                        last = V.tensor_tensor(GN[0:rows, i, :], GN[0:rows, i, :], g_row[0:rows, :], ALU.mult)
                    last.then_inc(S["ln_step"], 1)

                def ln_bias():
                    dve.wait_ge(S["ln_step"], 5)
                    for i, rows in tiles:
                        last = V.tensor_tensor(GN[0:rows, i, :], GN[0:rows, i, :], b_row[0:rows, :], ALU.add)
                    last.then_inc(S["ln_done"], 1)

                def mask_spatial():
                    dve.wait_ge(S["F_sums"], 1)
                    V.tensor_scalar(F_neg[:].rearrange("p i h -> p (i h)"), B[5][:, 0:TT * NH], -1.0, None, ALU.mult)
                    V.tensor_scalar(Fn_neg[:], B[5][0:NS, 64:64 + NH], -1.0, None, ALU.mult)
                    dve.wait_ge(S["ws_turned"], 1)
                    for h in range(2):
                        last = V.tensor_tensor(WST[:, 4 * h:4 * h + 4, :], B[6 + h][:, :].rearrange("p (g t) -> p g t", t=P),
                                               upto[:].unsqueeze(1).broadcast_to([P, 4, P]), ALU.mult)
                    last.then_inc(S["ws_masked"], 1)

                def spread_spatial():
                    dve.wait_ge(S["rep_done"], 1)
                    rep = B[4][0:NS, 0:GB * NT].rearrange("p (g t) -> p g t", t=NT)
                    for b in range(NB):
                        last = V.tensor_scalar(WBD[:, :, b, :], rep, seq_same[:, b:b + 1], None, ALU.mult)
                    last.then_inc(S["bd_set"], 1)

                def gate(c):
                    dve.wait_ge(S["mixed"], c + 1)
                    t = TMP[:, c % 2, :]
                    V.tensor_tensor(t[:, 0:NP].rearrange("p (i t) -> p i t", t=P), B[4 + 2 * (c % 2)][:, :].rearrange("p (i t) -> p i t", t=P),
                                    bs_row[:, c, :].unsqueeze(1).broadcast_to([P, TT, P]), ALU.add)
                    V.tensor_tensor(t[:, NP:T].rearrange("p (b t) -> p b t", t=NT),
                                    B[5 + 2 * (c % 2)][:, 0:NS].rearrange("p (b t) -> p b t", t=NT),
                                    bs_row[:, c, 0:NT].unsqueeze(1).broadcast_to([P, NB, NT]), ALU.add).then_inc(S["sgu_step"], 1)
                    dve.wait_ge(S["sgu_step"], c + 1)
                    V.tensor_tensor(PB[:, c, :], t, PB[:, c, :], ALU.mult).then_inc(S["sgu_out"], 1)

                def conv_rows():
                    dve.wait_ge(S["evac_dve"], G_QKV[1] + 2)
                    dve.wait_ge(S["evac_act"], G_QKV[1] + 2)
                    V.memset(UE[:, :, 0:2], 0.0)
                    V.tensor_tensor(UE[:, :, 2:2 + NP], PB[:, CT:2 * CT, 0:NP], PB[:, 2 * CT:3 * CT, 0:NP], ALU.mult)

                def conv_sample_rows():
                    dve.wait_ge(S["state_turned"], 1)
                    for c in range(CT):
                        V.tensor_copy(SE[:, c, :, 0:2], B[4][:, c * 2 * NB:(c + 1) * 2 * NB].rearrange("p (b r) -> p b r", r=2))
                        last = V.tensor_tensor(SE[:, c, :, 2:2 + NT], PB[:, CT + c, NP:T].rearrange("p (b t) -> p b t", t=NT),
                                               PB[:, 2 * CT + c, NP:T].rearrange("p (b t) -> p b t", t=NT), ALU.mult)
                    last.then_inc(S["ue_set"], 1)
                    dve.wait_ge(S["ue_set"], 1)
                    V.tensor_copy(tail[:, :, 0:2], UE[:, :, NP:NP + 2])
                    for c in range(CT):
                        last = V.tensor_copy(tail[:, c, 2:2 + 2 * NB].rearrange("p (b r) -> p b r", r=2), SE[:, c, :, NT:NT + 2])
                    last.then_inc(S["tail_set"], 1)

                def conv_state_out():
                    dve.wait_ge(S["tail_turned"], 1)
                    V.tensor_copy(tail_n[:], B[5][0:2 + 2 * NB, :]).then_inc(S["tail_copied"], 1)

                def conv(c):
                    t = TMP[:, c % 2, :]
                    tp, ts = t[:, 0:NP], t[:, NP:T].rearrange("p (b t) -> p b t", t=NT)
                    for j in range(NCV):
                        w = vec[:, CONV_V + j * CT + c:CONV_V + j * CT + c + 1]
                        up, us = UE[:, c, j:j + NP], SE[:, c, :, j:j + NT]
                        if j == 0:
                            V.tensor_scalar(tp, up, w, None, ALU.mult)
                            V.tensor_scalar(ts, us, w, None, ALU.mult).then_inc(S["conv_step"], 1)
                        else:
                            V.scalar_tensor_tensor(tp, up, w, tp, ALU.mult, ALU.add)
                            V.scalar_tensor_tensor(ts, us, w, ts, ALU.mult, ALU.add).then_inc(S["conv_step"], 1)
                        dve.wait_ge(S["conv_step"], c * NCV + j + 1)
                    V.tensor_tensor(PB[:, c, :], t, PB[:, c, :], ALU.mult).then_inc(S["conv_out"], 1)

                if L == 0:
                    steps = {0: ln_stats, 1: ln_moments, 2: ln_scale, 4: ln_gain, 5: ln_bias, 6: mask_spatial,
                             8: spread_spatial, 10: lambda: gate(0), 11: lambda: gate(1)}
                else:
                    steps = {0: conv_rows, 2: conv_sample_rows, 4: conv_state_out,
                             5: lambda: conv(0), 6: lambda: conv(1), 7: lambda: conv(2), 8: lambda: conv(3)}
                for i in range(3 * CT):
                    evac_in(pa_tile)(G_QKV[L] + i, i, i % 2, "next")
                    if i in steps:
                        steps[i]()
                if L == 0:
                    gate(2)
                    gate(3)
                copy_natural(NG if L == 0 else 0, len(NAT[L]))
                name = "sgu" if L == 0 else "conv"
                for c in range(CT):
                    dve.wait_ge(S[f"{name}_high"], c + 1)
                    V.tensor_tensor(HL[:, CT + c, :], PB[:, c, :], HH[:, CT + c, :].bitcast(F32), ALU.subtract).then_inc(S[f"{name}_low"], 1)
                cut_low(G_OUT[L] + 1, 1)

                dve.wait_ge(S["stored_kn"], 32 * (L + 1))
                if L == 0:
                    dve.wait_ge(S["stored"], 16 * 3)
                else:
                    dve.wait_ge(S["stored"], 16 * 5)
                V.memset(QB[:], 0.0).then_inc(S[f"q_block{L}"], 1)
                dve.wait_ge(S[f"q_block{L}"], 1)
                for e in range(2):
                    r = slice(HD * e, HD * e + HD)
                    last = V.tensor_scalar(QB[r, :, :, e, :], PA[r, 0:CT, NP:T].rearrange("p c (b t) -> p c b t", t=NT), QS, None, ALU.mult)
                last.then_inc(S[f"q_block{L}"], 1)
                ex = PG * HT
                flat1 = lambda t: t.rearrange("p o t -> p (o t)")

                def stage_qk(it):
                    dve.wait_ge(S["qk_high"], it + (CT * L + 1))
                    V.scalar_tensor_tensor(qL[:], flat1(PA[:, ds(it, 1), 0:NP]), QS, qH[:].bitcast(F32), ALU.mult, ALU.subtract)
                    V.tensor_tensor(kL[:], flat1(PA[:, ds(it + CT, 1), 0:NP]), kH[:].bitcast(F32), ALU.subtract).then_inc(S["qk_low"], 1)

                def fox_bias(s):
                    dve.wait_ge(S["scores"], s + 1)
                    for j in range(TT):
                        f = F_neg[:, j, ds(s, 1)]
                        last = V.scalar_tensor_tensor(S_[:, OFF[j]:OFF[j] + P], sc_bank(j, 0, P), f, neg_causal[:], ALU.add, ALU.add)
                        if WID[j] > P:
                            last = V.tensor_scalar(S_[:, OFF[j] + P:OFF[j] + WID[j]], sc_bank(j, P, WID[j] - P), f, None, ALU.add)
                    last.then_inc(S["biased"], 1)
                    dve.wait_ge(S["biased"], s + 1)
                    V.tensor_tensor(MX[:], S_[:, P:NP], S_[:, OFF[1]:OFF[1] + WID[1]], ALU.max).then_inc(S["max_step"], 1)
                    for j in range(2, TT):
                        dve.wait_ge(S["max_step"], s * (TT - 1) + (j - 1))
                        m = MX[:, (j - 1) * P:]
                        V.tensor_tensor(m, m, S_[:, OFF[j]:OFF[j] + WID[j]], ALU.max).then_inc(S["max_step"], 1)

                def fox_sample_bias(s):
                    dve.wait_ge(S["dec_av"], s + 1)
                    V.memset(SS[NS:P, ex:ex + HT], NEG)
                    V.tensor_tensor(SS[:, 0:ex].rearrange("p (n t) -> p n t", t=NT), B7[:, :].rearrange("p (n t) -> p n t", t=NT),
                                    D_past[:, ds(s, 1), :, :].rearrange("p o j h -> p (o j h)").unsqueeze(2).broadcast_to([P, PG * NH, NT]), ALU.add)
                    V.tensor_tensor(SS[0:NS, ex:ex + HT], B5[0:NS, P:P + HT], NBI[:, ds(s, 1), :, :].rearrange("p o h t -> p (o h t)"),
                                    ALU.add).then_inc(S["dec_biased"], 1)
                    dve.wait_ge(S["dec_biased"], s + 1)
                    V.tensor_reduce(RD[:, 2 * P:2 * P + HT], SS[:, 0:ex + HT].rearrange("p (j n) -> p n j", n=HT), AX.X, ALU.max).then_inc(S["dec_max_part"], 1)

                def fox_shift(s):
                    dve.wait_ge(S["max_turned"], s + 1)
                    V.tensor_reduce(small[:, 0:TT], B[3][:, :].rearrange("p (i k) -> p i k", k=P), AX.X, ALU.max).then_inc(S["max_rows"], 1)
                    dve.wait_ge(S["max_rows"], s + 1)
                    V.tensor_tensor(MD[:], ident[:].unsqueeze(1).broadcast_to([P, TT, P]),
                                    small[:, 0:TT].unsqueeze(2).broadcast_to([P, TT, P]), ALU.mult).then_inc(S["max_diag"], 1)
                    dve.wait_ge(S["max_spread"], s + 1)
                    for j in range(TT):
                        sj = S_[:, OFF[j]:OFF[j] + WID[j]]
                        last = V.tensor_tensor(sj, sj, B[3][:, j * P:NP], ALU.subtract)
                    last.then_inc(S["shifted"], 1)

                def fox_sample_shift(s):
                    dve.wait_ge(S["dec_max_turned"], s + 1)
                    V.tensor_reduce(small[0:HT, 8:9], B4[0:HT, 0:P], AX.X, ALU.max).then_inc(S["dec_max_rows"], 1)
                    dve.wait_ge(S["dec_max_rows"], s + 1)
                    V.tensor_scalar(MDD[:], ident[0:HT, 0:HT], small[0:HT, 8:9], None, ALU.mult).then_inc(S["dec_max_diag"], 1)
                    dve.wait_ge(S["dec_max_spread"], s + 1)
                    V.tensor_tensor(SS[:, 0:ex + HT].rearrange("p (j n) -> p j n", n=HT), SS[:, 0:ex + HT].rearrange("p (j n) -> p j n", n=HT),
                                    B4[:, P:P + HT].unsqueeze(1).broadcast_to([P, PG + 1, HT]), ALU.subtract).then_inc(S["dec_shifted"], 1)

                def sb_prompt_weights(s):
                    dve.wait_ge(S["sb_ln"], s + 1)
                    for o in range(0, SC, 512):
                        n = min(512, SC - o)
                        last = V.scalar_tensor_tensor(S_[:, o:o + n], B[o // 512][:, 0:n], 0.0, L_[:, o:o + n], ALU.min, ALU.subtract)
                    last.then_inc(S["sb_min"], 1)
                    dve.wait_ge(S["sb_min"], s + 1)
                    for o in range(0, SC, 512):
                        n = min(512, SC - o)
                        last = V.scalar_tensor_tensor(L_[:, o:o + n], B[o // 512][:, 0:n], 0.0, L_[:, o:o + n], ALU.max, ALU.add)
                    last.then_inc(S["sb_ls"], 1)
                    dve.wait_ge(S["sb_ls"], s + 1)
                    d, l = S_[:, OFF[3]:OFF[3] + P], L_[:, OFF[3]:OFF[3] + P]
                    V.tensor_tensor(l, l, before[:], ALU.mult)
                    d2, l2 = (t[:, 0:1024].rearrange("p (j c) -> p j c", c=512)[:, :, 0:P] for t in (S_, L_))
                    V.tensor_tensor(l2, l2, before[:].unsqueeze(1).broadcast_to([P, 2, P]), ALU.mult)
                    e, m = S_[:, OFF[2]:OFF[2] + P], L_[:, OFF[2]:OFF[2] + P]
                    V.tensor_tensor(m, m, before[:], ALU.mult).then_inc(S["sb_sp"], 1)
                    V.tensor_tensor(d, d, neg_strict[:], ALU.add)
                    V.tensor_tensor(e, e, neg_strict[:], ALU.add)
                    V.tensor_tensor(d2, d2, neg_strict[:].unsqueeze(1).broadcast_to([P, 2, P]), ALU.add)
                    dve.wait_ge(S["sp_high"], s + 1)
                    V.tensor_tensor(PL[:], L_[:], PH[:].bitcast(F32), ALU.subtract).then_inc(S["sp_low"], 1)

                def sb_sample_weights(s):
                    dve.wait_ge(S["dsb_ln"], s + 1)
                    V.memset(SS[NS:P, ex:ex + HT], NEG)
                    V.scalar_tensor_tensor(SS[:, 0:ex], B7[:, :], 0.0, SL[:, 0:ex], ALU.min, ALU.subtract)
                    V.scalar_tensor_tensor(SS[0:NS, ex:ex + HT], B5[0:NS, P:P + HT], 0.0, SL[0:NS, ex:], ALU.min, ALU.subtract).then_inc(S["dsb_min"], 1)
                    dve.wait_ge(S["dsb_min"], s + 1)
                    V.scalar_tensor_tensor(SL[:, 0:ex], B7[:, :], 0.0, SL[:, 0:ex], ALU.max, ALU.add)
                    V.scalar_tensor_tensor(SL[0:NS, ex:], B5[0:NS, P:P + HT], 0.0, SL[0:NS, ex:], ALU.max, ALU.add).then_inc(S["dsb_sp"], 1)

                def sb_weights(s):
                    dve.wait_ge(S["cum"], s + 1)
                    for o in range(0, SC, 512):
                        n = min(512, SC - o)
                        last = V.tensor_tensor(S_[:, o:o + n], S_[:, o:o + n], B[o // 512][:, 0:n], ALU.subtract)
                    last.then_inc(S["shifted"], 1)
                    dve.wait_ge(S["dsb_sp"], s + 1)
                    h3 = lambda t: t[0:NS, ex:ex + HT].rearrange("p (h t) -> p h t", t=NT)
                    V.tensor_tensor(h3(SL), h3(SL), seq_before[:, ds(s, 1), :].broadcast_to([NS, NH, NT]), ALU.mult)
                    V.tensor_tensor(h3(SS), h3(SS), seq_neg_strict[:, ds(s, 1), :].broadcast_to([NS, NH, NT]), ALU.add).then_inc(S["dsb_masked"], 1)
                    dve.wait_ge(S["dsb_masked"], s + 1)
                    V.tensor_copy(SUF[:, PG - 1, :], SL[:, ex:]).then_inc(S["dec_suffix"], 1)
                    for j in range(PG - 2, -1, -1):
                        dve.wait_ge(S["dec_suffix"], s * PG + (PG - 1 - j))
                        V.tensor_tensor(SUF[:, j, :], SUF[:, j + 1, :], SL[:, (j + 1) * HT:(j + 2) * HT], ALU.add).then_inc(S["dec_suffix"], 1)

                def sb_sample_shift(s):
                    dve.wait_ge(S["dec_cum"], s + 1)
                    V.tensor_tensor(SS[:, 0:ex], SS[:, 0:ex], B[3][:, :], ALU.subtract)
                    V.tensor_tensor(SS[0:NS, ex:ex + HT], SS[0:NS, ex:ex + HT], B4[0:NS, 0:HT], ALU.subtract).then_inc(S["dec_shifted"], 1)

                def step(s, it, e, more):
                    r = slice(HD * e, HD * e + HD)
                    if L == 1:
                        sb_weights(s)
                    if e == 0:
                        dve.wait_ge(S["v_high"], it + (CT * L + 1))
                        V.tensor_tensor(vL[:], VN[:, 0:TT, ds(it * P, P)], vH[:].bitcast(F32), ALU.subtract).then_inc(S["v_low"], 1)
                    dve.wait_ge(S["p_high"], s + (NB * L + 1))
                    V.tensor_tensor(PL[:], S_[:], PH[:].bitcast(F32), ALU.subtract).then_inc(S["p_low"], 1)
                    if L == 0:
                        fox_sample_shift(s)
                    if e == 1 and more:
                        stage_qk(it + 1)
                    if L == 1:
                        sb_sample_shift(s)
                    if L == 0:
                        dve.wait_ge(S["den_summed"], s + 1)
                        V.reciprocal(RD[:], B[3][:, :]).then_inc(S["rden"], 1)
                    dve.wait_ge(S[f"prompt_av{L}"], s + 2)
                    if L == 0:
                        dve.wait_ge(S["rden"], s + 1)
                        V.tensor_tensor(OT[r, :], B4[r, :], RD[r, :], ALU.mult).then_inc(S["prompt_out"], 1)
                    else:
                        V.tensor_copy(OT[r, :], B4[r, :]).then_inc(S["prompt_out"], 1)
                    if e == 1:
                        dve.wait_ge(S["o_high"], it + (CT * L + 1))
                        V.tensor_tensor(flat1(HL[:, ds(it, 1), 0:NP]), OT[:], flat1(HH[:, ds(it, 1), 0:NP]).bitcast(F32), ALU.subtract).then_inc(S["o_low"], 1)
                    if L == 0 and more:
                        fox_bias(s + 1)
                        fox_shift(s + 1)
                    if L == 1 and more:
                        sb_prompt_weights(s + 1)
                    dve.wait_ge(S["dec_av"], s + ((NB + 1) * L + 2))
                    V.tensor_copy(RD[:, P:2 * P], B5[:, 0:P]).then_inc(S["av_copied"], 1)
                    if L == 0:
                        V.reciprocal(RD[:, 0:HT], B5[:, P + HT:P + 2 * HT]).then_inc(S["dec_rden"], 1)
                        if more:
                            fox_sample_bias(s + 1)
                        dve.wait_ge(S["dec_rden"], s + 1)
                    elif more:
                        sb_sample_weights(s + 1)
                    dve.wait_ge(S["av_turned"], s + (NB * L + 1))
                    for f in range(2):
                        rf = slice(HD * f, HD * f + HD)
                        src = B4[rf, 2 * P:3 * P].rearrange("p (c r) -> p c r", c=CT)[:, :, f * NT:(f + 1) * NT]
                        dst = OS[rf, :, ds(s * NT, NT)]
                        if L == 0:
                            last = V.tensor_tensor(dst, src, RD[rf, 0:HT].rearrange("p (c h t) -> p c h t", h=2, t=NT)[:, :, f, :], ALU.mult)
                        else:
                            last = V.tensor_copy(dst, src)
                    last.then_inc(S[f"dec_out{L}"], 1)

                stage_qk(0)
                V.memset(SL[:], 0.0)
                V.memset(SS[:, 0:(PG + 1) * HT], NEG)
                V.memset(RD[:], 0.0)
                V.memset(SS[:, (PG + 1) * HT:], 0.0)
                if L == 0:
                    for b in range(NB):
                        last = V.tensor_tensor(NBI[:, b, :, :], seq_neg_causal[:, b, :].unsqueeze(1).broadcast_to([NS, NH, NT]),
                                               Fn_neg[:].unsqueeze(2).broadcast_to([NS, NH, NT]), ALU.add)
                    last.then_inc(S["nbi_set"], 1)
                    dve.wait_ge(S["nbi_set"], 1)
                if L == 0:
                    fox_bias(0)
                    fox_shift(0)
                    fox_sample_bias(0)
                else:
                    sb_prompt_weights(0)
                    sb_sample_weights(0)
                with dve.Fori(0, CT - 1) as it:
                    for e in range(2):
                        step(it * 2 + e, it, e, True)
                for e in range(2):
                    step(NB - 2 + e, CT - 1, e, e == 0)
                dve.wait_ge(S["os_high"], L + 1)
                V.tensor_tensor(HL[:, 0:CT, NP:T], OS[:], HH[:, 0:CT, NP:T].bitcast(F32), ALU.subtract).then_inc(S["os_low"], 1)

                unit_loop(dve, evac_add(True), G_OUT[L], KT, first_plain=True)
                dve.wait_ge(S["stored_v"], 32 * (L + 1))
                cut_low(G_MLP[L] + 1, 1)
                norm(1 + 2 * L)
                g = G_MLP[L]
                for n, (kind, grp) in enumerate(MLP_ORDER):
                    last = L == 1 and n == len(MLP_ORDER) - 1
                    body = evac_up(L, grp) if kind == "up" else evac_add(grp == FG - 1)
                    unit_loop(dve, body, g, KT, last, n == 0)
                    g += KT
            norm(4)
            for k in range(KT):
                dve.wait_ge(S["y_turned"], k + 1)
                V.tensor_copy(XN[:, 0:TT, k * P:(k + 1) * P], B[2 * (k % 2)][:, :].rearrange("p (i c) -> p i c", c=P))
                V.tensor_copy(XN[0:NS, TT, k * P:(k + 1) * P], B[2 * (k % 2) + 1][0:NS, 0:P]).then_inc(S["y_copied"], 1)

        @block.tensor
        def _(pe):
            M = nc.tensor.matmul
            TR = nc.tensor.transpose
            pe.sem_inc(S["unit_done"], 1)
            for L in range(2):
                pe.sem_inc(S[f"k_turned{L}"], 4)
                pe.sem_inc(S[f"v_used{L}"], 1)
                pe.sem_inc(S[f"prompt_av{L}"], 1)
                pe.sem_inc(S[f"dec_out{L}"], 1)

            def unit(hi, lo):
                def body(g, i, u, more):
                    pe.wait_ge(S["w_low"], g + 3)
                    pe.wait_ge(S["evac_act"], g + 1)
                    pe.wait_ge(S["evac_dve"], g + 1)
                    for k in range(KT):
                        for n, (w, x) in enumerate(((WH, hi), (WH, lo), (WL, hi))):
                            for h in range(2):
                                last = M(B[2 * u + h][:, 0:TH], w[u][:, k, :], x[:, k, h * TH:(h + 1) * TH],
                                         start=(k == 0 and n == 0), stop=(k == KT - 1 and n == 2))
                    last.then_inc(S["unit_done"], 1)
                return body

            def first_pair(g, order, wait):
                pe.wait_ge(S["w_low"], g + 4)
                pe.wait_ge(S["evac_act"], g + 2)
                pe.wait_ge(S["evac_dve"], g + 2)
                for m, k in enumerate(order):
                    wait(k)
                    for u in range(2):
                        for n, (w, x) in enumerate(((WH, HH), (WH, HL), (WL, HH))):
                            for h in range(2):
                                last = M(B[2 * u + h][:, 0:TH], w[u][:, k, :], x[:, k, h * TH:(h + 1) * TH],
                                         start=(m == 0 and n == 0), stop=(m == KT - 1 and n == 2))
                        if m == KT - 1:
                            last.then_inc(S["unit_done"], 1)

            def pair_after_norm(z, g):
                first_pair(g, range(KT), lambda k: pe.wait_ge(S["norm_low"], z * KT + k + 1))

            def rms(z, name, value):
                pe.wait_ge(S[name], value)
                for h in range(2):
                    last = M(B[h][:, 0:TH], ones[:], SQS[:, h * TH:(h + 1) * TH], start=True, stop=True)
                last.then_inc(S["rms_sum"], 1)

            pe.wait_ge(S["consts"], 1)
            pe.wait_ge(S["vec_in"], 64)
            TR(B[6][:, 0:n_vec], vec_rows[:], ident[0:n_vec, 0:n_vec]).then_inc(S["vec_turned"], 1)
            pe.wait_ge(S["x_in"], 32)
            for k in range(KT):
                if k >= 2:
                    pe.wait_ge(S["x_copied"], k - 1)
                for i in range(TT):
                    TR(B[2 * (k % 2)][:, i * P:(i + 1) * P], XN[:, i, k * P:(k + 1) * P], ident[:])
                TR(B[2 * (k % 2) + 1][:, 0:NS], XN[0:NS, TT, k * P:(k + 1) * P], ident[0:NS, 0:NS]).then_inc(S["x_turned"], 1)
            rms(0, "x_summed", KT)
            for L in range(2):
                if L == 1:
                    rms(2, "sum_step", 2 * KT)
                pair_after_norm(2 * L, G_IN[L])
                unit_loop(pe, unit(HH, HL), G_IN[L] + 2, n_b[L] - 2)

                def natural(n0, n1, apart):
                    for n in range(n0, n1):
                        if n >= n0 + apart:
                            pe.wait_ge(S[f"nat_dve{L}" if n % 2 == 0 else f"nat_act{L}"], (n - apart) // 2 + 1)
                        kind, i = NAT[L][n]
                        for c in range(CT):
                            src = nat_src(kind, c, i)
                            rows = P if i < TT else NS
                            last = TR(nat_bank(L, n)[0:rows, c * P:(c + 1) * P], src, ident[:])
                        last.then_inc(S[f"nat_turned{L}"], 1)

                if L == 0:
                    pe.wait_ge(S["lfp_in"], 16 * NB * PG)
                    for h in range(NH):
                        last = TR(B[7][:, h * NB * PG:(h + 1) * NB * PG], lf_raw[:, :, h], ident[0:NB * PG, 0:NB * PG])
                    last.then_inc(S["lf_turned"], 1)
                    pe.wait_ge(S["wf_low"], 1)
                    for k in range(KT):
                        for n, (w, x) in enumerate(((WFH, HH), (WFH, HL), (WFL, HH))):
                            for h in range(2):
                                last = M(B[4 + h][:, 0:TH], w[:, k, :], x[:, k, h * TH:(h + 1) * TH],
                                         start=(k == 0 and n == 0), stop=(k == KT - 1 and n == 2))
                    last.then_inc(S["f_logits"], 1)
                    pe.wait_ge(S["lf_suffixed"], 1)
                    flat = lambda t: t[:].rearrange("p h b j -> p (h b j)")
                    M(B[7][:, :], after[:], flat(lf_pos), start=True, stop=False)
                    M(B[7][:, :], ones[:], flat(lf_suf), start=False, stop=True).then_inc(S["lf_tail"], 1)
                    pe.wait_ge(S["f_copied"], 1)
                    for i in range(TT + 1):
                        c0 = i * P if i < TT else T - P
                        last = TR(B[6][:, i * NH:(i + 1) * NH], FT[:, c0:c0 + P], ident[0:NH, 0:NH])
                    last.then_inc(S["f_turned"], 1)
                if L == 0:
                    pe.wait_ge(S["evac_act"], G_QKV[0] + 2)
                    pe.wait_ge(S["evac_dve"], G_QKV[0] + 2)
                    natural(0, NG, 2)
                    unit_loop(pe, unit(HH, HL), G_QKV[0], 6)
                    pe.wait_ge(S["nat_act0"], NG // 2)
                    pe.wait_ge(S["f_logf"], 1)
                    for i in range(TT):
                        for ii in range(i + 1):
                            M(B[5][:, i * NH:(i + 1) * NH], (upto if ii == i else ones)[:], LF[:, 3, ii, :], start=(ii == 0), stop=(ii == i))
                    M(B[5][0:NS, 64:64 + NH], seq_upto[NS:P].rearrange("p b t -> p (b t)"), LF[NS:P, 3, TT, :],
                      start=True, stop=True).then_inc(S["F_sums"], 1)
                    pe.wait_ge(S["sgu_in"], 16 * (3 + GB))
                    pe.wait_ge(S["d_past"], 1)
                    for g in range(GB):
                        last = TR(B[6 + g // 4][:, (g % 4) * P:(g % 4 + 1) * P], WSN[:, g, :], ident[:])
                    last.then_inc(S["ws_turned"], 1)
                    unit_loop(pe, unit(HH, HL), G_QKV[0] + 6, 2)
                    pe.wait_ge(S["ws_masked"], 1)
                    M(B[4][0:NS, 0:GB * NT], step_rep[:].rearrange("p b t -> p (b t)"), WST[0:NT, :, 0:NT], start=True, stop=True).then_inc(S["rep_done"], 1)
                    unit_loop(pe, unit(HH, HL), G_QKV[0] + 8, 2)
                    pe.wait_ge(S["bd_set"], 1)
                    pe.wait_ge(S["ln_done"], 1)

                    def mix(c):
                        if c >= 2:
                            pe.wait_ge(S["sgu_step"], c - 1)
                        for e in range(2):
                            g = 2 * c + e
                            r = slice(HD * e, HD * e + HD)
                            for i in range(TT):
                                M(B[4 + 2 * (c % 2)][r, i * P:(i + 1) * P], GN[:, i, g * HD:(g + 1) * HD], WST[:, g, :], start=True, stop=True)
                            last = M(B[5 + 2 * (c % 2)][r, 0:NS], GN[0:NS, TT, g * HD:(g + 1) * HD],
                                     WBD[:, g].rearrange("p b t -> p (b t)"), start=True, stop=True)
                        last.then_inc(S["mixed"], 1)

                    mix(0)
                    mix(1)
                    unit_loop(pe, unit(HH, HL), G_QKV[0] + 10, 2)
                    mix(2)
                    mix(3)
                else:
                    unit_loop(pe, unit(HH, HL), G_QKV[1], 2)
                    pe.wait_ge(S["state_in"], 16)
                    for c in range(CT):
                        last = TR(B[4][:, c * 2 * NB:(c + 1) * 2 * NB], prev_n[0:2 * NB, c * P:(c + 1) * P], ident[0:2 * NB, 0:2 * NB])
                    last.then_inc(S["state_turned"], 1)
                    unit_loop(pe, unit(HH, HL), G_QKV[1] + 2, 2)
                    pe.wait_ge(S["tail_set"], 1)
                    for c in range(CT):
                        last = TR(B[5][0:2 + 2 * NB, c * P:(c + 1) * P], tail[:, c, :], ident[:])
                    last.then_inc(S["tail_turned"], 1)
                    unit_loop(pe, unit(HH, HL), G_QKV[1] + 4, 3 * CT - 4)
                pe.wait_ge(S["evac_act"], G_OUT[L] + 2)
                pe.wait_ge(S["evac_dve"], G_OUT[L] + 2)
                natural(NG if L == 0 else 0, len(NAT[L]), 4)

                pe.wait_ge(S[f"q_block{L}"], 2)
                if L == 0:
                    pe.wait_ge(S["sgu_low"], CT)
                else:
                    pe.wait_ge(S["conv_low"], CT)
                ex = PG * HT
                new_s = B5[0:NS, P:P + HT]
                QW = 2 * NT
                QR = 32

                def page_scores(s, j):
                    pe.wait_ge(S[f"kt_copied{L}"], s * PG + (j + 1))
                    for c in range(CT):
                        M(B7[:, j * HT + c * 2 * NT:j * HT + (c + 1) * 2 * NT], KTS[:, j % 2, c * P:(c + 1) * P],
                          QB[:, c, ds(s, 1), :, :].rearrange("p o h t -> p (o h t)"), start=True, stop=True)

                def page(s, j, first):
                    pe.wait_ge(S[f"k_in{L}_{j % 4}"], s * (16 * PG // 4) + 16 * (j // 4 + 1))
                    if j >= 2:
                        pe.wait_ge(S[f"kt_copied{L}"], s * PG + (j - 1))
                    if j == 1 and not first:
                        pe.wait_ge(S["dec_biased" if L == 0 else "dsb_sp"], s)
                    for c in range(CT):
                        last = TR(B[6 - j % 2][:, c * P:(c + 1) * P], KR[:, j % 4, c * P:(c + 1) * P], ident[:])
                    last.then_inc(S[f"k_turned{L}"], 1)
                    if j >= 1:
                        page_scores(s, j - 1)
                    if j == PG - 1:
                        page_scores(s, j)

                def prompt_scores(s, e, it):
                    r = slice(HD * e, HD * e + HD)
                    if e == 0:
                        pe.wait_ge(S["qk_low"], it + (CT * L + 1))
                    for j in range(TT):
                        for n, (a, b) in enumerate(((kH, qH), (kH, qL), (kL, qH))):
                            last = M(sc_bank(j, 0, WID[j]), a[r, j * P:(j + 1) * P], b[r, j * P:NP], start=(n == 0), stop=(n == 2))
                    last.then_inc(S["scores"], 1)

                def new_scores(s):
                    for c in range(CT):
                        last = M(new_s[:, c * 2 * NT:(c + 1) * 2 * NT], PA[:, CT + c, NP:T],
                                 QB[:, c, ds(s, 1), :, :].rearrange("p o h t -> p (o h t)"), start=True, stop=True)
                    return last

                def ahead(s):
                    if L == 0:
                        pe.wait_ge(S["max_step"], s * (TT - 1) + (TT - 1))
                        for i in range(TT):
                            src = S_[:, 0:P] if i == 0 else MX[:, (i - 1) * P:i * P]
                            last = TR(B[3][:, i * P:(i + 1) * P], src, ident[:])
                        last.then_inc(S["max_turned"], 1)
                    else:
                        pe.wait_ge(S["sp_low"], s + 1)
                        for j in range(TT):
                            for jj in range(j, TT):
                                d = (jj - j) * P
                                for n, x in enumerate((PH, PL)):
                                    last = M(sc_bank(j, d, WID[jj]), (after_r if jj == j else ones_r)[:], x[:, OFF[jj]:OFF[jj] + WID[jj]],
                                             start=(jj == j and n == 0), stop=(jj == TT - 1 and n == 1))
                        last.then_inc(S["cum"], 1)

                def spread_max(s):
                    pe.wait_ge(S["max_diag"], s + 1)
                    M(B[3][:, :], ones_r[:], MD[:].rearrange("p i q -> p (i q)"), start=True, stop=True).then_inc(S["max_spread"], 1)

                def step(s, it, e, more):
                    def pages_after(*js):
                        for j in js if more else ():
                            page(s + 1, j, False)

                    if L == 0:
                        pages_after(0)
                        pe.wait_ge(S["dec_max_part"], s + 1)
                        pe.wait_ge(S["dec_out0"], s + 1)
                        TR(B4[:, 0:P], RD[:, 2 * P:3 * P], ident[:]).then_inc(S["dec_max_turned"], 1)
                        pages_after(1)
                        pe.wait_ge(S["dec_max_diag"], s + 1)
                        M(B4[:, P:P + HT], ones_r[0:HT, :], MDD[:], start=True, stop=True).then_inc(S["dec_max_spread"], 1)
                    else:
                        pages_after(0, 1)
                        pe.wait_ge(S["dec_suffix"], s * PG + PG)
                        pe.wait_ge(S["dec_out1"], s + 1)
                        M(B[3][:, :], after[:], SL[:, 0:ex], start=True, stop=False)
                        M(B[3][:, :], ones[:], SUF[:].rearrange("p j n -> p (j n)"), start=False, stop=True)
                        M(B4[0:NS, 0:HT], after[0:NS, 0:NS], SL[0:NS, ex:ex + HT], start=True, stop=True).then_inc(S["dec_cum"], 1)
                        pages_after(2)
                    pe.wait_ge(S["v_low"], it + (CT * L + 1))
                    pe.wait_ge(S["p_low"], s + (NB * L + 1))
                    if L == 0:
                        for j in range(TT):
                            for n, x in enumerate((PH, PL)):
                                last = M(B[3][:, j * P:NP], ones_r[:], x[:, OFF[j]:OFF[j] + WID[j]], start=(j == 0 and n == 0), stop=(j == TT - 1 and n == 1))
                        last.then_inc(S["den_summed"], 1)
                    pe.wait_ge(S["dec_shifted"], s + (NB * L + 1))
                    for j in range(TT):
                        for n, (a, b) in enumerate(((vH, PH), (vH, PL), (vL, PH))):
                            last = M(B4[:, j * P:NP], a[:, j, :], b[:, OFF[j]:OFF[j] + WID[j]], start=(j == 0 and n == 0), stop=(j == TT - 1 and n == 2))
                    last.then_inc(S[f"prompt_av{L}"], 1)
                    if more:
                        prompt_scores(s + 1, 1 - e, it + e)
                        pages_after(*range(2 + L, PG))
                        if L == 0:
                            ahead(s + 1)
                        new_scores(s + 1)
                    pe.wait_ge(S["dec_probs"], s + (NB * L + 1))
                    if L == 0:
                        for q in range(P // QR):
                            for j in range(PG + 1):
                                M(B5[q * QR:(q + 1) * QR, P + HT:P + 2 * HT], ones[:, 0:QR], SS[:, j * HT:(j + 1) * HT], start=(j == 0), stop=(j == PG))
                        if more:
                            spread_max(s + 1)
                    pe.wait_ge(S[f"v_in{L}"], s * (16 * PG) + 16 * PG)
                    for c in range(CT):
                        o = c * QW
                        rows = slice(c * QR, (c + 1) * QR)
                        for j in range(PG):
                            last = M(B5[rows, 0:P], SS[:, j * HT + o:j * HT + o + QR], VR[:, j, c * P:(c + 1) * P], start=(j == 0), stop=False)
                        if c == CT - 1:
                            last.then_inc(S[f"v_used{L}"], 1)
                        last = M(B5[rows, 0:P], SS[0:NS, ex + o:ex + o + QR], VN[0:NS, TT, c * P:(c + 1) * P], start=False, stop=True)
                    last.then_inc(S["dec_av"], 1)
                    if L == 1 and more:
                        ahead(s + 1)
                    pe.wait_ge(S["av_copied"], s + (NB * L + 1))
                    TR(B4[:, 2 * P:3 * P], RD[:, P:2 * P], ident[:]).then_inc(S["av_turned"], 1)

                for j in range(PG):
                    page(0, j, True)
                prompt_scores(0, 0, 0)
                new_scores(0).then_inc(S["dec_av"], 1)
                ahead(0)
                if L == 0:
                    spread_max(0)
                with pe.Fori(0, CT - 1) as it:
                    for e in range(2):
                        step(it * 2 + e, it, e, True)
                for e in range(2):
                    step(NB - 2 + e, CT - 1, e, e == 0)

                def attention_out(k):
                    if k == 0:
                        pe.wait_ge(S["os_low"], L + 1)
                        pe.wait_ge(S["o_low"], CT * (L + 1))

                first_pair(G_OUT[L], [*range(CT, KT), *range(CT)], attention_out)
                unit_loop(pe, unit(HH, HL), G_OUT[L] + 2, KT - 2)
                rms(1 + 2 * L, "sum_step", (2 * L + 1) * KT)
                pair_after_norm(1 + 2 * L, G_MLP[L])
                g = G_MLP[L]
                up_end = {}
                for n, (kind, grp) in enumerate(MLP_ORDER):
                    if kind == "up":
                        first = 2 if n == 0 else 0
                        unit_loop(pe, unit(HH, HL), g + first, KT - first)
                        up_end[grp] = g + KT - 1
                    else:
                        pe.wait_ge(S["evac_dve"], up_end[grp] + 3)
                        unit_loop(pe, unit(ffH[grp % 2], ffL[grp % 2]), g, KT)
                    g += KT
            rms(4, "sum_step", 4 * KT)
            for k in range(KT):
                pe.wait_ge(S["normed"], 4 * KT + k + 1)
                if k >= 2:
                    pe.wait_ge(S["y_copied"], k - 1)
                for i in range(TT):
                    TR(B[2 * (k % 2)][:, i * P:(i + 1) * P], Y[:, k, i * P:(i + 1) * P], ident[:])
                TR(B[2 * (k % 2) + 1][0:NS, 0:P], Y[:, k, NP:T], ident[:]).then_inc(S["y_turned"], 1)


_INS = ["x_prompt", "x_sample", "cache_fox_k", "cache_fox_v", "cache_fox_logf", "cache_sb_k", "cache_sb_v", "state_conv",
        "page_table", "g_mix", "g_mlp", "g_final", "w_up", "w_down", "w_in_even", "b_forget", "sgu_g", "sgu_b",
        "w_spatial", "b_spatial", "w_out_even", "w_in_odd", "conv_w", "w_out_odd"]
_OUTS = [(1, 512, 1024), (8, 8, 1024), (1, 1, 512, 8, 64), (1, 1, 512, 8, 64), (1, 1, 512, 8), (1, 1, 512, 8, 64),
         (1, 1, 512, 8, 64), (1, 1, 2, 512), (1, 8, 8, 8, 64), (1, 8, 8, 8, 64), (1, 8, 8, 8), (1, 8, 8, 8, 64),
         (1, 8, 8, 8, 64), (1, 8, 2, 512), (1, 8, 8, 512)]


def kernel(**inputs):
    import numpy as _np
    import concourse.bacc as _bacc
    from concourse import mybir as _mybir
    from concourse.bass_utils import run_bass_kernel_spmd as _run

    nc = _bacc.Bacc("TRN2", target_bir_lowering=False, num_devices=1)
    arrays, args = {}, []
    for name in _INS:
        a = _np.ascontiguousarray(inputs[name])
        arrays[f"in_{name}_dram"] = a
        args.append(nc.dram_tensor(f"in_{name}_dram", a.shape, _mybir.dt.from_np(a.dtype), kind="ExternalInput").ap())
    for i, shape in enumerate(_OUTS):
        args.append(nc.dram_tensor(f"out_{i}_dram", shape, _mybir.dt.float32, kind="ExternalOutput").ap())
    trunk(nc, *args)
    r = _run(nc, [arrays], core_ids=[0])
    return tuple(r.results[0][f"out_{i}_dram"] for i in range(len(_OUTS)))
```
